# Optimizing a Trainium2 kernel written in Bass

```python
import functools
import math
import jax
import jax.numpy as jnp
from jax import lax
import numpy as np

D_MODEL = 1024
BATCH = 1
SEQ = 1024
DEPTH = 1
DEC_BATCH = 8
DEC_SEQ = 4
PAST_LEN = 4096
PAGE_SIZE = 128

CONV_CH = 512
CONV_W = 31
GDN_HEADS = 4
GDN_DK = 128
GDN_DV = 128
GDN_CONV_W = 4
GDN_CHUNK = 64
NSA_HEADS = 8
NSA_KV = 2
NSA_GQ = NSA_HEADS // NSA_KV
NSA_DH = 64
L_CMP = 32
L_SEL = 64
N_SEL = 16
WINDOW = 512
Q_BLOCK = 128
FORCE_BONUS = 1e4
N_MEM = 256
X_HEADS = 4
X_DH = D_MODEL // X_HEADS
D_FF = 4 * D_MODEL
N_BUCKETS = 32
MAX_DIST = 128
EPS = 1e-6
F32 = jnp.float32

A_COLS = 2 * CONV_CH
GDN_QK = GDN_HEADS * GDN_DK
GDN_V = GDN_HEADS * GDN_DV
GDN_QKV = 2 * GDN_QK + GDN_V
B_COLS = GDN_QKV + GDN_V + 2 * GDN_HEADS
NSA_Q = NSA_HEADS * NSA_DH
NSA_KVW = NSA_KV * NSA_DH
C_COLS = NSA_Q + 6 * NSA_KVW + 3 * NSA_HEADS
G_COLS = 3 * D_MODEL
N_IN = A_COLS + B_COLS + C_COLS + G_COLS

kernel_name = 'hybrid_conv_gdn_nsa_decoder_step'

def rmsnorm(x, g):
    xf = x.astype(F32)
    y = xf * lax.rsqrt(jnp.mean(xf * xf, axis=-1, keepdims=True) + EPS)
    return (y * g.astype(F32)).astype(x.dtype)

def layernorm(x, g, b):
    xf = x.astype(F32)
    mu = jnp.mean(xf, axis=-1, keepdims=True)
    var = jnp.mean(jnp.square(xf - mu), axis=-1, keepdims=True)
    return ((xf - mu) * lax.rsqrt(var + EPS) * g.astype(F32) + b.astype(F32)).astype(x.dtype)

def l2norm(x):
    xf = x.astype(F32)
    return xf * lax.rsqrt(jnp.sum(xf * xf, axis=-1, keepdims=True) + EPS)

def masked_softmax(s, mask):
    s = jnp.where(mask, s.astype(F32), -1e30)
    m = jnp.max(s, axis=-1, keepdims=True)
    e = jnp.exp(s - m) * mask
    return e / jnp.maximum(jnp.sum(e, axis=-1, keepdims=True), 1e-30)

def t5_bucket(rel):
    n = jnp.maximum(rel, 0)
    max_exact = N_BUCKETS // 2
    nf = jnp.maximum(n, 1).astype(F32)
    large = max_exact + (jnp.log(nf / max_exact) / math.log(MAX_DIST / max_exact) * (N_BUCKETS - max_exact)).astype(jnp.int32)
    large = jnp.minimum(large, N_BUCKETS - 1)
    return jnp.where(n < max_exact, n, large)

def head_bias(rel_bias, rel):
    b = rel_bias[t5_bucket(rel)].astype(F32)
    b = b.reshape(b.shape[:-1] + (NSA_KV, NSA_GQ))
    return jnp.moveaxis(b, (-2, -1), (-4, -3))

def causal_dwconv(x, buf, w):
    xcat = jnp.concatenate([buf.astype(x.dtype), x], axis=1)
    y = lax.conv_general_dilated(xcat, w.astype(x.dtype)[:, None, :], window_strides=(1,), padding='VALID',
                                 dimension_numbers=('NWC', 'WIO', 'NWC'), feature_group_count=x.shape[-1])
    return y, xcat[:, xcat.shape[1] - (w.shape[0] - 1):]

def conformer_conv(u, buf, w_dw, b_dw, ln_g, ln_b, w_p):
    a, gate = jnp.split(u, 2, axis=-1)
    glu = a * jax.nn.sigmoid(gate)
    y, new_buf = causal_dwconv(glu, buf, w_dw)
    y = jax.nn.silu(layernorm(y + b_dw.astype(y.dtype), ln_g, ln_b))
    return y @ w_p, new_buf

def gdn_chunked(q, k, v, g, beta, s0):
    B, T, H, DK = q.shape
    DV = v.shape[-1]
    C = min(GDN_CHUNK, T)
    N = T // C

    def to_chunks(a):
        a = a.astype(F32).reshape((B, N, C, H) + a.shape[3:])
        return jnp.moveaxis(a, (1, 3), (0, 2))

    qc, kc, vc, gc, bc = map(to_chunks, (q, k, v, g, beta))
    gc = jnp.cumsum(gc, axis=-1)
    i = jnp.arange(C)
    incl = i[:, None] >= i[None, :]
    strict = i[:, None] > i[None, :]
    decay = jnp.exp(jnp.where(incl, gc[..., :, None] - gc[..., None, :], -jnp.inf))
    kb = kc * bc[..., None]
    a_low = jnp.where(strict, jnp.einsum('nbhid,nbhjd->nbhij', kb, kc) * decay, 0.0)
    lhs = a_low + jnp.eye(C, dtype=F32)
    rhs = jnp.concatenate([vc * bc[..., None], kb * jnp.exp(gc)[..., None]], axis=-1)
    sol = lax.linalg.triangular_solve(lhs, rhs, left_side=True, lower=True, unit_diagonal=True)
    v_w, k_cd = sol[..., :DV], sol[..., DV:]
    qk = jnp.where(incl, jnp.einsum('nbhid,nbhjd->nbhij', qc, kc) * decay, 0.0)

    def step(S, xs):
        q_i, k_i, vw_i, kcd_i, qk_i, g_i = xs
        v_new = vw_i - jnp.einsum('bhck,bhkv->bhcv', kcd_i, S)
        o_i = jnp.einsum('bhck,bhkv->bhcv', q_i * jnp.exp(g_i)[..., None], S) + jnp.einsum('bhij,bhjv->bhiv', qk_i, v_new)
        g_end = g_i[..., -1]
        S = S * jnp.exp(g_end)[..., None, None] + jnp.einsum('bhck,bhcv->bhkv', k_i * jnp.exp(g_end[..., None] - g_i)[..., None], v_new)
        return S, o_i

    s_fin, o = lax.scan(step, s0.astype(F32), (qc, kc, v_w, k_cd, qk, gc))
    o = jnp.moveaxis(o, (0, 2), (1, 3)).reshape(B, T, H, DV)
    return o, s_fin

def gated_deltanet(u, qkv_buf, s0, w_conv, a_log, dt_bias, norm_g, w_p):
    B, T, _ = u.shape
    qkv, z, a, b = jnp.split(u, [GDN_QKV, GDN_QKV + GDN_V, GDN_QKV + GDN_V + GDN_HEADS], axis=-1)
    qkv_c, qkv_new = causal_dwconv(qkv, qkv_buf, w_conv)
    qkv_c = jax.nn.silu(qkv_c)
    q, k, v = jnp.split(qkv_c, [GDN_QK, 2 * GDN_QK], axis=-1)
    q = l2norm(q.reshape(B, T, GDN_HEADS, GDN_DK)) * (GDN_DK ** -0.5)
    k = l2norm(k.reshape(B, T, GDN_HEADS, GDN_DK))
    v = v.reshape(B, T, GDN_HEADS, GDN_DV)
    g = -jnp.exp(a_log.astype(F32)) * jax.nn.softplus(a.astype(F32) + dt_bias.astype(F32))
    beta = jax.nn.sigmoid(b.astype(F32))
    o, s_new = gdn_chunked(q, k, v, g, beta, s0)
    o = rmsnorm(o, norm_g) * jax.nn.silu(z.astype(F32)).reshape(B, T, GDN_HEADS, GDN_DV)
    return o.reshape(B, T, GDN_V).astype(u.dtype) @ w_p, qkv_new, s_new

def nsa_compress(kv2, w_pos):
    B, Tk = kv2.shape[:2]
    nc = Tk // L_CMP
    blocks = kv2[:, :nc * L_CMP].reshape(B, nc, L_CMP, 2, NSA_KV, NSA_DH)
    kvc = jnp.einsum('bnlsgd,sl->bnsgd', blocks, w_pos.astype(kv2.dtype))
    end_pos = jnp.arange(nc) * L_CMP + (L_CMP - 1)
    return kvc[:, :, 0], kvc[:, :, 1], end_pos

def nsa_cmp_slc(q, q_pos, kc, vc, c_end, ksb, vsb, rel_bias):
    B, Tq = q.shape[:2]
    scale = NSA_DH ** -0.5
    rel_c = q_pos[:, None] - c_end[None, :]
    s_c = jnp.einsum('bqgrd,bngd->bgrqn', q, kc).astype(F32) * scale + head_bias(rel_bias, rel_c)
    p_c = masked_softmax(s_c, rel_c >= 0)
    o_c = jnp.einsum('bgrqn,bngd->bqgrd', p_c.astype(vc.dtype), vc)
    nsb = ksb.shape[2]
    ratio = L_SEL // L_CMP
    imp = p_c.sum(axis=2)
    nc = imp.shape[-1]
    imp = jnp.pad(imp, ((0, 0), (0, 0), (0, 0), (0, nsb * ratio - nc))).reshape(B, NSA_KV, Tq, nsb, ratio).sum(-1)
    blk = jnp.arange(nsb)[None, :]
    cur = (q_pos // L_SEL)[:, None]
    valid = blk <= cur
    forced = (blk == 0) | (blk == cur) | (blk == cur - 1)
    score = jnp.where(valid, imp + jnp.where(forced, FORCE_BONUS, 0.0), -1.0)
    n_sel = min(N_SEL, nsb)
    _, idx = lax.top_k(score, n_sel)
    gather = jax.vmap(jax.vmap(lambda blocks, ix: blocks[ix]))
    ks = gather(ksb, idx).reshape(B, NSA_KV, Tq, n_sel * L_SEL, NSA_DH)
    vs = gather(vsb, idx).reshape(B, NSA_KV, Tq, n_sel * L_SEL, NSA_DH)
    pos = (idx[..., None] * L_SEL + jnp.arange(L_SEL)).reshape(B, NSA_KV, Tq, n_sel * L_SEL)
    rel_s = q_pos[:, None] - pos
    tb = rel_bias.astype(F32).reshape(N_BUCKETS, NSA_KV, NSA_GQ)
    bias_s = jnp.moveaxis(tb[t5_bucket(rel_s), jnp.arange(NSA_KV)[None, :, None, None]], -1, 2)
    s_s = jnp.einsum('bqgrd,bgqkd->bgrqk', q, ks).astype(F32) * scale + bias_s
    p_s = masked_softmax(s_s, (rel_s >= 0)[:, :, None])
    o_s = jnp.einsum('bgrqk,bgqkd->bqgrd', p_s.astype(vs.dtype), vs)
    return o_c, o_s

def nsa_window(q, q_pos, k, v, k_pos, rel_bias):
    rel = q_pos[:, :, None] - k_pos[:, None, :]
    mask = (rel >= 0) & (rel < WINDOW) & (k_pos[:, None, :] >= 0)
    s = jnp.einsum('bnqgrd,bnkgd->bngrqk', q, k).astype(F32) * (NSA_DH ** -0.5) + head_bias(rel_bias, rel)
    p = masked_softmax(s, mask[:, None, None])
    return jnp.einsum('bngrqk,bnkgd->bnqgrd', p.astype(v.dtype), v)

def nsa_prompt(q, kv, rel_bias, w_pos):
    B, T = q.shape[:2]
    q_pos = jnp.arange(T)
    kc, vc, c_end = nsa_compress(kv[:, :, 0:2], w_pos)
    nsb = T // L_SEL
    ksb = kv[:, :, 2].reshape(B, nsb, L_SEL, NSA_KV, NSA_DH).transpose(0, 3, 1, 2, 4)
    vsb = kv[:, :, 3].reshape(B, nsb, L_SEL, NSA_KV, NSA_DH).transpose(0, 3, 1, 2, 4)
    nqb = T // Q_BLOCK
    qb = jnp.moveaxis(q.reshape(B, nqb, Q_BLOCK, NSA_KV, NSA_GQ, NSA_DH), 1, 0)
    pb = q_pos.reshape(nqb, Q_BLOCK)
    o_c, o_s = lax.map(lambda xs: nsa_cmp_slc(xs[0], xs[1], kc, vc, c_end, ksb, vsb, rel_bias), (qb, pb))
    o_c = jnp.moveaxis(o_c, 0, 1).reshape(B, T, NSA_KV, NSA_GQ, NSA_DH)
    o_s = jnp.moveaxis(o_s, 0, 1).reshape(B, T, NSA_KV, NSA_GQ, NSA_DH)
    n_prev = WINDOW // Q_BLOCK
    kvw = jnp.pad(kv[:, :, 4:6], ((0, 0), (WINDOW, 0), (0, 0), (0, 0), (0, 0)))
    kvw = kvw.reshape(B, nqb + n_prev, Q_BLOCK, 2, NSA_KV, NSA_DH)
    band = jnp.concatenate([kvw[:, j:j + nqb] for j in range(n_prev + 1)], axis=2)
    k_pos = (jnp.arange(nqb)[:, None] - n_prev) * Q_BLOCK + jnp.arange((n_prev + 1) * Q_BLOCK)[None, :]
    o_w = nsa_window(q.reshape(B, nqb, Q_BLOCK, NSA_KV, NSA_GQ, NSA_DH), pb, band[:, :, :, 0], band[:, :, :, 1], k_pos, rel_bias)
    o_w = o_w.reshape(B, T, NSA_KV, NSA_GQ, NSA_DH)
    wb = min(WINDOW, T)
    return o_c, o_s, o_w, kv[:, :, :4], kv[:, T - wb:, 4:6]

def nsa_sample(q, kv, rel_bias, w_pos, past_kv, win_buf):
    B, T = q.shape[:2]
    past = past_kv.shape[1]
    q_pos = past + jnp.arange(T)
    full = jnp.concatenate([past_kv.astype(kv.dtype), kv[:, :, :4]], axis=1)
    Tk = past + T
    kc, vc, c_end = nsa_compress(full[:, :, 0:2], w_pos)
    nsb = -(-Tk // L_SEL)
    sel = jnp.pad(full[:, :, 2:4], ((0, 0), (0, nsb * L_SEL - Tk), (0, 0), (0, 0), (0, 0)))
    sel = sel.reshape(B, nsb, L_SEL, 2, NSA_KV, NSA_DH)
    ksb = sel[:, :, :, 0].transpose(0, 3, 1, 2, 4)
    vsb = sel[:, :, :, 1].transpose(0, 3, 1, 2, 4)
    o_c, o_s = nsa_cmp_slc(q, q_pos, kc, vc, c_end, ksb, vsb, rel_bias)
    wb = win_buf.shape[1]
    wkv = jnp.concatenate([win_buf.astype(kv.dtype), kv[:, :, 4:6]], axis=1)
    k_pos = past - wb + jnp.arange(wb + T)
    o_w = nsa_window(q[:, None], q_pos[None], wkv[:, None, :, 0], wkv[:, None, :, 1], k_pos[None], rel_bias)[:, 0]
    return o_c, o_s, o_w, kv[:, :, :4], wkv[:, T:]

def parallel_mixers(h, p, l, conv_buf, qkv_buf, s0, nsa_attend):
    Bh, Th, _ = h.shape
    u = h @ p['w_in'][l]
    u_a, u_b, u_c, u_g = jnp.split(u, [A_COLS, A_COLS + B_COLS, A_COLS + B_COLS + C_COLS], axis=-1)
    y_a, conv_new = conformer_conv(u_a, conv_buf, p['conv_a_w'][l], p['conv_a_b'][l], p['ln_a_g'][l], p['ln_a_b'][l], p['w_pa'][l])
    y_b, qkv_new, s_new = gated_deltanet(u_b, qkv_buf, s0, p['gdn_conv_w'][l], p['gdn_a_log'][l], p['gdn_dt_bias'][l],
                                         p['gdn_norm_g'][l], p['w_pb'][l])
    q, kv, gl = jnp.split(u_c, [NSA_Q, NSA_Q + 6 * NSA_KVW], axis=-1)
    q = q.reshape(Bh, Th, NSA_KV, NSA_GQ, NSA_DH)
    kv = kv.reshape(Bh, Th, 6, NSA_KV, NSA_DH)
    gt = jax.nn.sigmoid(gl).reshape(Bh, Th, 3, NSA_KV, NSA_GQ, 1)
    o_c, o_s, o_w, rows, win = nsa_attend(q, kv, p['rel_bias'], p['nsa_cmp_w'][l])
    o = gt[:, :, 0] * o_c + gt[:, :, 1] * o_s + gt[:, :, 2] * o_w
    y_c = o.reshape(Bh, Th, NSA_Q) @ p['w_pc'][l]
    g_a, g_b, g_c = jnp.split(jax.nn.sigmoid(u_g), 3, axis=-1)
    y = (g_a * y_a + g_b * y_b + g_c * y_c) @ p['w_o'][l]
    return y, conv_new, qkv_new, s_new, rows, win

def cross_attn(h, mem_k, mem_v, w_q, w_o):
    B, T, _ = h.shape
    q = (h @ w_q).reshape(B, T, X_HEADS, X_DH)
    s = jnp.einsum('bqhd,bmhd->bhqm', q, mem_k).astype(F32) * (X_DH ** -0.5)
    pr = jax.nn.softmax(s, axis=-1)
    o = jnp.einsum('bhqm,bmhd->bqhd', pr.astype(mem_v.dtype), mem_v).reshape(B, T, D_MODEL)
    return o @ w_o

def sq_relu_mlp(h, w1, w2):
    return jnp.square(jax.nn.relu(h @ w1)) @ w2

def setup_inputs(seed: int = 0) -> dict:
    key = jax.random.key(seed)
    ks = iter(jax.random.split(key, 48))

    def nrm(shape, scale):
        return jax.random.normal(next(ks), shape, F32) * scale

    def gain(shape):
        return 1.0 + nrm(shape, 0.1)

    n_pages = PAST_LEN // PAGE_SIZE
    n_used = DEC_BATCH * n_pages
    n_pool = n_used + max(1, n_used // 4)
    w_buf = min(WINDOW, PAST_LEN)
    x_prompt = nrm((BATCH, SEQ, D_MODEL), 1.0)
    x_sample = nrm((DEC_BATCH, DEC_SEQ, D_MODEL), 1.0)
    cache_nsa_kv = nrm((DEPTH, n_pool, PAGE_SIZE, 4, NSA_KV, NSA_DH), 1.0)
    cache_win_kv = nrm((DEPTH, DEC_BATCH, w_buf, 2, NSA_KV, NSA_DH), 1.0)
    state_conv_a = nrm((DEPTH, DEC_BATCH, CONV_W - 1, CONV_CH), 0.5)
    state_conv_qkv = nrm((DEPTH, DEC_BATCH, GDN_CONV_W - 1, GDN_QKV), 1.0)
    state_gdn = nrm((DEPTH, DEC_BATCH, GDN_HEADS, GDN_DK, GDN_DV), 0.1)
    cache_mem_kv = nrm((DEPTH, DEC_BATCH, N_MEM, 2, X_HEADS, X_DH), 1.0)
    page_table = jax.random.permutation(next(ks), n_pool)[:n_used].reshape(DEC_BATCH, n_pages).astype(jnp.int32)
    mem_prompt = nrm((BATCH, N_MEM, D_MODEL), 1.0)
    dt = jax.random.uniform(next(ks), (DEPTH, GDN_HEADS), F32, 0.001, 0.1)
    return {
        'x_prompt': x_prompt,
        'x_sample': x_sample,
        'cache_nsa_kv': cache_nsa_kv,
        'cache_win_kv': cache_win_kv,
        'state_conv_a': state_conv_a,
        'state_conv_qkv': state_conv_qkv,
        'state_gdn': state_gdn,
        'cache_mem_kv': cache_mem_kv,
        'page_table': page_table,
        'mem_prompt': mem_prompt,
        'rel_bias': nrm((N_BUCKETS, NSA_HEADS), 0.5),
        'norm_mix': gain((DEPTH, D_MODEL)),
        'w_in': nrm((DEPTH, D_MODEL, N_IN), D_MODEL ** -0.5),
        'conv_a_w': nrm((DEPTH, CONV_W, CONV_CH), CONV_W ** -0.5),
        'conv_a_b': nrm((DEPTH, CONV_CH), 0.02),
        'ln_a_g': gain((DEPTH, CONV_CH)),
        'ln_a_b': nrm((DEPTH, CONV_CH), 0.02),
        'w_pa': nrm((DEPTH, CONV_CH, D_MODEL), CONV_CH ** -0.5),
        'gdn_conv_w': nrm((DEPTH, GDN_CONV_W, GDN_QKV), GDN_CONV_W ** -0.5),
        'gdn_a_log': jnp.log(jax.random.uniform(next(ks), (DEPTH, GDN_HEADS), F32, 1.0, 16.0)),
        'gdn_dt_bias': jnp.log(jnp.expm1(dt)),
        'gdn_norm_g': gain((DEPTH, GDN_DV)),
        'w_pb': nrm((DEPTH, GDN_V, D_MODEL), GDN_V ** -0.5),
        'nsa_cmp_w': (1.0 + nrm((DEPTH, 2, L_CMP), 0.1)) / L_CMP,
        'w_pc': nrm((DEPTH, NSA_Q, D_MODEL), NSA_Q ** -0.5),
        'w_o': nrm((DEPTH, D_MODEL, D_MODEL), D_MODEL ** -0.5),
        'norm_x': gain((DEPTH, D_MODEL)),
        'w_xq': nrm((DEPTH, D_MODEL, D_MODEL), D_MODEL ** -0.5),
        'w_xk': nrm((DEPTH, D_MODEL, D_MODEL), D_MODEL ** -0.5),
        'w_xv': nrm((DEPTH, D_MODEL, D_MODEL), D_MODEL ** -0.5),
        'w_xo': nrm((DEPTH, D_MODEL, D_MODEL), D_MODEL ** -0.5),
        'norm_mlp': gain((DEPTH, D_MODEL)),
        'w_ff1': nrm((DEPTH, D_MODEL, D_FF), D_MODEL ** -0.5),
        'w_ff2': nrm((DEPTH, D_FF, D_MODEL), D_FF ** -0.5),
        'norm_final': gain((D_MODEL,)),
    }

def reference(x_prompt, x_sample, cache_nsa_kv, cache_win_kv, state_conv_a, state_conv_qkv, state_gdn, cache_mem_kv,
              page_table, mem_prompt, rel_bias, norm_mix, w_in, conv_a_w, conv_a_b, ln_a_g, ln_a_b, w_pa, gdn_conv_w,
              gdn_a_log, gdn_dt_bias, gdn_norm_g, w_pb, nsa_cmp_w, w_pc, w_o, norm_x, w_xq, w_xk, w_xv, w_xo,
              norm_mlp, w_ff1, w_ff2, norm_final):
    p = {'rel_bias': rel_bias, 'w_in': w_in, 'conv_a_w': conv_a_w, 'conv_a_b': conv_a_b, 'ln_a_g': ln_a_g,
         'ln_a_b': ln_a_b, 'w_pa': w_pa, 'gdn_conv_w': gdn_conv_w, 'gdn_a_log': gdn_a_log, 'gdn_dt_bias': gdn_dt_bias,
         'gdn_norm_g': gdn_norm_g, 'w_pb': w_pb, 'nsa_cmp_w': nsa_cmp_w, 'w_pc': w_pc, 'w_o': w_o}
    xp, xs = x_prompt, x_sample
    Bp = xp.shape[0]
    Bs = xs.shape[0]
    n_pages = page_table.shape[1]
    p_rows, p_win, p_conv, p_qkv, p_gdn, p_mem = [], [], [], [], [], []
    s_rows, s_win, s_conv, s_qkv, s_gdn = [], [], [], [], []
    for l in range(DEPTH):
        h = rmsnorm(xp, norm_mix[l])
        conv0 = jnp.zeros((Bp, CONV_W - 1, CONV_CH), xp.dtype)
        qkv0 = jnp.zeros((Bp, GDN_CONV_W - 1, GDN_QKV), xp.dtype)
        s0 = jnp.zeros((Bp, GDN_HEADS, GDN_DK, GDN_DV), F32)
        y, conv_n, qkv_n, s_n, rows, win = parallel_mixers(h, p, l, conv0, qkv0, s0, nsa_prompt)
        xp = xp + y
        mem_kv = jnp.stack([mem_prompt @ w_xk[l], mem_prompt @ w_xv[l]], axis=2).reshape(Bp, N_MEM, 2, X_HEADS, X_DH)
        xp = xp + cross_attn(rmsnorm(xp, norm_x[l]), mem_kv[:, :, 0], mem_kv[:, :, 1], w_xq[l], w_xo[l])
        xp = xp + sq_relu_mlp(rmsnorm(xp, norm_mlp[l]), w_ff1[l], w_ff2[l])
        p_rows.append(rows); p_win.append(win); p_conv.append(conv_n); p_qkv.append(qkv_n); p_gdn.append(s_n); p_mem.append(mem_kv)
        h = rmsnorm(xs, norm_mix[l])
        past = cache_nsa_kv[l][page_table].reshape(Bs, n_pages * PAGE_SIZE, 4, NSA_KV, NSA_DH)
        nsa_fn = functools.partial(nsa_sample, past_kv=past, win_buf=cache_win_kv[l])
        y, conv_n, qkv_n, s_n, rows, win = parallel_mixers(h, p, l, state_conv_a[l], state_conv_qkv[l], state_gdn[l], nsa_fn)
        xs = xs + y
        mkv = cache_mem_kv[l].astype(xs.dtype)
        xs = xs + cross_attn(rmsnorm(xs, norm_x[l]), mkv[:, :, 0], mkv[:, :, 1], w_xq[l], w_xo[l])
        xs = xs + sq_relu_mlp(rmsnorm(xs, norm_mlp[l]), w_ff1[l], w_ff2[l])
        s_rows.append(rows); s_win.append(win); s_conv.append(conv_n); s_qkv.append(qkv_n); s_gdn.append(s_n)
    y_prompt = rmsnorm(xp, norm_final)
    y_sample = rmsnorm(xs, norm_final)
    new_nsa_kv_prompt = jnp.stack(p_rows, axis=0)
    new_win_kv_prompt = jnp.stack(p_win, axis=0)
    new_conv_a_prompt = jnp.stack(p_conv, axis=0)
    new_conv_qkv_prompt = jnp.stack(p_qkv, axis=0)
    new_gdn_prompt = jnp.stack(p_gdn, axis=0)
    new_mem_kv_prompt = jnp.stack(p_mem, axis=0)
    new_nsa_kv_sample = jnp.stack(s_rows, axis=0)
    new_win_kv_sample = jnp.stack(s_win, axis=0)
    new_conv_a_sample = jnp.stack(s_conv, axis=0)
    new_conv_qkv_sample = jnp.stack(s_qkv, axis=0)
    new_gdn_sample = jnp.stack(s_gdn, axis=0)
    return (y_prompt, y_sample, new_nsa_kv_prompt, new_win_kv_prompt, new_conv_a_prompt, new_conv_qkv_prompt,
            new_gdn_prompt, new_mem_kv_prompt, new_nsa_kv_sample, new_win_kv_sample, new_conv_a_sample,
            new_conv_qkv_sample, new_gdn_sample)


_drawn_inputs = setup_inputs


def setup_inputs(seed=0):
    import zlib

    import numpy as np

    out = dict(_drawn_inputs(seed))
    spreads = {}
    factors = {'cache_nsa_kv': 3.462,
     'rel_bias': 2.969,
     'conv_a_b': 4.214,
     'ln_a_b': 8.0,
     'nsa_cmp_w': 8.0,
     'norm_x': 5.499}
    for name, (base, spread) in spreads.items():
        noise = np.random.default_rng([zlib.crc32(name.encode()), seed]).standard_normal(out[name].shape)
        drawn = base * np.exp(spread * noise) if base else spread * noise
        out[name] = jnp.asarray(drawn.astype(out[name].dtype))
    for name, factor in factors.items():
        out[name] = (out[name] * factor).astype(out[name].dtype)
    return out
```

```python
from contextlib import ExitStack
import math

import numpy as np
import concourse.bass as bass
from concourse import mybir

ALU = mybir.AluOpType
ACT = mybir.ActivationFunctionType
AX_X = mybir.AxisListType.X
F32 = mybir.dt.float32
I32 = mybir.dt.int32

P = 128
D = 1024
TP = 1024
NB, TS = 8, 4
W = TP + NB * TS
NT = TP // P
CHUNKS = D // P
SPLIT = 3
WN = W // SPLIT
BANK = 512
EPS = 1e-6

CONV_CH, CONV_W = 512, 31
GH, GDN_CONV_W = 4, 4
NSA_HEADS, NSA_KV, GQ, DH = 8, 2, 4, 64
L_CMP, L_SEL, N_SEL, WINDOW = 32, 64, 16, 512
FORCE_BONUS = 1e4
N_BUCKETS, MAX_DIST = 32, 128
PAST, PAGE = 4096, 128
N_PAGES = PAST // PAGE
N_POOL = NB * N_PAGES + NB * N_PAGES // 4
N_MEM, XH, XD = 256, 4, 256
D_FF = 4096
NEG = -1e30

T_A, T_AG, T_QKV, T_Z, T_Q, T_KV, T_MISC, T_GATE = 0, 4, 8, 20, 24, 28, 34, 35
N_LINEAR, N_GATE = 35, 24
KV_KCMP, KV_VCMP, KV_KSLC, KV_VSLC, KV_KWIN, KV_VWIN = range(6)


def bucket_onehot(rel):
    n = np.maximum(rel, 0)
    exact = N_BUCKETS // 2
    large = exact + (np.log(np.maximum(n, 1).astype(np.float32) / exact) / math.log(MAX_DIST / exact)
                     * (N_BUCKETS - exact)).astype(np.int32)
    b = np.where(n < exact, n, np.minimum(large, N_BUCKETS - 1))
    out = np.zeros((N_BUCKETS + 1, rel.size), np.float32)
    out[np.where(rel >= 0, b, N_BUCKETS), np.arange(rel.size)] = 1.0
    return out


def sb(ctx, nc, name, shape, dt=F32, **kw):
    return ctx.enter_context(nc.sbuf_tensor(name, shape, dt, **kw))


def banks(ctx, nc, name, n):
    return ctx.enter_context(nc.psum_tensor(name, [P, n, BANK], F32))


def phase_semaphores(ctx, nc, prefix):
    taken = []

    def clear():
        nc.clear_and_free_semaphores(taken)
        nc.all_engine_barrier()

    ctx.callback(clear)

    def sem(name):
        taken.append(nc.alloc_semaphore(name=prefix + name))
        return taken[-1]

    return sem


class Chain:

    def __init__(self, eng, sem, base=0):
        self.eng, self.sem, self.base, self.n = eng, sem, base, 0

    def __call__(self, ins):
        self.n += 1
        ins.then_inc(self.sem, 1)
        self.eng.wait_ge(self.sem, self.base + self.n)
        return ins


def gemm(nc, name, weights, parts, k, n_cols, finish, on_vector=False):
    split = SPLIT if n_cols == W else 1
    wn = n_cols // split
    total = sum(n for _, n, _ in parts)
    stores, has_aux = "dram" in parts[0][2], "aux" in parts[0][2]
    with ExitStack() as ctx:
        ring = sb(ctx, nc, name + "_ring", [P, 2, k * P])
        stage = sb(ctx, nc, name + "_stage", [P, 2, n_cols])
        aux = sb(ctx, nc, name + "_aux", [P, 2, n_cols]) if has_aux else None
        psum = banks(ctx, nc, name + "_psum", 2 * split).ap().rearrange("p (s n) c -> p s n c", s=2)
        sem = phase_semaphores(ctx, nc, name)
        w_in = [sem("_w_in0"), sem("_w_in1")]
        aux_in = [sem("_aux_in0"), sem("_aux_in1")]
        mm_done = sem("_mm_done")
        finished = sem("_finished")
        stored = [sem("_stored0"), sem("_stored1")]
        chain = sem("_chain")
        block = ctx.enter_context(nc.Block())
        thirds = lambda ap: ap.rearrange("p (n c) -> p n c", n=split)

        def steps(eng, body):
            done = 0
            for first, n, args in parts:
                if n >= 2:
                    with eng.Fori(0, n // 2) as i:
                        for s in range(2):
                            body(i * 2 + (done + s), (done + s) % 2, i * 2 + (first + s), args, i * 2 + s)
                if n % 2:
                    body(done + n - 1, (done + n - 1) % 2, first + n - 1, args, n - 1)
                done += n

        def slot_uses(step, slot):
            return step // 2 if isinstance(step, int) else (step - slot) // 2

        @block.sync
        def _(sp):
            def load(step, slot, tile, args, j):
                sp.wait_ge(mm_done, step + 1)
                sp.dma_start(ring[:, slot, :], weights[bass.DynSlice(tile, 1), :, :].rearrange("a p n -> (a p) n")
                             ).then_inc(w_in[slot], 16)
                if has_aux:
                    sp.wait_ge(finished, step + 1)
                    sp.dma_start(aux[:, slot, :], args["aux"][bass.DynSlice(j + args["aux_at"], 1), :, :].rearrange("a p n -> (a p) n")
                                 ).then_inc(aux_in[slot], 16)
            steps(sp, load)

        @block.tensor
        def _(pe):
            pe.sem_inc(mm_done, 2)

            def mult(step, slot, tile, args, j):
                pe.wait_ge(w_in[slot], slot_uses(step, slot) * 16 + 16)
                pe.wait_ge(finished, step + 1)
                for n in range(split):
                    for c in range(k):
                        last = nc.tensor.matmul(psum[:, slot, n, 0:wn], ring[:, slot, c * P:(c + 1) * P],
                                                args["rhs"][:, c, n * wn:(n + 1) * wn], start=c == 0, stop=c == k - 1)
                last.then_inc(mm_done, 1)
            steps(pe, mult)

        def take_out(eng):
            eng.sem_inc(finished, 2)

            def evacuate(step, slot, tile, args, j):
                eng.wait_ge(mm_done, step + 3)
                if stores:
                    eng.wait_ge(stored[slot], slot_uses(step, slot) * 16)
                if has_aux:
                    eng.wait_ge(aux_in[slot], slot_uses(step, slot) * 16 + 16)
                finish(nc, eng, psum[:, slot, :, 0:wn], thirds(stage[:, slot, :]),
                       thirds(aux[:, slot, :]) if has_aux else None, args, j, step, chain).then_inc(finished, 1)
                if stores:
                    eng.wait_ge(finished, step + 3)
                    eng.dma_start(args["dram"][bass.DynSlice(j + args.get("at", 0), 1), :, :].rearrange("a p n -> (a p) n"),
                                  stage[:, slot, :]).then_inc(stored[slot], 16)
            steps(eng, evacuate)
            if stores:
                for slot in range(2):
                    eng.wait_ge(stored[slot], (total + 1 - slot) // 2 * 16)

        if on_vector:
            @block.vector
            def _(dve):
                take_out(dve)
        else:
            @block.scalar
            def _(act):
                take_out(act)


def tile_of(buf, j):
    return buf[:, bass.DynSlice(j, 1), :].rearrange("p a (n c) -> p (a n) c", n=SPLIT)


def finish_copy(nc, act, psum, stage, aux, args, j, step, chain):
    return nc.scalar.activation(stage, psum, args["func"], scale=args.get("scale", 1.0))


def finish_square(nc, act, psum, stage, aux, args, j, step, chain):
    nc.scalar.activation(stage, psum, ACT.Relu).then_inc(chain, 1)
    act.wait_ge(chain, step + 1)
    return nc.scalar.activation(tile_of(args["out"], j), stage, ACT.Square)


def finish_residual(nc, dve, psum, stage, aux, args, j, step, chain):
    out = tile_of(args["out"], j)
    return nc.vector.tensor_tensor(out, out, psum, ALU.add)


def finish_gated(nc, dve, psum, stage, aux, args, j, step, chain):
    if args["first"]:
        return nc.vector.tensor_tensor(tile_of(args["out"], j), psum, aux, ALU.mult)
    nc.vector.tensor_tensor(stage, psum, aux, ALU.mult).then_inc(chain, 1)
    dve.wait_ge(chain, step - (CHUNKS - 1))
    out = tile_of(args["out"], j)
    return nc.vector.tensor_tensor(out, out, stage, ALU.add)


def rmsnorm(nc, name, x, gain, ones, h, sq_buf):
    with ExitStack() as ctx:
        rstd = sb(ctx, nc, name + "_rstd", [P, W])
        psum = banks(ctx, nc, name + "_psum", SPLIT)
        sem = phase_semaphores(ctx, nc, name)
        sq_ready, summed, mean_ready, root_ready, chain = (sem(s) for s in
            ("_sq_ready", "_summed", "_mean_ready", "_root_ready", "_chain"))
        block = ctx.enter_context(nc.Block())

        @block.scalar
        def _(act):
            for c in range(CHUNKS):
                if c >= 2:
                    act.wait_ge(summed, c - 1)
                act.activation(sq_buf[:, c % 2, :], x[:, c, :], ACT.Square).then_inc(sq_ready, 1)
            act.wait_ge(mean_ready, 1)
            act.activation(rstd[:, :], rstd[:, :], ACT.Sqrt).then_inc(root_ready, 1)

        @block.tensor
        def _(pe):
            for c in range(CHUNKS):
                pe.wait_ge(sq_ready, c + 1)
                for n in range(SPLIT):
                    last = nc.tensor.matmul(psum[:, n, 0:WN], ones[:, :], sq_buf[:, c % 2, n * WN:(n + 1) * WN],
                                            start=c == 0, stop=c == CHUNKS - 1)
                last.then_inc(summed, 1)

        @block.vector
        def _(dve):
            link = Chain(dve, chain)
            dve.wait_ge(summed, CHUNKS)
            link(nc.vector.tensor_scalar(rstd[:, :].rearrange("p (n c) -> p n c", n=SPLIT), psum[:, :, 0:WN],
                                         1.0 / D, EPS, ALU.mult, ALU.add))
            nc.vector.reciprocal(rstd[:, :], rstd[:, :]).then_inc(mean_ready, 1)
            dve.wait_ge(root_ready, 1)
            for c in range(CHUNKS):
                nc.vector.scalar_tensor_tensor(out=h[:, c, :], in0=x[:, c, :], scalar=gain[:, c:c + 1],
                                               in1=rstd[:, :], op0=ALU.mult, op1=ALU.mult)


def load_all(nc, name, pairs):
    with ExitStack() as ctx:
        landed = phase_semaphores(ctx, nc, name)("_landed")
        block = ctx.enter_context(nc.Block())

        @block.sync
        def _(sp):
            for dst, src in pairs[0::2]:
                sp.dma_start(dst, src).then_inc(landed, 16)
            sp.wait_ge(landed, 16 * len(pairs))

        @block.scalar
        def _(act):
            for dst, src in pairs[1::2]:
                act.dma_start(dst, src).then_inc(landed, 16)


def conv_module(nc, u, t, ones, out, conv_out):
    CT, PAD = CONV_CH // P, CONV_W - 1
    with ExitStack() as ctx:
        val = sb(ctx, nc, "glu_value", [P, CT, W])
        gate = sb(ctx, nc, "glu_gate", [P, CT, W])
        gp = sb(ctx, nc, "glu_prompt", [P, CT, PAD + TP])
        gs = sb(ctx, nc, "glu_sample", [P, CT, NB, PAD + TS])
        taps = sb(ctx, nc, "conv_a_taps", [P, CONV_W, CT])
        vecs = sb(ctx, nc, "conv_a_vecs", [P, 3, CT])
        rstd = sb(ctx, nc, "ln_rstd", [P, W])
        psum = banks(ctx, nc, "ln_psum", 2 * SPLIT).ap().rearrange("p (s n) c -> p s n c", s=2)
        sem = phase_semaphores(ctx, nc, "conv_a_")
        params_in = sem("params_in")
        tile_in = [sem(f"tile_in{c}") for c in range(CT)]
        gate_ready, glu_ready, conv_done, summed, centred, sq_ready, sq_summed, var_ready, root_ready, scaled, out_done, chain, states_out = (
            sem(s) for s in ("gate_ready", "glu_ready", "conv_done", "summed", "centred", "sq_ready", "sq_summed",
                             "var_ready", "root_ready", "scaled", "out_done", "chain", "states_out"))
        block = ctx.enter_context(nc.Block())
        thirds = lambda ap: ap.rearrange("p (n c) -> p n c", n=SPLIT)

        @block.sync
        def _(sp):
            sp.dma_start(taps[:, :, :], t["conv_a_w"]).then_inc(params_in, 16)
            sp.dma_start(vecs[:, :, :], t["conv_a_vecs"]).then_inc(params_in, 16)
            for c in range(CT):
                sp.dma_start(val[:, c, :], u[T_A + c]).then_inc(tile_in[c], 16)
                sp.dma_start(gate[:, c, :], u[T_AG + c]).then_inc(tile_in[c], 16)
                sp.dma_start(gs[:, c, :, 0:PAD], t["state_conv_a"][c]).then_inc(tile_in[c], 16)
            sp.wait_ge(glu_ready, CT)
            for c in range(CT):
                sp.dma_start(conv_out[0][c], gp[:, c, TP:TP + PAD]).then_inc(states_out, 16)
                sp.dma_start(conv_out[1][c], gs[:, c, :, TS:TS + PAD]).then_inc(states_out, 16)
            sp.wait_ge(states_out, 32 * CT)

        @block.scalar
        def _(act):
            for c in range(CT):
                act.wait_ge(tile_in[c], 48)
                act.activation(gate[:, c, :], gate[:, c, :], ACT.Sigmoid).then_inc(gate_ready, 1)
            for c in range(CT):
                act.wait_ge(centred, c + 1)
                act.activation(val[:, c, :], out[:, c, :], ACT.Square).then_inc(sq_ready, 1)
            act.wait_ge(var_ready, 1)
            act.activation(rstd[:, :], rstd[:, :], ACT.Sqrt).then_inc(root_ready, 1)
            for c in range(CT):
                act.wait_ge(scaled, c + 1)
                act.activation(out[:, c, :], out[:, c, :], ACT.Silu, bias=vecs[:, 2, c:c + 1]).then_inc(out_done, 1)
            act.wait_ge(out_done, CT)

        @block.tensor
        def _(pe):
            for c in range(CT):
                pe.wait_ge(conv_done, c + 1)
                for n in range(SPLIT):
                    last = nc.tensor.matmul(psum[:, 0, n, 0:WN], ones[:, :], out[:, c, n * WN:(n + 1) * WN],
                                            start=c == 0, stop=c == CT - 1)
                last.then_inc(summed, 1)
            for c in range(CT):
                pe.wait_ge(sq_ready, c + 1)
                for n in range(SPLIT):
                    last = nc.tensor.matmul(psum[:, 1, n, 0:WN], ones[:, :], val[:, c, n * WN:(n + 1) * WN],
                                            start=c == 0, stop=c == CT - 1)
                last.then_inc(sq_summed, 1)

        @block.vector
        def _(dve):
            link = Chain(dve, chain)
            link(nc.vector.memset(gp[:, :, 0:PAD], 0.0))
            dve.wait_ge(params_in, 32)
            for c in range(CT):
                dve.wait_ge(gate_ready, c + 1)
                link(nc.vector.tensor_tensor(gp[:, c, PAD:PAD + TP], val[:, c, 0:TP], gate[:, c, 0:TP], ALU.mult))
                nc.vector.tensor_tensor(gs[:, c, :, PAD:PAD + TS], val[:, c, TP:W].rearrange("p (b s) -> p b s", b=NB),
                                        gate[:, c, TP:W].rearrange("p (b s) -> p b s", b=NB), ALU.mult).then_inc(glu_ready, 1)
                dve.wait_ge(glu_ready, c + 1)
                yp = out[:, c, 0:TP]
                ys = out[:, c, TP:W].rearrange("p (b s) -> p b s", b=NB)
                for k in range(CONV_W):
                    w = taps[:, k, c:c + 1]
                    last = None
                    for y, src in ((yp, gp[:, c, k:k + TP]), (ys, gs[:, c, :, k:k + TS])):
                        if k == 0:
                            last = nc.vector.tensor_scalar(y, src, w, vecs[:, 0, c:c + 1], ALU.mult, ALU.add)
                        else:
                            last = nc.vector.scalar_tensor_tensor(out=y, in0=src, scalar=w, in1=y,
                                                                  op0=ALU.mult, op1=ALU.add)
                        if y is yp:
                            last.then_inc(chain, 1)
                    link.n += 2
                    last.then_inc(chain, 1)
                    dve.wait_ge(chain, link.n)
                dve.sem_inc(conv_done, 1)
            dve.wait_ge(summed, CT)
            for c in range(CT):
                nc.vector.scalar_tensor_tensor(out=thirds(out[:, c, :]), in0=psum[:, 0, :, 0:WN], scalar=-1.0 / CONV_CH,
                                               in1=thirds(out[:, c, :]), op0=ALU.mult, op1=ALU.add).then_inc(centred, 1)
            dve.wait_ge(sq_summed, CT)
            link(nc.vector.tensor_scalar(thirds(rstd[:, :]), psum[:, 1, :, 0:WN], 1.0 / CONV_CH, EPS, ALU.mult, ALU.add))
            nc.vector.reciprocal(rstd[:, :], rstd[:, :]).then_inc(var_ready, 1)
            dve.wait_ge(root_ready, 1)
            dve.wait_ge(centred, CT)
            for c in range(CT):
                nc.vector.scalar_tensor_tensor(out=out[:, c, :], in0=out[:, c, :], scalar=vecs[:, 1, c:c + 1],
                                               in1=rstd[:, :], op0=ALU.mult, op1=ALU.mult).then_inc(scaled, 1)


def gdn_inputs(nc, u, t, ones, ident, qkv, by_token, conv_out):
    NTILE, PAD = 12, GDN_CONV_W - 1
    RING = 3
    with ExitStack() as ctx:
        xp = sb(ctx, nc, "short_prompt", [P, RING, PAD + TP])
        xs = sb(ctx, nc, "short_sample", [P, RING, NB, PAD + TS])
        sq = sb(ctx, nc, "qk_sq", [P, 2, W])
        rn = sb(ctx, nc, "qk_rnorm", [P, 2, W])
        taps = sb(ctx, nc, "short_taps", [P, GDN_CONV_W, NTILE])
        misc = sb(ctx, nc, "misc", [64, W])
        mabs = sb(ctx, nc, "misc_abs", [64, W])
        avec = sb(ctx, nc, "decay_vecs", [64, 3])
        psum = banks(ctx, nc, "qk_psum", 2 * SPLIT).ap().rearrange("p (s n) c -> p s n c", s=2)
        tpsum = banks(ctx, nc, "misc_psum", 1)
        sem = phase_semaphores(ctx, nc, "gdn_in_")
        params_in, misc_in, states_out = sem("params_in"), sem("misc_in"), sem("states_out")
        tile_in = [sem(f"tile_in{c}") for c in range(RING)]
        states_sent = [sem(f"states_sent{c}") for c in range(RING)]
        padded, conv_done, silu_done, sq_ready, sq_summed, mean_ready, root_ready, chain, achain, misc_ready, turned = (
            sem(s) for s in ("padded", "conv_done", "silu_done", "sq_ready", "sq_summed", "mean_ready", "root_ready",
                             "chain", "achain", "misc_ready", "turned"))
        block = ctx.enter_context(nc.Block())
        thirds = lambda ap: ap.rearrange("p (n c) -> p n c", n=SPLIT)
        A = slice(32, 36)

        @block.sync
        def _(sp):
            sp.dma_start(misc[0:32, :], u[T_MISC, 0:32, :]).then_inc(misc_in, 16)
            sp.dma_start(misc[A, :], u[T_MISC, 0:4, :]).then_inc(misc_in, 16)
            sp.dma_start(avec[A, 0:2], t["decay_vecs"]).then_inc(misc_in, 16)
            sp.dma_start(taps[:, :, :], t["gdn_conv_w"]).then_inc(params_in, 16)
            for c in range(NTILE):
                s = c % RING
                if c >= RING:
                    sp.wait_ge(conv_done, c - RING + 1)
                    sp.wait_ge(states_sent[s], 32 * (c // RING))
                sp.dma_start(xp[:, s, PAD:PAD + TP], u[T_QKV + c, :, 0:TP]).then_inc(tile_in[s], 16)
                sp.dma_start(xs[:, s, :, 0:PAD], t["state_conv_qkv"][c]).then_inc(tile_in[s], 16)
                sp.dma_start(xs[:, s, :, PAD:PAD + TS], u[T_QKV + c, :, TP:W].rearrange("p (b s) -> p b s", b=NB)
                             ).then_inc(tile_in[s], 16)

        @block.gpsimd
        def _(pool):
            nc.gpsimd.memset(xp[:, :, 0:PAD], 0.0).then_inc(padded, 1)

        @block.scalar
        def _(act):
            def send_state(c):
                s = c % RING
                act.wait_ge(tile_in[s], 48 * (c // RING + 1))
                act.dma_start(conv_out[0][c], xp[:, s, TP:TP + PAD]).then_inc(states_sent[s], 16)
                act.dma_start(conv_out[1][c], xs[:, s, :, TS:TS + PAD]).then_inc(states_sent[s], 16)
            for c in range(NTILE):
                send_state(c)
                act.wait_ge(conv_done, c + 1)
                act.activation(qkv[:, c, :], qkv[:, c, :], ACT.Silu).then_inc(silu_done, 1)
            link = Chain(act, achain)
            act.wait_ge(misc_in, 48)
            link(act.activation(mabs[A, :], misc[A, :], ACT.Abs, bias=avec[A, 1:2]))
            link(act.activation(misc[0:32, :], misc[0:32, :], ACT.Sigmoid))
            link(act.activation(mabs[A, :], mabs[A, :], ACT.Exp, scale=-1.0))
            link(act.activation(avec[A, 2:3], avec[A, 0:1], ACT.Exp))
            link(act.activation(mabs[A, :], mabs[A, :], ACT.Ln, bias=1.0))
            act.wait_ge(silu_done, 8)
            for c in range(8 + 2):
                if c >= 2:
                    act.wait_ge(mean_ready, c - 1)
                    act.activation(rn[:, c % 2, :], rn[:, c % 2, :], ACT.Sqrt).then_inc(root_ready, 1)
                if c < 8:
                    act.activation(sq[:, c % 2, :], qkv[:, c, :], ACT.Square).then_inc(sq_ready, 1)
            for s in range(RING):
                act.wait_ge(states_sent[s], 32 * (NTILE // RING))

        @block.tensor
        def _(pe):
            for c in range(8):
                pe.wait_ge(sq_ready, c + 1)
                if c >= 2:
                    pe.wait_ge(mean_ready, c - 1)
                for n in range(SPLIT):
                    last = nc.tensor.matmul(psum[:, c % 2, n, 0:WN], ones[:, :], sq[:, c % 2, n * WN:(n + 1) * WN],
                                            start=True, stop=True)
                last.then_inc(sq_summed, 1)
            pe.wait_ge(misc_ready, 1)
            for i in range(NT + 1):
                n = P if i < NT else NB * TS
                last = nc.tensor.transpose(tpsum[0:n, 0, i * 36:(i + 1) * 36], misc[0:36, i * P:i * P + n], ident[0:36, 0:36])
            last.then_inc(turned, 1)

        @block.vector
        def _(dve):
            link = Chain(dve, chain)
            dve.wait_ge(params_in, 16)
            dve.wait_ge(padded, 1)
            for c in range(NTILE):
                s = c % RING
                dve.wait_ge(tile_in[s], 48 * (c // RING + 1))
                yp = qkv[:, c, 0:TP]
                ys = qkv[:, c, TP:W].rearrange("p (b s) -> p b s", b=NB)
                for k in range(GDN_CONV_W):
                    w = taps[:, k, c:c + 1]
                    for y, src in ((yp, xp[:, s, k:k + TP]), (ys, xs[:, s, :, k:k + TS])):
                        if k == 0:
                            last = nc.vector.tensor_scalar(y, src, w, None, ALU.mult)
                        else:
                            last = nc.vector.scalar_tensor_tensor(out=y, in0=src, scalar=w, in1=y,
                                                                  op0=ALU.mult, op1=ALU.add)
                        if k < GDN_CONV_W - 1 or y is yp:
                            last.then_inc(chain, 1)
                            link.n += 1
                        else:
                            last.then_inc(conv_done, 1)
                    dve.wait_ge(chain, link.n)
            dve.wait_ge(achain, 5)
            link(nc.vector.tensor_scalar(misc[A, :], misc[A, :], avec[A, 1:2], 0.0, ALU.add, ALU.max))
            link(nc.vector.tensor_tensor(misc[A, :], misc[A, :], mabs[A, :], ALU.add))
            nc.vector.tensor_scalar(misc[A, :], misc[A, :], avec[A, 2:3], -1.0, ALU.mult, ALU.mult).then_inc(misc_ready, 1)
            for c in range(8):
                dve.wait_ge(sq_summed, c + 1)
                if c >= 2:
                    dve.wait_ge(chain, link.n)
                link(nc.vector.tensor_scalar(thirds(rn[:, c % 2, :]), psum[:, c % 2, :, 0:WN], EPS, None, ALU.add))
                nc.vector.reciprocal(rn[:, c % 2, :], rn[:, c % 2, :]).then_inc(mean_ready, 1)
                dve.wait_ge(root_ready, c + 1)
                scale = float(P) ** -0.5 if c < GH else 1.0
                link(nc.vector.scalar_tensor_tensor(out=qkv[:, c, :], in0=qkv[:, c, :], scalar=scale, in1=rn[:, c % 2, :],
                                                    op0=ALU.mult, op1=ALU.mult))
            dve.wait_ge(turned, 1)
            link(nc.vector.tensor_copy(by_token[:, 0:NT, :], tpsum[:, 0, 0:NT * 36].rearrange("p (t c) -> p t c", c=36)))
            link(nc.vector.tensor_copy(by_token[0:NB * TS, NT, :], tpsum[0:NB * TS, 0, NT * 36:(NT + 1) * 36]))


def delta_rule(nc, name, qkv, by_token, ones, ident, masks, t_dram, n, levels, tiles, at, out, state_out, batches=0):
    H, Q = GH, GH * n
    CH = 3
    with ExitStack() as ctx:
        S = lambda nm, shape: sb(ctx, nc, name + "_" + nm, shape)
        tri, bound, lmask = S("tri", [n, n]), S("bound", [n, n]), S("lmask", [n, levels, n])
        qs, ks, vs = S("q", [P, H, n]), S("k", [P, H, n]), S("v", [P, H, n])
        gu, bi = S("gu", [n, H, n]), S("bi", [n, H, n])
        gc, egc, be = S("gc", [n, H]), S("egc", [n, H]), S("be", [n, H])
        dt_, egrow = S("dt", [n, H, n]), S("egrow", [P, H, n])
        at_, atl, qkt = S("at", [n, H, n]), S("atl", [n, levels, H, n]), S("qkt", [n, H, n])
        ys, x, xt = S("y", [n, H, n]), S("x", [n, H, n]), S("xt", [n, H, n])
        kbg, vb, kd, qg = S("kbg", [n, H, P]), S("vb", [n, H, P]), S("kd", [n, H, P]), S("qg", [P, H, n])
        vw, kcd, vn = S("vw", [n, H, P]), S("kcd", [P, H, n]), S("vn", [n, H, P])
        dend = S("dend", [n, H])
        if batches:
            bmask, rmask = S("bmask", [P, batches, n]), S("rmask", [n, batches])
            state = S("state", [P, batches, H, P])
            kcdm, vexp, oin = S("kcdm", [P, H, batches, n]), S("vexp", [n, H, batches, P]), S("oin", [P, H, n])
        else:
            state = S("state", [P, H, P])
        ps = banks(ctx, nc, name + "_psum", 8)
        hv = lambda b, p=P, w=n: ps[0:p, b, 0:H * w].rearrange("p (h c) -> p h c", h=H)
        ROW, BETA, COL, KK, KQ, KT, VT, Y = range(8)
        XY, YX, VW, KCD, P1, OUT, DS = KK, KQ, KT, VT, Y, ROW, BETA
        sem = phase_semaphores(ctx, nc, name + "_")
        (params_in, state_ready, in_ready, gu_ready, pre_mm, gc_ready, egc_ready, diff_ready, dt_ready, egrow_ready,
         at_ready, level_ready, factors_ready, y_mm, y_ready, xy_mm, x_ready, sol_mm, sol_ready, p1_mm, vn_ready,
         o_mm, o_out, ds_mm, chain, updated, sent) = (sem(s) for s in (
            "params_in", "state_ready", "in_ready", "gu_ready", "pre_mm", "gc_ready", "egc_ready", "diff_ready",
            "dt_ready", "egrow_ready", "at_ready", "level_ready", "factors_ready", "y_mm", "y_ready", "xy_mm",
            "x_ready", "sol_mm", "sol_ready", "p1_mm", "vn_ready", "o_mm", "o_out", "ds_mm", "chain", "updated", "sent"))
        block = ctx.enter_context(nc.Block())
        wide = lambda ap, k: ap.unsqueeze(2).to_broadcast([ap.shape[0], ap.shape[1], k])
        heads = lambda ap: ap.unsqueeze(1).to_broadcast([ap.shape[0], H, ap.shape[1]])

        def tile_loop(eng, body):
            if tiles == 1:
                body(0)
            else:
                with eng.Fori(0, tiles) as t:
                    body(t)

        @block.sync
        def _(sp):
            sp.dma_start(tri[:, :], masks["tri"]).then_inc(params_in, 16)
            sp.dma_start(bound[:, :], masks["bound"]).then_inc(params_in, 16)
            sp.dma_start(lmask[:, :, :], masks["levels"]).then_inc(params_in, 16)
            if batches:
                sp.dma_start(bmask[:, :, :], masks["batch_cols"]).then_inc(params_in, 16)
                sp.dma_start(rmask[:, :], masks["batch_rows"]).then_inc(params_in, 16)
                sp.dma_start(state[:, :, :, :], t_dram["state_gdn"]).then_inc(state_ready, 16)
            if batches:
                sp.wait_ge(updated, 2 * H)
            else:
                sp.wait_ge(state_ready, tiles + 1)
            sp.dma_start(state_out, state.ap()).then_inc(sent, 16)
            sp.wait_ge(sent, 16)

        @block.scalar
        def _(act):
            def body(t):
                if not batches:
                    act.wait_ge(state_ready, t + 1)
                cols = bass.DynSlice(t * n + at, n)
                act.activation(qs[:, :, :], qkv[:, 0:4, cols], ACT.Copy)
                act.activation(ks[:, :, :], qkv[:, 4:8, cols], ACT.Copy)
                act.activation(vs[:, :, :], qkv[:, 8:12, cols], ACT.Copy).then_inc(in_ready, 1)
                act.wait_ge(pre_mm, t + 1)
                act.activation(egrow[:, :, :], hv(ROW), ACT.Exp).then_inc(egrow_ready, 1)
                act.wait_ge(gc_ready, t + 1)
                act.activation(egc[:, :], gc[:, :], ACT.Exp).then_inc(egc_ready, 1)
                act.wait_ge(diff_ready, t + 1)
                act.activation(dt_[:, :, :], dt_[:, :, :], ACT.Exp).then_inc(dt_ready, 1)
                for l in range(levels):
                    act.wait_ge(y_mm, t * levels + l + 1)
                    act.activation(ys[:, :, :], hv(Y, n), ACT.Copy).then_inc(y_ready, 1)
                act.wait_ge(sol_mm, t + 1)
                act.activation(vw[:, :, :], hv(VW, n, P), ACT.Copy)
                act.activation(kcd[:, :, :], hv(KCD), ACT.Copy).then_inc(sol_ready, 1)
                act.wait_ge(o_mm, t + 1)
                if batches:
                    act.activation(oin[:, :, :], hv(COL), ACT.Copy).then_inc(o_out, 1)
                else:
                    act.activation(out[:, :, cols], hv(OUT), ACT.Copy).then_inc(o_out, 1)
            tile_loop(act, body)

        @block.gpsimd
        def _(pool):
            pool.wait_ge(params_in, 80 if batches else 48)

            def body(t):
                pool.wait_ge(at_ready, t + 1)
                for l in range(levels):
                    nc.gpsimd.tensor_tensor(atl[:, l, :, :], at_[:, :, :], heads(lmask[:, l, :]), ALU.mult
                                            ).then_inc(level_ready, 1)
                pool.wait_ge(level_ready, (t + 1) * levels)
            tile_loop(pool, body)

        @block.tensor
        def _(pe):
            mm = nc.tensor.matmul

            def body(t):
                pe.wait_ge(in_ready, t + 1)
                pe.wait_ge(gu_ready, t + 1)
                mm(ps[:, ROW, 0:Q], ones[0:n, :], gu[:, :, :], start=True, stop=True)
                mm(ps[0:n, BETA, 0:Q], ones[0:n, 0:n], bi[:, :, :], start=True, stop=True)
                mm(ps[0:n, COL, 0:H], tri[:, :], by_token[0:n, bass.DynSlice(t + at // P, 1), 32:36].rearrange("p a h -> p (a h)"),
                   start=True, stop=True)
                for h in range(H):
                    mm(hv(KK, n)[:, h, :], ks[:, h, :], ks[:, h, :], start=True, stop=True)
                for h in range(H):
                    mm(hv(KQ, n)[:, h, :], ks[:, h, :], qs[:, h, :], start=True, stop=True)
                for h in range(H):
                    nc.tensor.transpose(hv(KT, n, P)[:, h, :], ks[:, h, :], ident[:, :])
                for h in range(H):
                    last = nc.tensor.transpose(hv(VT, n, P)[:, h, :], vs[:, h, :], ident[:, :])
                last.then_inc(pre_mm, 1)
                for l in range(levels):
                    pe.wait_ge(level_ready, t * levels + l + 1)
                    if l:
                        pe.wait_ge(x_ready, t * levels + l)
                    for h in range(H):
                        last = mm(hv(Y, n)[:, h, :], atl[:, l, h, :], x[:, h, :] if l else ident[0:n, 0:n],
                                  start=True, stop=True)
                    last.then_inc(y_mm, 1)
                    pe.wait_ge(y_ready, t * levels + l + 1)
                    if l < levels - 1:
                        for h in range(H):
                            mm(hv(XY, n)[:, h, :], xt[:, h, :] if l else ident[0:n, 0:n], ys[:, h, :], start=True, stop=True)
                    for h in range(H):
                        last = mm(hv(YX, n)[:, h, :], ys[:, h, :], xt[:, h, :] if l else ident[0:n, 0:n],
                                  start=True, stop=True)
                    last.then_inc(xy_mm, 1)
                pe.wait_ge(x_ready, (t + 1) * levels)
                pe.wait_ge(factors_ready, t + 1)
                for h in range(H):
                    mm(hv(VW, n, P)[:, h, :], xt[:, h, :], vb[:, h, :], start=True, stop=True)
                for h in range(H):
                    last = mm(hv(KCD)[:, h, :], kbg[:, h, :], xt[:, h, :], start=True, stop=True)
                last.then_inc(sol_mm, 1)
                if batches:
                    pe.wait_ge(state_ready, 16)
                    pe.wait_ge(vn_ready, 1)
                    for h in range(H):
                        for b in range(batches):
                            last = mm(hv(P1, n, P)[:, h, :], kcdm[:, h, b, :], state[:, b, h, :],
                                      start=b == 0, stop=b == batches - 1)
                    last.then_inc(p1_mm, 1)
                    for h in range(H):
                        for b in range(batches):
                            w = n // batches
                            mm(hv(OUT)[:, h, b * w:(b + 1) * w], state[:, b, h, :], qg[:, h, b * w:(b + 1) * w],
                               start=True, stop=True)
                    pe.wait_ge(vn_ready, 2)
                    for h in range(H):
                        last = mm(hv(COL)[:, h, :], vn[:, h, :], qkt[:, h, :], start=True, stop=True)
                    last.then_inc(o_mm, 1)
                    for h in range(H):
                        pe.wait_ge(vn_ready, 3 + h)
                        if h >= 1:
                            pe.wait_ge(updated, 2 * h)
                        for half in range(2):
                            last = mm(ps[:, KQ + half, :], kd[:, h, :],
                                      vexp[:, h, half * 4:(half + 1) * 4, :], start=True, stop=True)
                        last.then_inc(ds_mm, 1)
                else:
                    pe.wait_ge(sol_ready, t + 1)
                    for h in range(H):
                        last = mm(hv(P1, n, P)[:, h, :], kcd[:, h, :], state[:, h, :], start=True, stop=True)
                    last.then_inc(p1_mm, 1)
                    pe.wait_ge(vn_ready, t + 1)
                    for h in range(H):
                        last = mm(hv(DS, P, P)[:, h, :], kd[:, h, :], vn[:, h, :], start=True, stop=True)
                    for h in range(H):
                        mm(hv(OUT)[:, h, :], state[:, h, :], qg[:, h, :], start=True, stop=False)
                        last = mm(hv(OUT)[:, h, :], vn[:, h, :], qkt[:, h, :], start=False, stop=True)
                    last.then_inc(o_mm, 1)
            tile_loop(pe, body)

        @block.vector
        def _(dve):
            V = nc.vector
            dve.wait_ge(params_in, 80 if batches else 48)
            if not batches:
                V.memset(state[:, :, :], 0.0).then_inc(state_ready, 1)
                dve.wait_ge(state_ready, 1)

            def body(t):
                cols = by_token[0:n, bass.DynSlice(t + at // P, 1), :].rearrange("p a c -> p (a c)")
                g, beta = cols[:, 32:36], cols[:, 4:8]
                V.tensor_tensor(gu[:, :, :], heads(tri[:, :]), wide(g, n), ALU.mult)
                V.tensor_tensor(bi[:, :, :], heads(ident[0:n, 0:n]), wide(beta, n), ALU.mult).then_inc(gu_ready, 1)
                dve.wait_ge(pre_mm, t + 1)
                V.tensor_copy(gc[:, :], ps[0:n, COL, 0:H]).then_inc(gc_ready, 1)
                dve.wait_ge(gc_ready, t + 1)
                dve.wait_ge(egrow_ready, t + 1)
                for h in range(H):
                    last = V.scalar_tensor_tensor(out=dt_[:, h, :], in0=hv(ROW, n)[:, h, :], scalar=gc[:, h:h + 1],
                                                  in1=bound[:, :], op0=ALU.subtract, op1=ALU.min)
                last.then_inc(diff_ready, 1)
                dve.wait_ge(dt_ready, t + 1)
                V.tensor_tensor(at_[:, :, :], hv(KK, n), dt_[:, :, :], ALU.mult).then_inc(chain, 1)
                V.tensor_tensor(qkt[:, :, :], hv(KQ, n), dt_[:, :, :], ALU.mult)
                if batches:
                    V.tensor_reduce(dend[:, :], dt_[:, :, TS - 1::TS], AX_X, ALU.add).then_inc(chain, 1)
                else:
                    V.tensor_copy(dend[:, :], dt_[:, :, n - 1]).then_inc(chain, 1)
                dve.wait_ge(chain, t * CH + 2)
                V.tensor_tensor(at_[:, :, :], at_[:, :, :], hv(BETA, n), ALU.mult).then_inc(at_ready, 1)
                dve.wait_ge(egc_ready, t + 1)
                V.tensor_tensor(be[:, :], beta, egc[:, :], ALU.mult).then_inc(chain, 1)
                V.tensor_tensor(vb[:, :, :], hv(VT, n, P), wide(beta, P), ALU.mult)
                V.tensor_tensor(kd[:, :, :], hv(KT, n, P), wide(dend[:, :], P), ALU.mult)
                V.tensor_tensor(qg[:, :, :], qs[:, :, :], egrow[:, :, :], ALU.mult)
                dve.wait_ge(chain, t * CH + 3)
                V.tensor_tensor(kbg[:, :, :], hv(KT, n, P), wide(be[:, :], P), ALU.mult).then_inc(factors_ready, 1)
                for l in range(levels):
                    dve.wait_ge(xy_mm, t * levels + l + 1)
                    if l:
                        dve.wait_ge(x_ready, t * levels + l)
                    if l < levels - 1:
                        V.tensor_tensor(x[:, :, :], x[:, :, :] if l else heads(ident[0:n, 0:n]), hv(XY, n), ALU.subtract)
                    V.tensor_tensor(xt[:, :, :], xt[:, :, :] if l else heads(ident[0:n, 0:n]), hv(YX, n), ALU.subtract
                                    ).then_inc(x_ready, 1)
                dve.wait_ge(sol_ready, t + 1)
                if batches:
                    w = n // batches
                    for h in range(H):
                        last = V.tensor_tensor(kcdm[:, h, :, :], bmask[:, :, :],
                                               kcd[:, h, :].unsqueeze(1).to_broadcast([P, batches, n]), ALU.mult)
                    last.then_inc(vn_ready, 1)
                    dve.wait_ge(p1_mm, 1)
                    V.tensor_tensor(vn[:, :, :], vw[:, :, :], hv(P1, n, P), ALU.subtract).then_inc(vn_ready, 1)
                    dve.wait_ge(vn_ready, 2)
                    for h in range(H):
                        V.tensor_tensor(vexp[:, h, :, :], vn[:, h, :].unsqueeze(1).to_broadcast([n, batches, P]),
                                        wide(rmask[:, :], P), ALU.mult).then_inc(vn_ready, 1)
                    dve.wait_ge(o_out, 1)
                    V.tensor_tensor(out[:, :, at:at + n], oin[:, :, :], hv(OUT), ALU.add)
                    dve.wait_ge(state_ready, 16)
                    for h in range(H):
                        sh = state[:, :, h, :]
                        dve.wait_ge(p1_mm, 1)
                        dve.wait_ge(o_mm, 1)
                        V.tensor_tensor(sh, sh, wide(egrow[:, h, w - 1::w], P), ALU.mult).then_inc(updated, 1)
                        dve.wait_ge(updated, 2 * h + 1)
                        dve.wait_ge(ds_mm, h + 1)
                        V.tensor_tensor(sh, sh, ps[:, KQ:KQ + 2, :].rearrange("p a (b c) -> p (a b) c", b=4), ALU.add
                                        ).then_inc(updated, 1)
                else:
                    dve.wait_ge(p1_mm, t + 1)
                    V.tensor_tensor(vn[:, :, :], vw[:, :, :], hv(P1, n, P), ALU.subtract).then_inc(vn_ready, 1)
                    dve.wait_ge(o_mm, t + 1)
                    for h in range(H):
                        last = V.scalar_tensor_tensor(out=state[:, h, :], in0=state[:, h, :], scalar=egrow[:, h, n - 1:n],
                                                      in1=hv(DS, P, P)[:, h, :], op0=ALU.mult, op1=ALU.add)
                    last.then_inc(state_ready, 1)
                    dve.wait_ge(state_ready, t + 2)
            tile_loop(dve, body)


def gate_output(nc, o, u, ones, norm_g, out):
    with ExitStack() as ctx:
        z = sb(ctx, nc, "z", [P, GH, W])
        sq = sb(ctx, nc, "o_sq", [P, 2, W])
        rn = sb(ctx, nc, "o_rnorm", [P, 2, W])
        psum = banks(ctx, nc, "o_psum", 2 * SPLIT).ap().rearrange("p (s n) c -> p s n c", s=2)
        sem = phase_semaphores(ctx, nc, "gate_")
        z_in, z_ready, sq_ready, summed, mean_ready, root_ready, chain, scaled = (sem(s) for s in (
            "z_in", "z_ready", "sq_ready", "summed", "mean_ready", "root_ready", "chain", "scaled"))
        block = ctx.enter_context(nc.Block())
        thirds = lambda ap: ap.rearrange("p (n c) -> p n c", n=SPLIT)

        @block.sync
        def _(sp):
            sp.dma_start(z[:, :, :], u[T_Z:T_Z + GH].rearrange("h p n -> p h n")).then_inc(z_in, 16)

        @block.scalar
        def _(act):
            for h in range(GH):
                if h >= 2:
                    act.wait_ge(summed, h - 1)
                act.activation(sq[:, h % 2, :], o[:, h, :], ACT.Square).then_inc(sq_ready, 1)
            act.wait_ge(z_in, 16)
            act.activation(z[:, :, :], z[:, :, :], ACT.Silu).then_inc(z_ready, 1)
            for h in range(GH):
                act.wait_ge(mean_ready, h + 1)
                act.activation(rn[:, h % 2, :], rn[:, h % 2, :], ACT.Sqrt).then_inc(root_ready, 1)

        @block.tensor
        def _(pe):
            for h in range(GH):
                pe.wait_ge(sq_ready, h + 1)
                if h >= 2:
                    pe.wait_ge(mean_ready, h - 1)
                for n in range(SPLIT):
                    last = nc.tensor.matmul(psum[:, h % 2, n, 0:WN], ones[:, :], sq[:, h % 2, n * WN:(n + 1) * WN],
                                            start=True, stop=True)
                last.then_inc(summed, 1)

        @block.vector
        def _(dve):
            link = Chain(dve, chain)
            dve.wait_ge(z_ready, 1)
            for h in range(GH):
                dve.wait_ge(summed, h + 1)
                link(nc.vector.tensor_scalar(thirds(rn[:, h % 2, :]), psum[:, h % 2, :, 0:WN], 1.0 / P, EPS, ALU.mult, ALU.add))
                nc.vector.reciprocal(rn[:, h % 2, :], rn[:, h % 2, :]).then_inc(mean_ready, 1)
                link(nc.vector.scalar_tensor_tensor(out=z[:, h, :], in0=z[:, h, :], scalar=norm_g, in1=o[:, h, :],
                                                    op0=ALU.mult, op1=ALU.mult))
                dve.wait_ge(root_ready, h + 1)
                nc.vector.tensor_tensor(out[:, h, :], z[:, h, :], rn[:, h % 2, :], ALU.mult).then_inc(scaled, 1)
                dve.wait_ge(scaled, h + 1)


LB_FULL, LB_WIN = 1152, 768


def bias_rows(nc, t, rows, toeplitz, rb):
    L = LB_FULL + LB_WIN
    with ExitStack() as ctx:
        hot = sb(ctx, nc, "prompt_onehot", [N_BUCKETS + 1, L])
        out = sb(ctx, nc, "bias_out", [NSA_HEADS, L])
        psum = banks(ctx, nc, "bias_psum", 5)
        sem = phase_semaphores(ctx, nc, "bias_")
        hot_in, mm, copied, sent, spread = (sem(s) for s in ("hot_in", "mm", "copied", "sent", "spread"))
        block = ctx.enter_context(nc.Block())
        WB = 384

        @block.sync
        def _(sp):
            sp.dma_start(hot[:, :], t["prompt_onehot"]).then_inc(hot_in, 16)
            sp.wait_ge(copied, 1)
            sp.dma_start(rows, out[:, :]).then_inc(sent, 16)
            sp.wait_ge(sent, 16)
            for off, n, to in ((0, TP, 0), (LB_FULL, 640, TP)):
                src = bass.AP(rows.tensor, off + P - 1, [[L, NSA_HEADS], [-1, P], [1, n]])
                sp.dma_start(toeplitz[:, :, to:to + n], src).then_inc(spread, 16)
            sp.wait_ge(spread, 32)

        @block.tensor
        def _(pe):
            pe.wait_ge(hot_in, 16)
            for i in range(L // WB):
                last = nc.tensor.matmul(psum[0:NSA_HEADS, i, 0:WB], rb[:, :], hot[:, i * WB:(i + 1) * WB], start=True, stop=True)
            last.then_inc(mm, 1)

        @block.vector
        def _(dve):
            dve.wait_ge(mm, 1)
            nc.vector.tensor_copy(out[:, :].rearrange("p (n c) -> p n c", c=WB), psum[0:NSA_HEADS, :, 0:WB]).then_inc(copied, 1)


def sparse_prompt(nc, t, u, kv, toeplitz, ident, by_token, out):
    NC = TP // L_CMP
    with ExitStack() as ctx:
        kvp = sb(ctx, nc, "kv_prompt", [P, 6, TP])
        vtok = sb(ctx, nc, "v_by_token", [P, 2, NT, P])
        kc, vct = sb(ctx, nc, "k_cmp", [P, NC]), sb(ctx, nc, "v_cmp_t", [P, NC])
        vc = sb(ctx, nc, "v_cmp", [NC, P])
        with ExitStack() as c2:
            wpos = sb(c2, nc, "w_pos", [P, 2, L_CMP])
            tmp = sb(c2, nc, "cmp_tmp", [P, 2, TP])
            ps = banks(c2, nc, "nsa_prep_psum", 5)
            sem = phase_semaphores(c2, nc, "nsa_prep_")
            kv_in, w_in, cmp_ready, turned, chain, copied = (sem(s) for s in ("kv_in", "w_in", "cmp_ready", "turned", "chain", "copied"))
            block = c2.enter_context(nc.Block())

            @block.sync
            def _(sp):
                sp.dma_start(wpos[:, :, :].rearrange("p a b -> p (a b)"),
                             t["nsa_cmp_w"].partition_broadcast(P)).then_inc(w_in, 16)
                sp.dma_start(kvp[:, :, :], kv[:, :, 0:TP].rearrange("k p n -> p k n")).then_inc(kv_in, 16)

            @block.vector
            def _(dve):
                dve.wait_ge(w_in, 16)
                dve.wait_ge(kv_in, 16)
                blocks = lambda ap: ap.rearrange("p (n l) -> p n l", l=L_CMP)
                for s in range(2):
                    nc.vector.tensor_tensor(blocks(tmp[:, s, :]), blocks(kvp[:, s, :]),
                                            wpos[:, s, :].unsqueeze(1).to_broadcast([P, NC, L_CMP]), ALU.mult).then_inc(chain, 1)
                dve.wait_ge(chain, 2)
                nc.vector.tensor_reduce(kc[:, :], blocks(tmp[:, 0, :]), AX_X, ALU.add)
                nc.vector.tensor_reduce(vct[:, :], blocks(tmp[:, 1, :]), AX_X, ALU.add).then_inc(cmp_ready, 1)

            @block.tensor
            def _(pe):
                pe.wait_ge(kv_in, 16)
                for i, kind in enumerate((KV_VSLC, KV_VWIN)):
                    for b in range(NT):
                        nc.tensor.transpose(ps[:, 2 * i + b // 4, (b % 4) * P:(b % 4 + 1) * P],
                                            kvp[:, kind, b * P:(b + 1) * P], ident[:, :])
                pe.wait_ge(cmp_ready, 1)
                nc.tensor.transpose(ps[0:NC, 4, 0:P], vct[:, :], ident[:, :]).then_inc(turned, 1)

            @block.scalar
            def _(act):
                act.wait_ge(turned, 1)
                act.activation(vtok[:, :, :, :], ps[:, 0:4, :], ACT.Copy)
                act.activation(vc[:, :], ps[0:NC, 4, 0:P], ACT.Copy).then_inc(copied, 1)

        q = sb(ctx, nc, "q_heads", [P, 2, TP])
        rfull = sb(ctx, nc, "bias_full", [P, 2, 2, TP])
        rwin = sb(ctx, nc, "bias_win", [P, 2, 2, 640])
        WOFF, COFF, SW = TP, TP + 640, TP + 640 + 32
        s_ = sb(ctx, nc, "probs", [P, 2, SW])
        mx, negm, sums, scale = (sb(ctx, nc, "nsa_" + n, [P, 2, 3]) for n in ("max", "negmax", "sums", "scale"))
        idle = sb(ctx, nc, "idle", [1, 1])
        pt = sb(ctx, nc, "probs_t", [P, 2, 4, P])
        ps = banks(ctx, nc, "nsa_psum", 8)
        flat = ps.ap().rearrange("p b c -> p (b c)")
        sem = phase_semaphores(ctx, nc, "nsa_")
        loads = [sem("loads0"), sem("loads1")]
        (scores_mm, biased, negm_ready, exp_ready, chain, probs_ready, pt_mm, pt_out, pv_mm, o_out) = (sem(s) for s in (
            "scores_mm", "biased", "negm_ready", "exp_ready", "chain", "probs_ready", "pt_mm", "pt_out", "pv_mm", "o_out"))
        block = ctx.enter_context(nc.Block())

        items = [(tt, g) for tt in range(NT) for g in range(2)]

        def sizes(tt):
            return P * (tt + 1), P * min(tt + 1, 5), 4 * (tt + 1)

        def groups(tt):
            blocks = [("slc", b * P, b) for b in range(tt + 1)]
            blocks += [("win", WOFF + j * P, max(0, tt - 4) + j) for j in range(min(tt + 1, 5))]
            return [blocks[i:i + 4] for i in range(0, len(blocks), 4)] + [[("cmp", COFF, 0)]]

        first_group, NG = [], 0
        for tt, g in items:
            first_group.append(NG)
            NG += len(groups(tt))
        NI = len(items)

        def head_loop(eng, body):
            with eng.Fori(0, 2) as i:
                for s in range(2):
                    body(i * 2 + s, s, i)

        @block.sync
        def _(sp):
            def body(r, slot, i2):
                sp.wait_ge(o_out, i2 * (NI * (1 + slot)))
                sp.dma_start(q[:, slot, :], u[bass.DynSlice(r + T_Q, 1), :, 0:TP].rearrange("a p n -> (a p) n")).then_inc(loads[slot], 16)
                for g in range(2):
                    for dst, off, n in ((rfull[:, slot, g, :], 0, TP), (rwin[:, slot, g, :], TP, 640)):
                        sp.dma_start(dst, toeplitz[bass.DynSlice(r + g * GQ, 1), :, off:off + n].rearrange("a p n -> (a p) n")
                                     ).then_inc(loads[slot], 16)
            head_loop(sp, body)

        @block.tensor
        def _(pe):
            mm = nc.tensor.matmul

            def scores(r, slot, i):
                tt, g = items[i]
                nk, nw, ncmp = sizes(tt)
                if i == 0:
                    pe.wait_ge(loads[slot], (r - slot) * 40 + 80)
                pe.wait_ge(biased, r * NI + i)
                rowsg = slice(g * DH, (g + 1) * DH)
                qt = q[rowsg, slot, tt * P:(tt + 1) * P]
                for c in range(0, nk, BANK):
                    w = min(BANK, nk - c)
                    mm(flat[:, c:c + w], qt, kvp[rowsg, KV_KSLC, c:c + w], start=True, stop=True)
                k0 = max(0, tt - 4) * P
                for c in range(0, nw, BANK):
                    w = min(BANK, nw - c)
                    mm(flat[:, WOFF + c:WOFF + c + w], qt, kvp[rowsg, KV_KWIN, k0 + c:k0 + c + w], start=True, stop=True)
                mm(flat[:, COFF:COFF + ncmp], qt, kc[rowsg, 0:ncmp], start=True, stop=True).then_inc(scores_mm, 1)

            def tail(r, slot, i):
                tt, g = items[i]
                nk, nw, ncmp = sizes(tt)
                gs = groups(tt)
                pe.wait_ge(probs_ready, r * NI + (i + 1))
                pe.wait_ge(o_out, r * NI + max(i - 1, 0))
                done = 0
                for k in range(len(gs) + 1):
                    G = first_group[i] + k
                    if k < len(gs):
                        pe.wait_ge(pt_out, r * NG + max(G - 1, 0))
                        for j, (kind, col, vb) in enumerate(gs[k]):
                            w = ncmp if kind == "cmp" else P
                            last = nc.tensor.transpose(ps[0:w, 4 + G % 2, j * P:(j + 1) * P], s_[:, i % 2, col:col + w], ident[:, :])
                        last.then_inc(pt_mm, 1)
                    if k >= 1:
                        pe.wait_ge(pt_out, r * NG + G)
                        for j, (kind, col, vb) in enumerate(gs[k - 1]):
                            w = ncmp if kind == "cmp" else P
                            v = vc[0:w, :] if kind == "cmp" else vtok[:, 0 if kind == "slc" else 1, vb, :]
                            last = mm(ps[:, 6 + i % 2, 0:P], v, pt[0:w, (G - 1) % 2, j, :], start=done == 0, stop=kind == "cmp")
                            done += 1
                        last.then_inc(pv_mm, 1)

            def body(r, slot, i2):
                scores(r, slot, 0)
                for i in range(1, NI):
                    scores(r, slot, i)
                    tail(r, slot, i - 1)
                tail(r, slot, NI - 1)
            head_loop(pe, body)

        @block.vector
        def _(dve):
            V = nc.vector

            def biases(r, slot, i):
                tt, g = items[i]
                nk, nw, ncmp = sizes(tt)
                if i == 0:
                    dve.wait_ge(loads[slot], (r - slot) * 40 + 80)
                dve.wait_ge(scores_mm, r * NI + (i + 1))
                if i >= 2:
                    dve.wait_ge(pv_mm, r * NG + first_group[i - 1])
                p = i % 2
                V.memset(idle[:, :], 0.0)
                V.tensor_tensor_reduce(s_[:, p, 0:nk], flat[:, 0:nk], rfull[:, slot, g, 896 - P * tt:896 - P * tt + nk],
                                       1.0, NEG * 3, ALU.add, ALU.max, mx[:, p, 1:2])
                w0 = 512 - P * min(tt, 4)
                V.tensor_tensor_reduce(s_[:, p, WOFF:WOFF + nw], flat[:, WOFF:WOFF + nw], rwin[:, slot, g, w0:w0 + nw],
                                       1.0, NEG * 3, ALU.add, ALU.max, mx[:, p, 2:3])
                c0 = L_CMP - 1 + 896 - P * tt
                V.tensor_tensor_reduce(s_[:, p, COFF:COFF + ncmp], flat[:, COFF:COFF + ncmp],
                                       rfull[:, slot, g, c0:c0 + L_CMP * (ncmp - 1) + 1:L_CMP],
                                       1.0, NEG * 3, ALU.add, ALU.max, mx[:, p, 0:1]).then_inc(biased, 1)
                dve.wait_ge(biased, r * NI + (i + 1))
                V.tensor_scalar(negm[:, p, :], mx[:, p, :], 0.1 * NEG, -1.0, ALU.max, ALU.mult).then_inc(negm_ready, 1)

            def scales(r, slot, i):
                tt, g = items[i]
                nk, nw, ncmp = sizes(tt)
                p = i % 2
                dve.wait_ge(exp_ready, r * NI + (i + 1))
                V.tensor_scalar(scale[:, p, :], sums[:, p, :], 1e-30, None, ALU.max).then_inc(chain, 1)
                dve.wait_ge(chain, r * 3 * NI + 3 * i + 1)
                V.reciprocal(scale[:, p, :], scale[:, p, :]).then_inc(chain, 1)
                dve.wait_ge(chain, r * 3 * NI + 3 * i + 2)
                gates = by_token[:, tt, bass.DynSlice(r + (8 + g * GQ), 3, 8)]
                V.tensor_tensor(scale[:, p, :], scale[:, p, :], gates, ALU.mult).then_inc(chain, 1)
                dve.wait_ge(chain, r * 3 * NI + 3 * i + 3)
                V.tensor_scalar(s_[:, p, 0:nk], s_[:, p, 0:nk], scale[:, p, 1:2], None, ALU.mult)
                V.tensor_scalar(s_[:, p, WOFF:WOFF + nw], s_[:, p, WOFF:WOFF + nw], scale[:, p, 2:3], None, ALU.mult)
                V.tensor_scalar(s_[:, p, COFF:COFF + ncmp], s_[:, p, COFF:COFF + ncmp], scale[:, p, 0:1], None, ALU.mult
                                ).then_inc(probs_ready, 1)

            def body(r, slot, i2):
                biases(r, slot, 0)
                for i in range(1, NI):
                    biases(r, slot, i)
                    scales(r, slot, i - 1)
                scales(r, slot, NI - 1)
            head_loop(dve, body)

        @block.scalar
        def _(act):
            def exps(r, i):
                tt, g = items[i]
                nk, nw, ncmp = sizes(tt)
                p = i % 2
                act.wait_ge(negm_ready, r * NI + (i + 1))
                for x, col, n in ((1, 0, nk), (2, WOFF, nw), (0, COFF, ncmp)):
                    last = act.activation(s_[:, p, col:col + n], s_[:, p, col:col + n], ACT.Exp, bias=negm[:, p, x:x + 1],
                                          accum_out=sums[:, p, x:x + 1])
                last.then_inc(exp_ready, 1)

            def copies(r, i):
                tt, g = items[i]
                ncmp = sizes(tt)[2]
                for k, group in enumerate(groups(tt)):
                    G = first_group[i] + k
                    act.wait_ge(pt_mm, r * NG + (G + 1))
                    act.wait_ge(pv_mm, r * NG + max(G - 1, 0))
                    w, n = (ncmp, P) if group[0][0] == "cmp" else (P, P * len(group))
                    act.activation(pt[0:w, G % 2, :, :].rearrange("p a b -> p (a b)")[:, 0:n], ps[0:w, 4 + G % 2, 0:n], ACT.Copy).then_inc(pt_out, 1)
                act.wait_ge(pv_mm, r * NG + (first_group[i] + len(groups(tt))))
                half = slice(g * DH, (g + 1) * DH)
                act.activation(out[half, bass.DynSlice(r, 1), tt * P:(tt + 1) * P].rearrange("p a n -> p (a n)"),
                               ps[half, 6 + i % 2, 0:P], ACT.Copy).then_inc(o_out, 1)

            def body(r, slot, i2):
                exps(r, 0)
                for i in range(1, NI):
                    exps(r, i)
                    copies(r, i - 1)
                copies(r, NI - 1)
            head_loop(act, body)


def compress_cache(nc, t, pages, kct, vct):
    SETS, PER = 2, 8
    BPP = PAGE // L_CMP
    ROUNDS = NB * N_PAGES // (SETS * PER)
    with ExitStack() as ctx:
        ring = sb(ctx, nc, "cmp_ring", [P, SETS, PER, 2 * P])
        wsel = sb(ctx, nc, "cmp_wsel", [P, 2, BPP])
        ps = banks(ctx, nc, "cmp_psum", SETS)
        sem = phase_semaphores(ctx, nc, "cmp_")
        w_in, mm, out_k, out_v = (sem(s) for s in ("w_in", "mm", "out_k", "out_v"))
        pages_in = [sem("pages_in0"), sem("pages_in1")]
        zeroed = sem("zeroed")
        block = ctx.enter_context(nc.Block())

        @block.gpsimd
        def _(pool):
            nc.gpsimd.memset(wsel[:, :, :], 0.0).then_inc(zeroed, 1)

        @block.sync
        def _(sp):
            sp.wait_ge(zeroed, 1)
            for b in range(BPP):
                for s in range(2):
                    sp.dma_start(wsel[b * L_CMP:(b + 1) * L_CMP, s, b:b + 1],
                                 t["nsa_cmp_w"][s * L_CMP:(s + 1) * L_CMP].rearrange("(l a) -> l a", a=1)).then_inc(w_in, 16)
            with sp.Fori(0, ROUNDS) as i:
                for s in range(SETS):
                    sp.wait_ge(mm, i * 2 + s + 1)
                    for k in range(PER):
                        page = sp.value_load(pages[0:1, bass.DynSlice(i * (SETS * PER) + (s * PER + k), 1)],
                                             min_val=0, max_val=N_POOL - 1)
                        sp.dma_start(ring[:, s, k, :], t["cache_cmp"][bass.DynSlice(page, 1), :, :].rearrange("a p n -> (a p) n")
                                     ).then_inc(pages_in[s], 16)

        @block.tensor
        def _(pe):
            pe.sem_inc(mm, 2)
            pe.wait_ge(w_in, 16 * 2 * BPP)
            with pe.Fori(0, ROUNDS) as i:
                for s in range(SETS):
                    pe.wait_ge(pages_in[s], i * (16 * PER) + 16 * PER)
                    pe.wait_ge(out_k, i * 2 + s + 1)
                    for k in range(PER):
                        for kv in range(2):
                            last = nc.tensor.matmul(ps[:, s, kv * 32 + k * BPP:kv * 32 + (k + 1) * BPP],
                                                    ring[:, s, k, kv * P:(kv + 1) * P], wsel[:, kv, :], start=True, stop=True)
                    last.then_inc(mm, 1)

        @block.vector
        def _(dve):
            dve.sem_inc(out_k, 2)
            with dve.Fori(0, ROUNDS) as i:
                for s in range(SETS):
                    dve.wait_ge(mm, i * 2 + s + 3)
                    at = bass.DynSlice(i * 64 + s * 32, 32)
                    nc.vector.tensor_copy(kct[:, at], ps[:, s, 0:32])
                    nc.vector.tensor_copy(vct[:, at], ps[:, s, 32:64]).then_inc(out_k, 1)


def sparse_sample(nc, t, u, kv, pages, kct, vct, rb, ident, by_token, gate_rows, out):
    HB, SETS = NB // 2, 2
    NBLK = N_PAGES * PAGE // L_SEL + 1
    NCMP, NW, NX = PAST // L_CMP, WINDOW + TS, TS
    C_CMP, C_WIN, C_DIFF, C_FAR = 0, NCMP, NCMP + NW, NCMP + NW + PAGE + TS
    NBIAS = C_FAR + 1
    NT_ALL = N_PAGES + 4 + 1
    with ExitStack() as ctx:
        S = lambda nm, shape: sb(ctx, nc, "ss_" + nm, shape)
        hot, rbx, bias = S("hot", [N_BUCKETS + 1, TS, NBIAS]), S("rbx", [N_BUCKETS + 1, TS, P]), S("bias", [P, NBIAS])
        qs, kvs = S("q", [P, GQ, NB * TS]), S("kv_new", [P, 6, NB * TS])
        same, forced, lower = S("same", [P, P]), S("forced", [P, NBLK]), S("lower", [P, NBLK, NBLK])
        gates = S("gates", [P, 2, 3])
        qp = S("q_padded", [P, HB, P])
        kvn, vcth, vc, vn = S("kvn", [P, 6, HB * TS]), S("vcth", [P, HB * P]), S("vc", [P, HB, P]), S("vn", [TS, 2, HB, P])
        kwin, vwin = S("kwin", [P, HB, WINDOW]), S("vwin", [P, HB, 4, P])
        kring, vring = S("kring", [P, SETS, HB, 4 * PAGE]), S("vring", [P, SETS, 16, P])
        sc, sw, ss = S("s_cmp", [P, NCMP]), S("s_win", [P, NW]), S("s_slc", [P, NBLK * NBLK])
        gtm = ss[:, :].rearrange("p (a b) -> p a b", a=NBLK)
        score, cnt, addm = S("score", [P, NBLK]), S("cnt", [P, NBLK]), S("addm", [P, NBLK])
        mx, negm, sums, scale = S("max", [P, 3]), S("negm", [P, 3]), S("sums", [P, 3]), S("scale", [P, 3])
        pt, ptx = S("pt", [P, NT_ALL, P]), S("ptx", [TS, 2, P])
        eqm = pt[:, :, :].rearrange("p a b -> p (a b)")[:, 0:NBLK * NBLK].rearrange("p (a b) -> p a b", a=NBLK)
        ps = banks(ctx, nc, "ss_psum", 8)
        B_CMP, B_WIN, B_X, B_S, B_T, B_O = 0, 1, 2, 3, 5, 7
        sem = phase_semaphores(ctx, nc, "ss_")
        (consts_in, gates_out, gates_in, rbx_ready, bias_mm, bias_ready, win_in, staged, turn_mm, turned, q_ready,
         c_mm, c_negm, c_exp, pc_ready, imp_mm, w_mm, w_negm, w_exp, s_mm, s_ev, s_negm, s_exp, probs_ready,
         pt_mm, pt_out, b_done, o_out, chain) = (sem(s) for s in (
            "consts_in", "gates_out", "gates_in", "rbx_ready", "bias_mm", "bias_ready", "win_in", "staged", "turn_mm",
            "turned", "q_ready", "c_mm", "c_negm", "c_exp", "pc_ready", "imp_mm", "w_mm", "w_negm", "w_exp", "s_mm",
            "s_ev", "s_negm", "s_exp", "probs_ready", "pt_mm", "pt_out", "b_done", "o_out", "chain"))
        k_in = [sem("k_in0"), sem("k_in1")]
        v_in = [sem("v_in0"), sem("v_in1")]
        v_used = sem("v_used")
        block = ctx.enter_context(nc.Block())
        CHUNK = N_PAGES // 4
        NG = 11
        GROUPS = [[(sc, 0, NT_ALL - 1)], [(sw, j * P, N_PAGES + j) for j in range(4)]]
        GROUPS += [[(ss, (4 * c + j) * P, 4 * c + j) for j in range(4)] for c in range(8)]

        @block.sync
        def _(sp):
            def page(index, dst, src, landed):
                n = sp.value_load(pages[0:1, bass.DynSlice(index, 1)], min_val=0, max_val=N_POOL - 1)
                sp.dma_start(dst, src[bass.DynSlice(n, 1), :, :].rearrange("a p n -> (a p) n")).then_inc(landed, 16)

            for b in range(NB):
                sp.dma_start(gate_rows[b * 32:(b + 1) * 32, :].rearrange("(h t) x -> t x h", t=TS),
                             by_token[b * TS:(b + 1) * TS, NT, 8:32].rearrange("t (x h) -> t x h", x=3),
                             allow_slow_non_contiguous=True).then_inc(gates_out, 16)
            loads = [(hot[:, :, :], t["sample_onehot"]), (same[:, :], t["same_query"]),
                     (forced[:, :], t["forced"].partition_broadcast(P)),
                     (lower[:, :, :].rearrange("p a b -> p (a b)"), t["lower"].partition_broadcast(P)),
                     (qs[:, :, :], u[T_Q:T_Q + GQ, :, TP:W].rearrange("r p n -> p r n")),
                     (kvs[:, :, :], kv[:, :, TP:W].rearrange("k p n -> p k n"))]
            for dst, src in loads:
                sp.dma_start(dst, src).then_inc(consts_in, 16)
            sp.wait_ge(gates_out, 16 * NB)
            sp.dma_start(gates[:, :, :], gate_rows.rearrange("(a p) x -> p a x", p=P)).then_inc(gates_in, 16)
            with sp.Fori(0, 2) as hf:
                sp.wait_ge(b_done, hf * HB)
                sp.dma_start(kwin[:, :, :], t["cache_kwin"][bass.DynSlice(hf * HB, HB), :, :].rearrange("b p n -> p b n")
                             ).then_inc(win_in, 16)
                sp.dma_start(vwin[:, :, :, :].rearrange("p b j n -> p b (j n)"),
                             t["cache_vwin"][bass.DynSlice(hf * HB, HB), :, :].rearrange("b p n -> p b n")).then_inc(win_in, 16)
                with sp.Fori(0, CHUNK // 2) as i:
                    for s in range(SETS):
                        sp.wait_ge(s_mm, hf * CHUNK + i * 2 + (s + 1))
                        for b in range(HB):
                            for k in range(4):
                                page(hf * (HB * N_PAGES) + i * 8 + (b * N_PAGES + s * 4 + k),
                                     kring[:, s, b, k * PAGE:(k + 1) * PAGE], t["cache_kslc"], k_in[s])
                with sp.Fori(0, HB) as b:
                    for s in range(SETS):
                        sp.wait_ge(v_used, hf * (2 * HB) + b * 2 + (s + 1))
                        for k in range(16):
                            page(hf * (HB * N_PAGES) + b * N_PAGES + (s * 16 + k), vring[:, s, k, :], t["cache_vslc"], v_in[s])

        @block.tensor
        def _(pe):
            mm, tr = nc.tensor.matmul, nc.tensor.transpose
            pe.sem_inc(s_mm, 2)
            pe.sem_inc(v_used, 2)
            pe.wait_ge(rbx_ready, 1)
            for c0, c1, b in ((0, BANK, 0), (BANK, NBIAS, 1)):
                for tt in range(TS):
                    last = mm(ps[:, b, 0:c1 - c0], rbx[:, tt, :], hot[:, tt, c0:c1], start=tt == 0, stop=tt == TS - 1)
            last.then_inc(bias_mm, 1)
            pe.wait_ge(bias_ready, 1)
            with pe.Fori(0, 2) as hf:
                pe.wait_ge(staged, hf + 1)
                for b in range(HB):
                    tr(ps[:, B_T, b * P:(b + 1) * P], vcth[:, b * P:(b + 1) * P], ident[:, :])
                for b in range(HB):
                    tr(ps[0:TS, B_T + 1, b * P:(b + 1) * P], kvn[:, KV_VSLC, b * TS:(b + 1) * TS], ident[:, :])
                for b in range(HB):
                    last = tr(ps[0:TS, B_S, b * P:(b + 1) * P], kvn[:, KV_VWIN, b * TS:(b + 1) * TS], ident[:, :])
                last.then_inc(turn_mm, 1)
                pe.wait_ge(q_ready, hf + 1)
                for b in range(HB):
                    last = mm(ps[:, B_CMP, 0:NCMP], qp[:, b, :], kct[:, bass.DynSlice(hf * (HB * NCMP) + b * NCMP, NCMP)],
                              start=b == 0, stop=b == HB - 1)
                last.then_inc(c_mm, 1)
                pe.wait_ge(win_in, hf * 32 + 32)
                for b in range(HB):
                    mm(ps[:, B_WIN, :], qp[:, b, :], kwin[:, b, :], start=b == 0, stop=b == HB - 1)
                for j, kind in enumerate((KV_KWIN, KV_KSLC)):
                    for b in range(HB):
                        last = mm(ps[:, B_X, j * TS:(j + 1) * TS], qp[:, b, :], kvn[:, kind, b * TS:(b + 1) * TS],
                                  start=b == 0, stop=b == HB - 1)
                last.then_inc(w_mm, 1)
                pe.wait_ge(turned, hf + 1)
                pe.wait_ge(pc_ready, hf + 1)
                mm(ps[:, B_CMP, NCMP:2 * NCMP], same[:, :], sc[:, :], start=True, stop=True).then_inc(imp_mm, 1)
                with pe.Fori(0, CHUNK // 2) as i:
                    for s in range(SETS):
                        pe.wait_ge(k_in[s], hf * (256 * CHUNK // 2) + i * 256 + 256)
                        pe.wait_ge(s_ev, hf * CHUNK + i * 2 + (s + 1))
                        for b in range(HB):
                            last = mm(ps[:, B_S + s, :], qp[:, b, :], kring[:, s, b, :], start=b == 0, stop=b == HB - 1)
                        last.then_inc(s_mm, 1)
                for k, group in enumerate(GROUPS):
                    pe.wait_ge(probs_ready, hf * 3 + min(k + 1, 3))
                    pe.wait_ge(pt_out, hf * NG + max(k - 1, 0))
                    for j, (src, col, to) in enumerate(group):
                        last = tr(ps[:, B_T + k % 2, j * P:(j + 1) * P], src[:, col:col + P], ident[:, :])
                    last.then_inc(pt_mm, 1)
                pe.wait_ge(pt_out, hf * NG + NG - 2)
                tr(ps[0:TS, B_T, 0:P], sw[:, WINDOW:WINDOW + TS], ident[:, :])
                tr(ps[0:TS, B_T, P:2 * P], ss[:, PAST:PAST + TS], ident[:, :]).then_inc(pt_mm, 1)
                pe.wait_ge(pt_out, hf * NG + NG)
                for b in range(HB):
                    o = ps[:, B_O, b * 32:(b + 1) * 32]
                    cols = slice(b * 32, (b + 1) * 32)
                    mm(o, vc[:, b, :], pt[:, NT_ALL - 1, cols], start=True, stop=False)
                    for j in range(4):
                        mm(o, vwin[:, b, j, :], pt[:, N_PAGES + j, cols], start=False, stop=False)
                    mm(o, vn[:, 1, b, :], ptx[:, 0, cols], start=False, stop=False)
                    mm(o, vn[:, 0, b, :], ptx[:, 1, cols], start=False, stop=False)
                    for s in range(SETS):
                        pe.wait_ge(v_in[s], hf * (256 * HB) + 256 * (b + 1))
                        for k in range(16):
                            last = mm(o, vring[:, s, k, :], pt[:, s * 16 + k, cols], start=False, stop=s == 1 and k == 15)
                        last.then_inc(v_used, 1)
                pe.wait_ge(v_used, hf * (2 * HB) + 2 * HB + 2)
                pe.sem_inc(b_done, HB)

        @block.scalar
        def _(act):
            act.wait_ge(bias_mm, 1)
            act.activation(bias[:, :], ps[:, 0:2, :].rearrange("p a b -> p (a b)")[:, 0:NBIAS], ACT.Copy).then_inc(bias_ready, 1)
            act.wait_ge(consts_in, 16 * 6)
            with act.Fori(0, 2) as hf:
                act.activation(kvn[:, :, :], kvs[:, :, bass.DynSlice(hf * (HB * TS), HB * TS)], ACT.Copy)
                act.activation(vcth[:, :], vct[:, bass.DynSlice(hf * (HB * P), HB * P)], ACT.Copy).then_inc(staged, 1)
                act.wait_ge(turn_mm, hf + 1)
                act.activation(vc[:, :, :], ps[:, B_T, :].rearrange("p (b n) -> p b n", b=HB), ACT.Copy)
                act.activation(vn[:, 0, :, :], ps[0:TS, B_T + 1, :].rearrange("p (b n) -> p b n", b=HB), ACT.Copy)
                act.activation(vn[:, 1, :, :], ps[0:TS, B_S, :].rearrange("p (b n) -> p b n", b=HB), ACT.Copy).then_inc(turned, 1)
                for x, (ready, done, src) in enumerate(((c_negm, c_exp, sc[:, :]), (w_negm, w_exp, sw[:, :]), (s_negm, s_exp, ss[:, 0:PAST + TS]))):
                    act.wait_ge(ready, hf + 1)
                    act.activation(src, src, ACT.Exp, bias=negm[:, x:x + 1], accum_out=sums[:, x:x + 1]).then_inc(done, 1)
                for k, group in enumerate(GROUPS):
                    act.wait_ge(pt_mm, hf * NG + (k + 1))
                    n, to = len(group), group[0][2]
                    act.activation(pt[:, to:to + n, :].rearrange("p a b -> p (a b)"), ps[:, B_T + k % 2, 0:n * P], ACT.Copy).then_inc(pt_out, 1)
                act.wait_ge(pt_mm, hf * NG + NG)
                act.activation(ptx[:, :, :].rearrange("p a b -> p (a b)"), ps[0:TS, B_T, 0:2 * P], ACT.Copy).then_inc(pt_out, 1)
                act.wait_ge(b_done, hf * HB + HB)
                for g in range(2):
                    half = slice(g * DH, (g + 1) * DH)
                    dst = out[half, :, bass.DynSlice(hf * (HB * TS) + TP, HB * TS)].rearrange("p r (b t) -> p b r t", b=HB)
                    src = ps[half, B_O, 0:HB * 32].rearrange("p (b g r t) -> p b g r t", g=2, r=GQ, t=TS)[:, :, g]
                    for b in range(HB):
                        last = act.activation(dst[:, b], src[:, b], ACT.Copy)
                last.then_inc(o_out, 1)
                act.wait_ge(o_out, hf + 1)

        @block.vector
        def _(dve):
            V = nc.vector
            V.memset(rbx[:, :, :], 0.0).then_inc(chain, 1)
            V.memset(qp[:, :, :], 0.0).then_inc(chain, 1)
            dve.wait_ge(chain, 2)
            for tt in range(TS):
                last = V.tensor_copy(rbx[:, tt, :].rearrange("k (b h t) -> k b h t", b=HB, t=TS)[:, :, :, tt],
                                     rb[:, :].unsqueeze(1).to_broadcast([N_BUCKETS + 1, HB, NSA_HEADS]))
            dve.wait_ge(consts_in, 16 * 6)
            last = V.tensor_copy(score[:, :], forced[:, :]).then_inc(rbx_ready, 1)
            dve.wait_ge(gates_in, 16)
            dve.wait_ge(bias_ready, 1)
            dve.sem_inc(s_ev, 2)
            L = 20
            with dve.Fori(0, 2) as hf:
                n_link = [0]

                def link(ins):
                    n_link[0] += 1
                    ins.then_inc(chain, 1)
                    dve.wait_ge(chain, hf * L + (2 + n_link[0]))

                dve.wait_ge(b_done, hf * HB)
                for b in range(HB):
                    for g in range(2):
                        half = slice(g * DH, (g + 1) * DH)
                        last = V.tensor_copy(qp[half, b, b * 32 + g * 16:b * 32 + (g + 1) * 16].rearrange("p (r t) -> p r t", t=TS),
                                             qs[half, :, bass.DynSlice(hf * (HB * TS) + b * TS, TS)])
                last.then_inc(q_ready, 1)
                dve.wait_ge(c_mm, hf + 1)
                link(V.tensor_tensor(sc[:, :], ps[:, B_CMP, 0:NCMP], bias[:, C_CMP:C_CMP + NCMP], ALU.add))
                link(V.tensor_reduce(mx[:, 0:1], sc[:, :], AX_X, ALU.max))
                V.tensor_scalar(negm[:, 0:1], mx[:, 0:1], -1.0, None, ALU.mult).then_inc(c_negm, 1)
                dve.wait_ge(w_mm, hf + 1)
                V.tensor_tensor(sw[:, 0:WINDOW], ps[:, B_WIN, :], bias[:, C_WIN:C_WIN + WINDOW], ALU.add)
                link(V.tensor_tensor(sw[:, WINDOW:NW], ps[:, B_X, 0:TS], bias[:, C_WIN + WINDOW:C_WIN + NW], ALU.add))
                link(V.tensor_reduce(mx[:, 1:2], sw[:, :], AX_X, ALU.max))
                V.tensor_scalar(negm[:, 1:2], mx[:, 1:2], -1.0, None, ALU.mult).then_inc(w_negm, 1)
                dve.wait_ge(c_exp, hf + 1)
                link(V.reciprocal(scale[:, 0:1], sums[:, 0:1]))
                V.tensor_scalar(sc[:, :], sc[:, :], scale[:, 0:1], None, ALU.mult).then_inc(pc_ready, 1)
                dve.wait_ge(imp_mm, hf + 1)
                link(V.tensor_reduce(score[:, 0:NBLK - 1], ps[:, B_CMP, NCMP:2 * NCMP].rearrange("p (n a) -> p n a", a=2), AX_X, ALU.add))
                link(V.tensor_tensor(score[:, 0:NBLK - 1], score[:, 0:NBLK - 1], forced[:, 0:NBLK - 1], ALU.add))
                col = score[:, :].unsqueeze(2).to_broadcast([P, NBLK, NBLK])
                row = score[:, :].unsqueeze(1).to_broadcast([P, NBLK, NBLK])
                V.tensor_tensor(gtm, row, col, ALU.is_gt)
                link(V.tensor_tensor(eqm, row, col, ALU.is_equal))
                link(V.tensor_tensor(eqm, eqm, lower[:, :, :], ALU.mult))
                link(V.tensor_tensor(gtm, gtm, eqm, ALU.add))
                link(V.tensor_reduce(cnt[:, :], gtm, AX_X, ALU.add))
                link(V.tensor_scalar(addm[:, :], cnt[:, :], N_SEL - 0.5, NEG, ALU.is_ge, ALU.mult))
                link(V.tensor_scalar(addm[:, :], addm[:, :], bias[:, C_FAR:C_FAR + 1], None, ALU.add))
                V.tensor_scalar(sc[:, :], sc[:, :], gates[:, bass.DynSlice(hf, 1), 0:1].rearrange("p a b -> p (a b)"), None, ALU.mult).then_inc(probs_ready, 1)
                dve.wait_ge(w_exp, hf + 1)
                link(V.reciprocal(scale[:, 1:2], sums[:, 1:2]))
                link(V.tensor_tensor(scale[:, 1:2], scale[:, 1:2], gates[:, bass.DynSlice(hf, 1), 1 + 1:3].rearrange("p a b -> p (a b)"), ALU.mult))
                V.tensor_scalar(sw[:, :], sw[:, :], scale[:, 1:2], None, ALU.mult).then_inc(probs_ready, 1)
                with dve.Fori(0, CHUNK // 2) as i:
                    for s in range(SETS):
                        dve.wait_ge(s_mm, hf * CHUNK + i * 2 + (s + 3))
                        V.tensor_tensor(ss[:, bass.DynSlice(i * 1024 + s * BANK, BANK)].rearrange("p (n l) -> p n l", l=L_SEL),
                                        ps[:, B_S + s, :].rearrange("p (n l) -> p n l", l=L_SEL),
                                        addm[:, bass.DynSlice(i * 16 + s * 8, 8)].unsqueeze(2).to_broadcast([P, 8, L_SEL]),
                                        ALU.add).then_inc(s_ev, 1)
                dve.wait_ge(s_ev, hf * CHUNK + (CHUNK + 2))
                link(V.tensor_scalar(ss[:, PAST:PAST + TS], ps[:, B_X, TS:2 * TS], addm[:, NBLK - 1:NBLK], None, ALU.add))
                near = ss[:, PAST - PAGE:PAST + TS]
                link(V.tensor_tensor(near, near, bias[:, C_DIFF:C_FAR], ALU.add))
                link(V.tensor_reduce(mx[:, 2:3], ss[:, 0:PAST + TS], AX_X, ALU.max))
                V.tensor_scalar(negm[:, 2:3], mx[:, 2:3], -1.0, None, ALU.mult).then_inc(s_negm, 1)
                dve.wait_ge(s_exp, hf + 1)
                link(V.reciprocal(scale[:, 2:3], sums[:, 2:3]))
                link(V.tensor_tensor(scale[:, 2:3], scale[:, 2:3], gates[:, bass.DynSlice(hf, 1), 1:2].rearrange("p a b -> p (a b)"), ALU.mult))
                V.tensor_scalar(ss[:, 0:PAST + TS], ss[:, 0:PAST + TS], scale[:, 2:3], None, ALU.mult).then_inc(probs_ready, 1)
                assert n_link[0] == L, n_link[0]


def cross_prompt(nc, xq, mem, ident, out):
    KC = XD // P
    MC = N_MEM // P
    NI = NT
    with ExitStack() as ctx:
        S = lambda nm, shape: sb(ctx, nc, "xp_" + nm, shape)
        q, kt, vt = S("q", [P, 2, KC, TP]), S("kt", [P, 2, KC, N_MEM]), S("vt", [P, 2, KC, N_MEM])
        v = S("v", [P, 2, MC, XD])
        s_, pt = S("probs", [P, 2, N_MEM]), S("pt", [P, 2, MC, P])
        mx, negm, sums, scale = (S(n, [P, 2]) for n in ("max", "negm", "sums", "scale"))
        ps = banks(ctx, nc, "xp_psum", 8)
        B_S, B_T, B_O, B_V = 0, 2, 4, 6
        sem = phase_semaphores(ctx, nc, "xp_")
        loads = [sem("loads0"), sem("loads1")]
        v_mm, v_ready, scores_mm, negm_ready, exp_ready, chain, probs_ready, pt_mm, pt_out, o_mm, o_out = (sem(s) for s in (
            "v_mm", "v_ready", "scores_mm", "negm_ready", "exp_ready", "chain", "probs_ready", "pt_mm", "pt_out", "o_mm", "o_out"))
        block = ctx.enter_context(nc.Block())

        def head_loop(eng, body):
            with eng.Fori(0, XH // 2) as i:
                for s in range(2):
                    body(i * 2 + s, s, i)

        @block.sync
        def _(sp):
            def body(h, slot, i):
                sp.wait_ge(o_out, i * (NI * (1 + slot)))
                tiles = lambda src, at: src[bass.DynSlice(h * KC + at, KC), :, :].rearrange("c p n -> p c n")
                sp.dma_start(q[:, slot, :, :], tiles(xq, 0)[:, :, 0:TP]).then_inc(loads[slot], 16)
                sp.dma_start(kt[:, slot, :, :], tiles(mem, 0)).then_inc(loads[slot], 16)
                sp.dma_start(vt[:, slot, :, :], tiles(mem, CHUNKS)).then_inc(loads[slot], 16)
            head_loop(sp, body)

        @block.tensor
        def _(pe):
            mm = nc.tensor.matmul

            def scores(h, slot, i, t):
                if t == 0:
                    pe.wait_ge(loads[slot], i * 48 + 48)
                    for c in range(KC):
                        for m in range(MC):
                            last = nc.tensor.transpose(ps[:, B_V, m * XD + c * P:m * XD + (c + 1) * P],
                                                       vt[:, slot, c, m * P:(m + 1) * P], ident[:, :])
                    last.then_inc(v_mm, 1)
                pe.wait_ge(exp_ready, h * NI + max(t - 1, 0))
                for c in range(KC):
                    last = mm(ps[:, B_S + t % 2, 0:N_MEM], q[:, slot, c, t * P:(t + 1) * P], kt[:, slot, c, :],
                              start=c == 0, stop=c == KC - 1)
                last.then_inc(scores_mm, 1)

            def tail(h, slot, t):
                pe.wait_ge(probs_ready, h * NI + (t + 1))
                for m in range(MC):
                    last = nc.tensor.transpose(ps[:, B_T + t % 2, m * P:(m + 1) * P], s_[:, t % 2, m * P:(m + 1) * P], ident[:, :])
                last.then_inc(pt_mm, 1)
                pe.wait_ge(pt_out, h * NI + (t + 1))
                pe.wait_ge(o_out, h * NI + max(t - 1, 0))
                pe.wait_ge(v_ready, h + 1)
                for c in range(KC):
                    for m in range(MC):
                        last = mm(ps[:, B_O + t % 2, c * P:(c + 1) * P], v[:, slot, m, c * P:(c + 1) * P],
                                  pt[:, t % 2, m, :], start=m == 0, stop=m == MC - 1)
                last.then_inc(o_mm, 1)

            def body(h, slot, i):
                scores(h, slot, i, 0)
                for t in range(1, NI):
                    scores(h, slot, i, t)
                    tail(h, slot, t - 1)
                tail(h, slot, NI - 1)
            head_loop(pe, body)

        @block.vector
        def _(dve):
            V = nc.vector

            def maxima(h, t):
                p = t % 2
                dve.wait_ge(scores_mm, h * NI + (t + 1))
                V.tensor_reduce(mx[:, p:p + 1], ps[:, B_S + p, 0:N_MEM], AX_X, ALU.max).then_inc(chain, 1)
                dve.wait_ge(chain, h * (2 * NI) + (2 * t + 1) if t == 0 else h * (2 * NI) + 2 * t)
                V.tensor_scalar(negm[:, p:p + 1], mx[:, p:p + 1], -1.0, None, ALU.mult).then_inc(negm_ready, 1)

            def scales(h, t):
                p = t % 2
                dve.wait_ge(exp_ready, h * NI + (t + 1))
                V.reciprocal(scale[:, p:p + 1], sums[:, p:p + 1]).then_inc(chain, 1)
                dve.wait_ge(chain, h * (2 * NI) + (2 * t + 3 if t < NI - 1 else 2 * NI))
                V.tensor_scalar(s_[:, p, :], s_[:, p, :], scale[:, p:p + 1], None, ALU.mult).then_inc(probs_ready, 1)

            def body(h, slot, i):
                maxima(h, 0)
                for t in range(1, NI):
                    maxima(h, t)
                    scales(h, t - 1)
                scales(h, NI - 1)
            head_loop(dve, body)

        @block.scalar
        def _(act):
            def exps(h, t):
                p = t % 2
                act.wait_ge(negm_ready, h * NI + (t + 1))
                act.wait_ge(pt_mm, h * NI + max(t - 1, 0))
                act.activation(s_[:, p, :], ps[:, B_S + p, 0:N_MEM], ACT.Exp, bias=negm[:, p:p + 1],
                               accum_out=sums[:, p:p + 1]).then_inc(exp_ready, 1)

            def copies(h, t):
                act.wait_ge(pt_mm, h * NI + (t + 1))
                act.wait_ge(o_mm, h * NI + max(t - 1, 0))
                act.activation(pt[:, t % 2, :, :].rearrange("p a b -> p (a b)"), ps[:, B_T + t % 2, 0:MC * P], ACT.Copy).then_inc(pt_out, 1)
                act.wait_ge(o_mm, h * NI + (t + 1))
                act.activation(out[:, bass.DynSlice(h * KC, KC), t * P:(t + 1) * P],
                               ps[:, B_O + t % 2, 0:KC * P].rearrange("p (c n) -> p c n", c=KC), ACT.Copy).then_inc(o_out, 1)

            def body(h, slot, i):
                exps(h, 0)
                act.wait_ge(v_mm, h + 1)
                act.activation(v[:, slot, :, :].rearrange("p a b -> p (a b)"), ps[:, B_V, :], ACT.Copy).then_inc(v_ready, 1)
                for t in range(1, NI):
                    exps(h, t)
                    copies(h, t - 1)
                copies(h, NI - 1)
            head_loop(act, body)


def cross_sample(nc, t, xq, ident, out):
    R = XH * TS
    MC = N_MEM // P
    with ExitStack() as ctx:
        S = lambda nm, shape: sb(ctx, nc, "xs_" + nm, shape)
        qs, qb = S("q", [P, CHUNKS, NB * TS]), S("qb", [P, 2, CHUNKS, R])
        kt, v = S("kt", [P, 2, CHUNKS, N_MEM]), S("v", [P, 2, MC, D])
        s_, pt = S("probs", [P, 2, N_MEM]), S("pt", [P, 2, MC, R])
        mx, negm, sums, scale = (S(n, [R, 2]) for n in ("max", "negm", "sums", "scale"))
        ps = banks(ctx, nc, "xs_psum", 6)
        B_S, B_T, B_O = 0, 2, 4
        sem = phase_semaphores(ctx, nc, "xs_")
        loads, q_in = [sem("loads0"), sem("loads1")], sem("q_in")
        qb_ready, scores_mm, negm_ready, exp_ready, chain, probs_ready, pt_mm, pt_out, o_mm, o_out, zeroed = (sem(s) for s in (
            "qb_ready", "scores_mm", "negm_ready", "exp_ready", "chain", "probs_ready", "pt_mm", "pt_out", "o_mm", "o_out", "zeroed"))
        block = ctx.enter_context(nc.Block())

        def batch_loop(eng, body):
            with eng.Fori(0, NB // 2) as i:
                for s in range(2):
                    body(i * 2 + s, s, i)

        @block.sync
        def _(sp):
            sp.dma_start(qs[:, :, :], xq[:, :, TP:W].rearrange("c p n -> p c n")).then_inc(q_in, 16)

            def body(b, s, i):
                sp.wait_ge(o_mm, b + 1)
                sp.dma_start(kt[:, s, :, :], t["cache_mem_k"][bass.DynSlice(b, 1)].rearrange("a p n -> (a p) n").rearrange("p (c n) -> p c n", c=CHUNKS)).then_inc(loads[s], 16)
                sp.dma_start(v[:, s, :, :], t["cache_mem_v"][bass.DynSlice(b, 1)].rearrange("a p n -> (a p) n").rearrange("p (c n) -> p c n", c=MC)).then_inc(loads[s], 16)
            batch_loop(sp, body)

        @block.tensor
        def _(pe):
            mm = nc.tensor.matmul
            pe.sem_inc(o_mm, 2)

            def body(b, s, i):
                pe.wait_ge(loads[s], i * 32 + 32)
                pe.wait_ge(qb_ready, b + 1)
                for c in range(CHUNKS):
                    last = mm(ps[0:R, B_S + s, 0:N_MEM], qb[:, s, c, :], kt[:, s, c, :], start=c == 0, stop=c == CHUNKS - 1)
                last.then_inc(scores_mm, 1)
                pe.wait_ge(probs_ready, b + 1)
                for m in range(MC):
                    last = nc.tensor.transpose(ps[:, B_T + s, m * P:(m + 1) * P], s_[:, s, m * P:(m + 1) * P], ident[:, :])
                last.then_inc(pt_mm, 1)
                pe.wait_ge(pt_out, b + 1)
                pe.wait_ge(o_out, b)
                for c in range(CHUNKS):
                    h = c // (CHUNKS // XH)
                    for m in range(MC):
                        last = mm(ps[:, B_O + s, c * TS:(c + 1) * TS], v[:, s, m, c * P:(c + 1) * P],
                                  pt[:, s, m, h * TS:(h + 1) * TS], start=m == 0, stop=m == MC - 1)
                last.then_inc(o_mm, 1)
            batch_loop(pe, body)

        @block.vector
        def _(dve):
            V = nc.vector
            V.memset(qb[:, :, :, :], 0.0).then_inc(zeroed, 1)
            V.memset(s_[:, :, :], 0.0).then_inc(zeroed, 1)
            dve.wait_ge(zeroed, 2)
            dve.wait_ge(q_in, 16)

            def body(b, s, i):
                dve.wait_ge(o_mm, b + 2)
                for h in range(XH):
                    last = V.tensor_copy(qb[:, s, 2 * h:2 * h + 2, h * TS:(h + 1) * TS],
                                         qs[:, 2 * h:2 * h + 2, bass.DynSlice(b * TS, TS)])
                last.then_inc(qb_ready, 1)
                dve.wait_ge(scores_mm, b + 1)
                V.tensor_reduce(mx[:, s:s + 1], ps[0:R, B_S + s, 0:N_MEM], AX_X, ALU.max).then_inc(chain, 1)
                dve.wait_ge(chain, b * 2 + 1)
                V.tensor_scalar(negm[:, s:s + 1], mx[:, s:s + 1], -1.0, None, ALU.mult).then_inc(negm_ready, 1)
                dve.wait_ge(exp_ready, b + 1)
                V.reciprocal(scale[:, s:s + 1], sums[:, s:s + 1]).then_inc(chain, 1)
                dve.wait_ge(chain, b * 2 + 2)
                V.tensor_scalar(s_[0:R, s, :], s_[0:R, s, :], scale[:, s:s + 1], None, ALU.mult).then_inc(probs_ready, 1)
            batch_loop(dve, body)

        @block.scalar
        def _(act):
            def body(b, s, i):
                act.wait_ge(negm_ready, b + 1)
                act.activation(s_[0:R, s, :], ps[0:R, B_S + s, 0:N_MEM], ACT.Exp, bias=negm[:, s:s + 1],
                               accum_out=sums[:, s:s + 1]).then_inc(exp_ready, 1)
                act.wait_ge(pt_mm, b + 1)
                act.activation(pt[:, s, :, :], ps[:, B_T + s, 0:MC * P].rearrange("p (m c) -> p m c", m=MC)[:, :, 0:R], ACT.Copy).then_inc(pt_out, 1)
                act.wait_ge(o_mm, b + 3)
                act.activation(out[:, :, bass.DynSlice(b * TS + TP, TS)],
                               ps[:, B_O + s, 0:CHUNKS * TS].rearrange("p (c n) -> p c n", c=CHUNKS), ACT.Copy).then_inc(o_out, 1)
            batch_loop(act, body)


def window_cache(nc, t, kv, ident, new_win):
    N = NB * TS
    with ExitStack() as ctx:
        new_t = sb(ctx, nc, "win_new_t", [P, 2, N])
        new = sb(ctx, nc, "win_new", [N, 2, P])
        ps = banks(ctx, nc, "win_psum", 1)
        sem = phase_semaphores(ctx, nc, "win_")
        landed, turned, copied, sent = (sem(s) for s in ("landed", "turned", "copied", "sent"))
        block = ctx.enter_context(nc.Block())

        @block.sync
        def _(sp):
            sp.dma_start(new_t[:, :, :], kv[KV_KWIN:KV_VWIN + 1, :, TP:W].rearrange("k p n -> p k n")).then_inc(landed, 16)
            sp.dma_start(new_win[:, 0:WINDOW - TS, :], t["cache_win"][:, TS:WINDOW, :]).then_inc(sent, 16)
            sp.wait_ge(copied, 1)
            for b in range(NB):
                sp.dma_start(new_win[b, WINDOW - TS:WINDOW, :], new[b * TS:(b + 1) * TS, :, :].rearrange("t k c -> t (k c)")
                             ).then_inc(sent, 16)
            sp.wait_ge(sent, 16 * (NB + 1))

        @block.tensor
        def _(pe):
            pe.wait_ge(landed, 16)
            for k in range(2):
                last = nc.tensor.transpose(ps[0:N, 0, k * P:(k + 1) * P], new_t[:, k, :], ident[:, :])
            last.then_inc(turned, 1)

        @block.vector
        def _(dve):
            dve.wait_ge(turned, 1)
            nc.vector.tensor_copy(new[:, :, :].rearrange("t k c -> t (k c)"), ps[0:N, 0, 0:2 * P]).then_inc(copied, 1)


def decoder_layer(nc, t, o):
    dram = lambda name, shape: nc.dram_tensor(name, shape, F32, kind=SCRATCH).ap()
    u = dram("u_scratch", [N_LINEAR + N_GATE, P, W])
    xq = dram("xq_scratch", [CHUNKS, P, W])
    toeplitz = dram("toeplitz", [NSA_HEADS, P, TP + 640])
    kv = o["kv"]
    with ExitStack() as top:
        ones = sb(top, nc, "ones", [P, P])
        ident = sb(top, nc, "ident", [P, P])
        gains = sb(top, nc, "gains", [P, 4, CHUNKS])
        rb = sb(top, nc, "rel_bias", [N_BUCKETS + 1, NSA_HEADS])
        norm_g = sb(top, nc, "norm_g", [P, 1])
        load_all(nc, "constants", [(ones[:, :], t["ones"]), (ident[:, :], t["ident"]), (gains[:, :, :], t["gains"]),
                                   (rb[:, :], t["rel_bias"]), (norm_g[:, :], t["gdn_norm_g"])])

        with ExitStack() as ctx:
            h = sb(ctx, nc, "h", [P, CHUNKS, W])
            with ExitStack() as c2:
                x = sb(c2, nc, "x_in", [P, CHUNKS, W])
                sq = sb(c2, nc, "sq", [P, 2, W])
                load_all(nc, "load_x", [(x[:, c, :], t["x"][c]) for c in range(CHUNKS)])
                rmsnorm(nc, "norm_mix", x, gains[:, 0, :], ones, h, sq)
            kept = dict(func=ACT.Copy, rhs=h, dram=u)
            gemm(nc, "w_in", t["w_in"], [
                (0, T_Q, kept),
                (T_Q, 4, dict(kept, at=T_Q, scale=DH ** -0.5)),
                (T_KV, 6, dict(kept, dram=kv)),
                (T_MISC, 1, dict(kept, at=T_MISC)),
                (T_GATE, N_GATE, dict(kept, at=T_GATE, func=ACT.Sigmoid))], CHUNKS, W, finish_copy)

        window_cache(nc, t, kv, ident, o["win_s"])
        with ExitStack() as mixers:
            branches = sb(mixers, nc, "branches", [P, 3, 4, W])
            by_token = sb(mixers, nc, "by_token", [P, NT + 1, 36])
            conv_module(nc, u, t, ones, branches[:, 0], (o["conv_a_p"], o["conv_a_s"]))
            with ExitStack() as ctx:
                qkv = sb(ctx, nc, "qkv", [P, 12, W])
                go = sb(ctx, nc, "gdn_o", [P, GH, W])
                gdn_inputs(nc, u, t, ones, ident, qkv, by_token, (o["conv_qkv_p"], o["conv_qkv_s"]))
                delta_rule(nc, "gdnp", qkv, by_token, ones, ident,
                           dict(tri=t["tri_p"], bound=t["bound_p"], levels=t["levels_p"]), t, P, 7, NT, 0, go, o["gdn_p"])
                delta_rule(nc, "gdns", qkv, by_token, ones, ident,
                           dict(tri=t["tri_s"], bound=t["bound_s"], levels=t["levels_s"],
                                batch_cols=t["batch_cols"], batch_rows=t["batch_rows"]),
                           t, NB * TS, 2, 1, TP, go, o["gdn_s"], batches=NB)
                gate_output(nc, go, u, ones, norm_g[:, 0:1], branches[:, 1])
            bias_rows(nc, t, dram("bias_rows", [NSA_HEADS, LB_FULL + LB_WIN]), toeplitz, rb)
            sparse_prompt(nc, t, u, kv, toeplitz, ident, by_token, branches[:, 2])
            with ExitStack() as ctx:
                pages = sb(ctx, nc, "pages", [1, NB * N_PAGES], I32)
                kct, vct = (sb(ctx, nc, n, [P, NB * PAST // L_CMP]) for n in ("kct", "vct"))
                load_all(nc, "load_pages", [(pages[:, :], t["page_table"])])
                compress_cache(nc, t, pages, kct, vct)
                sparse_sample(nc, t, u, kv, pages, kct, vct, rb, ident, by_token, dram("gate_rows", [NB * 32, 3]), branches[:, 2])

            x = sb(top, nc, "x", [P, CHUNKS, W], side="right")
            with ExitStack() as ctx:
                mix = sb(ctx, nc, "mix", [P, CHUNKS, W])
                gemm(nc, "w_branch", t["w_branch"], [
                    (8 * i, 8, dict(rhs=branches[:, i], out=mix, first=i == 0, aux=u, aux_at=T_GATE + 8 * i)) for i in range(3)],
                    4, W, finish_gated, on_vector=True)
                load_all(nc, "reload_x", [(x[:, c, :], t["x"][c]) for c in range(CHUNKS)])
                gemm(nc, "w_o", t["w_o"], [(0, CHUNKS, dict(rhs=mix, out=x))], CHUNKS, W, finish_residual, on_vector=True)

        with ExitStack() as ctx:
            h = sb(ctx, nc, "h_x", [P, CHUNKS, W])
            sq = sb(ctx, nc, "sq_x", [P, 2, W])
            mem = sb(ctx, nc, "mem", [P, CHUNKS, N_MEM])
            rmsnorm(nc, "norm_x", x, gains[:, 1, :], ones, h, sq)
            load_all(nc, "load_mem", [(mem[:, c, :], t["mem"][c]) for c in range(CHUNKS)])
            gemm(nc, "w_mem", t["w_mem"], [(0, 16, dict(func=ACT.Copy, rhs=mem, dram=o["mem"]))], CHUNKS, N_MEM, finish_copy)
            gemm(nc, "w_xq", t["w_xq"], [(0, CHUNKS, dict(func=ACT.Copy, rhs=h, dram=xq, scale=XD ** -0.5))],
                 CHUNKS, W, finish_copy)
        with ExitStack() as ctx:
            xo = sb(ctx, nc, "x_attended", [P, CHUNKS, W])
            cross_prompt(nc, xq, o["mem"], ident, xo)
            cross_sample(nc, t, xq, ident, xo)
            gemm(nc, "w_xo", t["w_xo"], [(0, CHUNKS, dict(rhs=xo, out=x))], CHUNKS, W, finish_residual, on_vector=True)

        with ExitStack() as ctx:
            h = sb(ctx, nc, "h_mlp", [P, CHUNKS, W])
            with ExitStack() as c2:
                rmsnorm(nc, "norm_mlp", x, gains[:, 2, :], ones, h, sb(c2, nc, "sq_mlp", [P, 2, W]))
            with ExitStack() as c2:
                hidden = sb(c2, nc, "hidden", [P, D_FF // P // 2, W])
                for half in range(2):
                    gemm(nc, f"w_ff1_{half}", t["w_ff1"], [(16 * half, 16, dict(rhs=h, out=hidden))], CHUNKS, W, finish_square)
                    gemm(nc, f"w_ff2_{half}", t["w_ff2"], [(8 * half, 8, dict(rhs=hidden, out=x))], 16, W,
                         finish_residual, on_vector=True)
            rmsnorm(nc, "norm_final", x, gains[:, 3, :], ones, h, sb(ctx, nc, "sq_final", [P, 2, W]))
            load_all(nc, "store_y", [(o["y"][c], h[:, c, :]) for c in range(CHUNKS)])


SCRATCH = "Internal"
OUTPUTS = {
    "y": [CHUNKS, P, W], "kv": [6, P, W],
    "gdn_p": [P, GH, P], "gdn_s": [P, NB, GH, P],
    "win_s": [NB, WINDOW, 2 * P],
    "mem": [16, P, N_MEM],
    "conv_a_p": [4, P, CONV_W - 1], "conv_a_s": [4, P, NB, CONV_W - 1],
    "conv_qkv_p": [12, P, GDN_CONV_W - 1], "conv_qkv_s": [12, P, NB, GDN_CONV_W - 1],
}


def weight_tiles(w):
    k, m = w.shape
    return np.ascontiguousarray(w.reshape(k // P, P, m // P, P).transpose(2, 1, 0, 3)).reshape(m // P, P, k)


def block_masks(n, block, levels):
    j, i = np.mgrid[0:n, 0:n]
    valid = (j <= i) & (j // block == i // block)
    parts = [(i // (2 << l) == j // (2 << l)) & (i >> l != j >> l) & (i > j) for l in range(levels)]
    return (valid.astype(np.float32), np.where(valid, 0.0, NEG).astype(np.float32),
            np.ascontiguousarray(np.stack(parts, 1)).astype(np.float32))


def per_channel(v):
    v = v.reshape(v.shape[:-1] + (v.shape[-1] // P, P))
    return np.ascontiguousarray(np.moveaxis(v, -1, 0))


def channel_major(x_prompt, x_sample):
    tokens = np.concatenate([x_prompt.reshape(TP, -1), x_sample.reshape(NB * TS, -1)], 0)
    return np.ascontiguousarray(tokens.T).reshape(-1, P, W)


def kernel(**inputs):
    import concourse.bacc as bacc
    from concourse.bass_utils import run_bass_kernel_spmd

    a = {k: np.asarray(v) for k, v in inputs.items()}
    arrays = {}
    arrays["x"] = channel_major(a["x_prompt"], a["x_sample"])
    arrays["ones"] = np.ones((P, P), np.float32)
    arrays["ident"] = np.eye(P, dtype=np.float32)
    arrays["gains"] = per_channel(np.stack([a["norm_mix"][0], a["norm_x"][0], a["norm_mlp"][0], a["norm_final"]]))
    w = a["w_in"][0]
    conv, qkvz, ab = w[:, :1024], w[:, 1024:3072], w[:, 3072:3080]
    q = w[:, 3080:3592].reshape(D, NSA_KV, GQ, DH).transpose(0, 2, 1, 3).reshape(D, 512)
    kv, gl, gates = w[:, 3592:4360], w[:, 4360:4384], w[:, 4384:]
    arrays["w_in"] = weight_tiles(np.concatenate([conv, qkvz, q, kv, ab, gl, np.zeros((D, 96), np.float32), gates], 1))
    arrays["conv_a_w"] = per_channel(a["conv_a_w"][0])
    arrays["conv_a_vecs"] = per_channel(np.stack([a["conv_a_b"][0], a["ln_a_g"][0], a["ln_a_b"][0]]))
    arrays["state_conv_a"] = np.ascontiguousarray(
        a["state_conv_a"][0].reshape(NB, CONV_W - 1, 4, P).transpose(2, 3, 0, 1))
    arrays["gdn_conv_w"] = per_channel(a["gdn_conv_w"][0])
    arrays["state_conv_qkv"] = np.ascontiguousarray(
        a["state_conv_qkv"][0].reshape(NB, GDN_CONV_W - 1, 12, P).transpose(2, 3, 0, 1))
    arrays["decay_vecs"] = np.stack([a["gdn_a_log"][0], a["gdn_dt_bias"][0]], 1)
    arrays["gdn_norm_g"] = a["gdn_norm_g"][0].reshape(P, 1)
    arrays["tri_p"], arrays["bound_p"], arrays["levels_p"] = block_masks(P, P, 7)
    arrays["tri_s"], arrays["bound_s"], arrays["levels_s"] = block_masks(NB * TS, TS, 2)
    own = (np.arange(NB)[:, None] == np.arange(NB * TS)[None, :] // TS).astype(np.float32)
    arrays["batch_cols"] = np.broadcast_to(own, (P, NB, NB * TS)).copy()
    arrays["batch_rows"] = own.T.copy()
    arrays["state_gdn"] = np.ascontiguousarray(a["state_gdn"][0].transpose(2, 0, 1, 3))
    arrays["nsa_cmp_w"] = a["nsa_cmp_w"][0].reshape(-1)
    arrays["rel_bias"] = np.concatenate([a["rel_bias"], np.full((1, NSA_HEADS), NEG, np.float32)], 0)
    far = 639 - np.arange(LB_WIN)
    arrays["prompt_onehot"] = np.concatenate([bucket_onehot(1023 - np.arange(LB_FULL)),
                                              bucket_onehot(np.where(far < WINDOW, far, -1))], 1)
    arrays["page_table"] = a["page_table"].reshape(1, -1)
    cache = a["cache_nsa_kv"][0].reshape(N_POOL, PAGE, 4, P)
    arrays["cache_cmp"] = np.ascontiguousarray(cache[:, :, 0:2]).reshape(N_POOL, PAGE, 2 * P)
    arrays["cache_kslc"] = np.ascontiguousarray(cache[:, :, 2].transpose(0, 2, 1))
    arrays["cache_vslc"] = np.ascontiguousarray(cache[:, :, 3])
    win = a["cache_win_kv"][0].reshape(NB, WINDOW, 2, P)
    arrays["cache_win"] = win.reshape(NB, WINDOW, 2 * P)
    arrays["cache_kwin"] = np.ascontiguousarray(win[:, :, 0].transpose(0, 2, 1))
    arrays["cache_vwin"] = np.ascontiguousarray(win[:, :, 1].reshape(NB, 4, P, P).transpose(0, 2, 1, 3)).reshape(NB, P, 4 * P)
    hots = []
    for s in range(TS):
        i = np.arange(WINDOW + TS)
        w = WINDOW + s - i
        near = PAGE + s - np.arange(PAGE + TS)
        last = bucket_onehot(np.array([MAX_DIST]))
        hots.append(np.concatenate([bucket_onehot(PAST + s - (np.arange(PAST // L_CMP) * L_CMP + L_CMP - 1)),
                                    bucket_onehot(np.where(w < WINDOW, w, -1)), bucket_onehot(near) - last, last], 1))
    arrays["sample_onehot"] = np.ascontiguousarray(np.stack(hots, 1))
    row = np.arange(P)
    query = row // 16 * TS + row % TS
    arrays["same_query"] = (query[:, None] == query[None, :]).astype(np.float32)
    blocks = np.arange(PAST // L_SEL + 1)
    cur = PAST // L_SEL
    arrays["forced"] = np.where((blocks == 0) | (blocks == cur) | (blocks == cur - 1), FORCE_BONUS, 0.0).astype(np.float32)
    arrays["lower"] = (blocks[None, :] < blocks[:, None]).astype(np.float32).reshape(-1)
    w_pc = a["w_pc"][0].reshape(NSA_KV, GQ, DH, D).transpose(1, 0, 2, 3).reshape(-1, D)
    arrays["w_branch"] = np.concatenate([weight_tiles(x) for x in (a["w_pa"][0], a["w_pb"][0], w_pc)], 0)
    for name in ("w_o", "w_xq", "w_xo", "w_ff1"):
        arrays[name] = weight_tiles(a[name][0])
    arrays["w_mem"] = weight_tiles(np.concatenate([a["w_xk"][0], a["w_xv"][0]], 1))
    arrays["w_ff2"] = np.concatenate([weight_tiles(a["w_ff2"][0][i:i + D_FF // 2]) for i in (0, D_FF // 2)], 0)
    arrays["mem"] = np.ascontiguousarray(a["mem_prompt"][0].T).reshape(CHUNKS, P, N_MEM)
    mkv = a["cache_mem_kv"][0].reshape(NB, N_MEM, 2, D)
    arrays["cache_mem_k"] = np.ascontiguousarray(mkv[:, :, 0].transpose(0, 2, 1).reshape(NB, CHUNKS, P, N_MEM)
                                                 .transpose(0, 2, 1, 3)).reshape(NB, P, CHUNKS * N_MEM)
    arrays["cache_mem_v"] = np.ascontiguousarray(mkv[:, :, 1].reshape(NB, 2, P, D).transpose(0, 2, 1, 3)).reshape(NB, P, 2 * D)
    nc = bacc.Bacc("TRN2", target_bir_lowering=False, num_devices=1)
    t = {k: nc.dram_tensor("in_" + k, v.shape, mybir.dt.from_np(v.dtype), kind="ExternalInput").ap()
         for k, v in arrays.items()}
    o = {k: nc.dram_tensor("out_" + k, s, F32, kind="ExternalOutput").ap() for k, s in OUTPUTS.items()}
    decoder_layer(nc, t, o)
    r = run_bass_kernel_spmd(nc, [{"in_" + k: v for k, v in arrays.items()}], core_ids=[0]).results[0]
    g = {k: r["out_" + k] for k in OUTPUTS}
    y, kv = (g[k].reshape(-1, W) for k in ("y", "kv"))
    y, kv = y.T, kv.T.reshape(W, 6, NSA_KV, DH)
    new = kv[TP:].reshape(NB, TS, 6, NSA_KV, DH)
    lay = lambda x, axes, shape: np.ascontiguousarray(x.transpose(axes).reshape(shape))
    return (
        np.ascontiguousarray(y[:TP]).reshape(1, TP, D),
        np.ascontiguousarray(y[TP:]).reshape(NB, TS, D),
        np.ascontiguousarray(kv[None, None, :TP, 0:4]),
        np.ascontiguousarray(kv[None, None, TP - WINDOW:TP, 4:6]),
        lay(g["conv_a_p"], (2, 0, 1), (1, 1, CONV_W - 1, CONV_CH)),
        lay(g["conv_qkv_p"], (2, 0, 1), (1, 1, GDN_CONV_W - 1, 12 * P)),
        lay(g["gdn_p"], (1, 0, 2), (1, 1, GH, P, P)),
        lay(g["mem"], (2, 0, 1), (1, 1, N_MEM, 2, XH, XD)),
        np.ascontiguousarray(new[None, :, :, 0:4]),
        g["win_s"].reshape(1, NB, WINDOW, 2, NSA_KV, DH),
        lay(g["conv_a_s"], (2, 3, 0, 1), (1, NB, CONV_W - 1, CONV_CH)),
        lay(g["conv_qkv_s"], (2, 3, 0, 1), (1, NB, GDN_CONV_W - 1, 12 * P)),
        lay(g["gdn_s"], (1, 2, 0, 3), (1, NB, GH, P, P)),
    )
```

```python
from contextlib import ExitStack
import math

import numpy as np
import concourse.bass as bass
from concourse import mybir

ALU = mybir.AluOpType
ACT = mybir.ActivationFunctionType
AX_X = mybir.AxisListType.X
F32 = mybir.dt.float32
F32R = mybir.dt.float32r
I32 = mybir.dt.int32

P = 128
D = 1024
TP = 1024
NB, TS = 8, 4
W = TP + NB * TS
NT = TP // P
CHUNKS = D // P
SPLIT = 3
WN = W // SPLIT
BANK = 512
EPS = 1e-6

CONV_CH, CONV_W = 512, 31
GH, GDN_CONV_W = 4, 4
NSA_HEADS, NSA_KV, GQ, DH = 8, 2, 4, 64
L_CMP, L_SEL, N_SEL, WINDOW = 32, 64, 16, 512
FORCE_BONUS = 1e4
N_BUCKETS, MAX_DIST = 32, 128
PAST, PAGE = 4096, 128
N_PAGES = PAST // PAGE
N_POOL = NB * N_PAGES + NB * N_PAGES // 4
N_MEM, XH, XD = 256, 4, 256
D_FF = 4096
NEG = -1e30

T_A, T_AG, T_QKV, T_Z, T_Q, T_KV, T_MISC, T_GATE = 0, 4, 8, 20, 24, 28, 34, 35
N_LINEAR, N_GATE = 35, 24
KV_KCMP, KV_VCMP, KV_KSLC, KV_VSLC, KV_KWIN, KV_VWIN = range(6)


def bucket_onehot(rel):
    n = np.maximum(rel, 0)
    exact = N_BUCKETS // 2
    large = exact + (np.log(np.maximum(n, 1).astype(np.float32) / exact) / math.log(MAX_DIST / exact)
                     * (N_BUCKETS - exact)).astype(np.int32)
    b = np.where(n < exact, n, np.minimum(large, N_BUCKETS - 1))
    out = np.zeros((N_BUCKETS + 1, rel.size), np.float32)
    out[np.where(rel >= 0, b, N_BUCKETS), np.arange(rel.size)] = 1.0
    return out


def sb(ctx, nc, name, shape, dt=F32, **kw):
    return ctx.enter_context(nc.sbuf_tensor(name, shape, dt, **kw))


def banks(ctx, nc, name, n):
    return ctx.enter_context(nc.psum_tensor(name, [P, n, BANK], F32))


def phase_semaphores(ctx, nc, prefix):
    taken = []

    def clear():
        nc.clear_and_free_semaphores(taken)
        nc.all_engine_barrier()

    ctx.callback(clear)

    def sem(name):
        taken.append(nc.alloc_semaphore(name=prefix + name))
        return taken[-1]

    return sem


class Chain:

    def __init__(self, eng, sem, base=0):
        self.eng, self.sem, self.base, self.n = eng, sem, base, 0

    def __call__(self, ins):
        self.n += 1
        ins.then_inc(self.sem, 1)
        self.eng.wait_ge(self.sem, self.base + self.n)
        return ins


def gemm(nc, name, weights, parts, k, n_cols, finish, on_vector=False, beside=None):
    split = SPLIT if n_cols == W else 1
    wn = n_cols // split
    total = sum(n for _, n, _ in parts)
    stores, has_aux = "dram" in parts[0][2], "aux" in parts[0][2]
    with ExitStack() as ctx:
        ring = sb(ctx, nc, name + "_ring", [P, 2, k * P])
        high = sb(ctx, nc, name + "_high", [P, 2, k * P], F32R)
        low = sb(ctx, nc, name + "_low", [P, 2, k * P], F32R)
        stage = sb(ctx, nc, name + "_stage", [P, 2, n_cols])
        aux = sb(ctx, nc, name + "_aux", [P, 2, n_cols]) if has_aux else None
        psum = banks(ctx, nc, name + "_psum", 2 * split).ap().rearrange("p (s n) c -> p s n c", s=2)
        sem = phase_semaphores(ctx, nc, name)
        w_in = [sem("_w_in0"), sem("_w_in1")]
        aux_in = [sem("_aux_in0"), sem("_aux_in1")]
        w_split = sem("_w_split")
        mm_done = sem("_mm_done")
        finished = sem("_finished")
        stored = [sem("_stored0"), sem("_stored1")]
        idle = sb(ctx, nc, name + "_idle", [1, 2])
        idle_ready = sem("_idle_ready")
        rounded = sem("_rounded")
        chain = (sem("_chain0"), sem("_chain1"))
        block = ctx.enter_context(nc.Block())
        thirds = lambda ap: ap.rearrange("p (n c) -> p n c", n=split)

        def steps(eng, body, settle=None):
            done = 0
            for first, n, args in parts:
                if settle and "settled" in args:
                    settle(done)
                if n >= 2:
                    with eng.Fori(0, n // 2) as i:
                        for s in range(2):
                            body(i * 2 + (done + s), (done + s) % 2, i * 2 + (first + s), args, i * 2 + s)
                if n % 2:
                    body(done + n - 1, (done + n - 1) % 2, first + n - 1, args, n - 1)
                done += n

        def slot_uses(step, slot):
            return step // 2 if isinstance(step, int) else (step - slot) // 2

        @block.sync
        def _(sp):
            if beside:
                beside["sync_first"](sp)

            def load(step, slot, tile, args, j):
                sp.wait_ge(w_split, step + 1)
                sp.dma_start(ring[:, slot, :], weights[bass.DynSlice(tile, 1), :, :].rearrange("a p n -> (a p) n")
                             ).then_inc(w_in[slot], 16)
                if has_aux:
                    sp.wait_ge(finished, step + 1)
                    sp.dma_start(aux[:, slot, :], args["aux"][bass.DynSlice(j + args["aux_at"], 1), :, :].rearrange("a p n -> (a p) n")
                                 ).then_inc(aux_in[slot], 16)
            steps(sp, load)
            if beside:
                beside["sync_last"](sp)

        @block.gpsimd
        def _(pool):
            pool.sem_inc(w_split, 2)
            if beside:
                nc.gpsimd.memset(idle[:, :], 0.0).then_inc(idle_ready, 1)
                pool.wait_ge(idle_ready, 1)

            def split_weights(step, slot, tile, args, j):
                if beside:
                    pool.wait_ge(w_in[slot], slot_uses(step, slot) * 16 + 16)
                    pool.wait_ge(mm_done, step + 1)
                    nc.gpsimd.tensor_tensor(idle[:, 1:2], idle[:, 0:1], idle[:, 0:1], ALU.add)
                    nc.gpsimd.tensor_copy(high[:, slot, :], ring[:, slot, :]).then_inc(rounded, 1)
                pool.wait_ge(rounded, step + 1)
                nc.gpsimd.tensor_tensor(low[:, slot, :], ring[:, slot, :], high[:, slot, :].bitcast(F32), ALU.subtract
                                        ).then_inc(w_split, 1)
            steps(pool, split_weights)

        @block.tensor
        def _(pe):
            pe.sem_inc(mm_done, 2)

            def mult(step, slot, tile, args, j):
                pe.wait_ge(w_split, step + 3)
                pe.wait_ge(finished, step + 1)
                a_high, a_low = args["rhs"]
                for n in range(split):
                    for x, (w, a) in enumerate(((low, a_high), (high, a_low), (high, a_high))):
                        for c in range(k):
                            last = nc.tensor.matmul(psum[:, slot, n, 0:wn], w[:, slot, c * P:(c + 1) * P],
                                                    a[:, c, n * wn:(n + 1) * wn],
                                                    start=x == 0 and c == 0, stop=x == 2 and c == k - 1)
                last.then_inc(mm_done, 1)
            steps(pe, mult, settle=lambda step: pe.wait_ge(finished, step + 2))

        def round_weights(eng, copy):
            def body(step, slot, tile, args, j):
                eng.wait_ge(w_in[slot], slot_uses(step, slot) * 16 + 16)
                eng.wait_ge(mm_done, step + 1)
                copy(high[:, slot, :], ring[:, slot, :]).then_inc(rounded, 1)
            return body

        def take_out(eng):
            eng.sem_inc(finished, 2)
            if stores:
                for slot in range(2):
                    eng.sem_inc(stored[slot], 1)

            def evacuate(step, slot, tile, args, j):
                eng.wait_ge(mm_done, step + 3)
                if stores:
                    eng.wait_ge(stored[slot], slot_uses(step, slot) * 16 + 1)
                if has_aux:
                    eng.wait_ge(aux_in[slot], slot_uses(step, slot) * 16 + 16)
                args.get("finish", finish)(nc, eng, psum[:, slot, :, 0:wn], thirds(stage[:, slot, :]),
                       thirds(aux[:, slot, :]) if has_aux else None, args, j, step, chain).then_inc(finished, 1)
                if stores:
                    eng.wait_ge(finished, step + 3)
                    eng.dma_start(args["dram"][bass.DynSlice(j + args.get("at", 0), 1), :, :].rearrange("a p n -> (a p) n"),
                                  stage[:, slot, :]).then_inc(stored[slot], 16)
            steps(eng, evacuate)
            if stores:
                for slot in range(2):
                    eng.wait_ge(stored[slot], (total + 1 - slot) // 2 * 16 + 1)

        if on_vector:
            @block.vector
            def _(dve):
                take_out(dve)

            @block.scalar
            def _(act):
                steps(act, round_weights(act, lambda out, in_: act.activation(out, in_, ACT.Copy)))
        else:
            @block.scalar
            def _(act):
                if beside:
                    beside["scalar_first"](act)
                take_out(act)

            @block.vector
            def _(dve):
                if beside:
                    beside["vector"](dve)
                else:
                    steps(dve, round_weights(dve, nc.vector.tensor_copy))


def tile_of(buf, j):
    return buf[:, bass.DynSlice(j, 1), :].rearrange("p a (n c) -> p (a n) c", n=SPLIT)


def finish_copy(nc, act, psum, stage, aux, args, j, step, chain):
    return nc.scalar.activation(stage, psum, args["func"], scale=args.get("scale", 1.0))


def finish_square(nc, dve, psum, stage, aux, args, j, step, chain):
    nth = step - args["skipped"]
    nc.vector.tensor_scalar(stage, psum, 0.0, None, ALU.max).then_inc(chain[0], 1)
    dve.wait_ge(chain[0], nth * 2 + 1)
    nc.vector.tensor_tensor(stage, stage, stage, ALU.mult).then_inc(chain[0], 1)
    dve.wait_ge(chain[0], nth * 2 + 2)
    high, low = (tile_of(part, j) for part in args["out"])
    nc.vector.tensor_copy(high, stage).then_inc(chain[1], 1)
    dve.wait_ge(chain[1], nth + 1)
    return nc.vector.tensor_tensor(low, stage, high.bitcast(F32), ALU.subtract)


def finish_residual(nc, dve, psum, stage, aux, args, j, step, chain):
    out = tile_of(args["out"], j)
    return nc.vector.tensor_tensor(out, out, psum, ALU.add)


def finish_gated(nc, dve, psum, stage, aux, args, j, step, chain):
    out = tile_of(args["out"], j)
    if args["part"] == 0:
        return nc.vector.tensor_tensor(out, psum, aux, ALU.mult)
    nc.vector.tensor_tensor(stage, psum, aux, ALU.mult).then_inc(chain[0], 1)
    dve.wait_ge(chain[0], step - (CHUNKS - 1))
    return nc.vector.tensor_tensor(out, out, stage, ALU.add)


def split_tiles(nc, name, tiles):
    with ExitStack() as ctx:
        rounded = phase_semaphores(ctx, nc, name)("_rounded")
        block = ctx.enter_context(nc.Block())

        @block.scalar
        def _(act):
            for value, high, low in tiles:
                act.activation(high, value, ACT.Copy).then_inc(rounded, 1)

        @block.vector
        def _(dve):
            for n, (value, high, low) in enumerate(tiles):
                dve.wait_ge(rounded, n + 1)
                nc.vector.tensor_tensor(low, value, high.bitcast(F32), ALU.subtract)


def rmsnorm(nc, name, x, gain, ones, h, sq_buf, high=None):
    with ExitStack() as ctx:
        rstd = sb(ctx, nc, name + "_rstd", [P, W])
        psum = banks(ctx, nc, name + "_psum", SPLIT)
        sem = phase_semaphores(ctx, nc, name)
        sq_ready, summed, mean_ready, root_ready, chain = (sem(s) for s in
            ("_sq_ready", "_summed", "_mean_ready", "_root_ready", "_chain"))
        normed, rounded, halved = sem("_normed"), sem("_rounded"), sem("_halved")
        block = ctx.enter_context(nc.Block())

        @block.scalar
        def _(act):
            for c in range(CHUNKS):
                if c >= 2:
                    act.wait_ge(summed, c - 1)
                act.activation(sq_buf[:, c % 2, :], x[:, c, :], ACT.Square).then_inc(sq_ready, 1)
            act.wait_ge(mean_ready, 1)
            act.activation(rstd[:, :], rstd[:, :], ACT.Sqrt).then_inc(root_ready, 1)
            for c in range(CHUNKS if high is not None else 0):
                act.wait_ge(normed, c + 1)
                act.activation(high[:, c, :], sq_buf[:, c % 2, :], ACT.Copy).then_inc(rounded, 1)

        @block.tensor
        def _(pe):
            for c in range(CHUNKS):
                pe.wait_ge(sq_ready, c + 1)
                for n in range(SPLIT):
                    last = nc.tensor.matmul(psum[:, n, 0:WN], ones[:, :], sq_buf[:, c % 2, n * WN:(n + 1) * WN],
                                            start=c == 0, stop=c == CHUNKS - 1)
                last.then_inc(summed, 1)

        @block.vector
        def _(dve):
            link = Chain(dve, chain)
            dve.wait_ge(summed, CHUNKS)
            link(nc.vector.tensor_scalar(rstd[:, :].rearrange("p (n c) -> p n c", n=SPLIT), psum[:, :, 0:WN],
                                         1.0 / D, EPS, ALU.mult, ALU.add))
            nc.vector.reciprocal(rstd[:, :], rstd[:, :]).then_inc(mean_ready, 1)
            dve.wait_ge(root_ready, 1)
            def rest(c):
                dve.wait_ge(rounded, c + 1)
                nc.vector.tensor_tensor(h[:, c, :], sq_buf[:, c % 2, :], high[:, c, :].bitcast(F32), ALU.subtract
                                        ).then_inc(halved, 1)

            for c in range(CHUNKS):
                if high is not None and c >= 2:
                    dve.wait_ge(halved, c - 1)
                nc.vector.scalar_tensor_tensor(out=h[:, c, :] if high is None else sq_buf[:, c % 2, :], in0=x[:, c, :],
                                               scalar=gain[:, c:c + 1], in1=rstd[:, :], op0=ALU.mult, op1=ALU.mult
                                               ).then_inc(normed, 1)
                if high is not None and c >= 1:
                    rest(c - 1)
            if high is not None:
                rest(CHUNKS - 1)


def load_all(nc, name, pairs):
    with ExitStack() as ctx:
        landed = phase_semaphores(ctx, nc, name)("_landed")
        block = ctx.enter_context(nc.Block())

        @block.sync
        def _(sp):
            for dst, src in pairs[0::2]:
                sp.dma_start(dst, src).then_inc(landed, 16)
            sp.wait_ge(landed, 16 * len(pairs))

        @block.scalar
        def _(act):
            for dst, src in pairs[1::2]:
                act.dma_start(dst, src).then_inc(landed, 16)


def conv_beside(ctx, nc, u, t, out, conv_out):
    CT, PAD = CONV_CH // P, CONV_W - 1
    val = sb(ctx, nc, "glu_value", [P, CT, W])
    gate = sb(ctx, nc, "glu_gate", [P, CT, W])
    gp = sb(ctx, nc, "glu_prompt", [P, CT, PAD + TP])
    gs = sb(ctx, nc, "glu_sample", [P, CT, NB, PAD + TS])
    taps = sb(ctx, nc, "conv_a_taps", [P, CONV_W, CT])
    bias = sb(ctx, nc, "conv_a_bias", [P, CT])
    sem = phase_semaphores(ctx, nc, "conv_a_")
    params_in, gate_ready, glu_ready, chain, states_out = (sem(s) for s in (
        "params_in", "gate_ready", "glu_ready", "chain", "states_out"))
    tile_in = [sem(f"tile_in{c}") for c in range(CT)]

    def sync_first(sp):
        sp.dma_start(taps[:, :, :], t["conv_a_w"]).then_inc(params_in, 16)
        sp.dma_start(bias[:, :], t["conv_a_vecs"][:, 0, :]).then_inc(params_in, 16)
        for c in range(CT):
            sp.dma_start(val[:, c, :], u[T_A + c]).then_inc(tile_in[c], 16)
            sp.dma_start(gate[:, c, :], u[T_AG + c]).then_inc(tile_in[c], 16)
            sp.dma_start(gs[:, c, :, 0:PAD], t["state_conv_a"][c]).then_inc(tile_in[c], 16)

    def sync_last(sp):
        sp.wait_ge(glu_ready, CT)
        for c in range(CT):
            sp.dma_start(conv_out[0][c], gp[:, c, TP:TP + PAD]).then_inc(states_out, 16)
            sp.dma_start(conv_out[1][c], gs[:, c, :, TS:TS + PAD]).then_inc(states_out, 16)
        sp.wait_ge(states_out, 32 * CT)

    def scalar_first(act):
        for c in range(CT):
            act.wait_ge(tile_in[c], 48)
            act.activation(gate[:, c, :], gate[:, c, :], ACT.Sigmoid).then_inc(gate_ready, 1)

    def vector(dve):
        link = Chain(dve, chain)
        link(nc.vector.memset(gp[:, :, 0:PAD], 0.0))
        dve.wait_ge(params_in, 32)
        for c in range(CT):
            dve.wait_ge(gate_ready, c + 1)
            link(nc.vector.tensor_tensor(gp[:, c, PAD:PAD + TP], val[:, c, 0:TP], gate[:, c, 0:TP], ALU.mult))
            nc.vector.tensor_tensor(gs[:, c, :, PAD:PAD + TS], val[:, c, TP:W].rearrange("p (b s) -> p b s", b=NB),
                                    gate[:, c, TP:W].rearrange("p (b s) -> p b s", b=NB), ALU.mult).then_inc(glu_ready, 1)
            dve.wait_ge(glu_ready, c + 1)
            yp = out[:, c, 0:TP]
            ys = out[:, c, TP:W].rearrange("p (b s) -> p b s", b=NB)
            for k in range(CONV_W):
                w = taps[:, k, c:c + 1]
                for y, src in ((yp, gp[:, c, k:k + TP]), (ys, gs[:, c, :, k:k + TS])):
                    if k == 0:
                        last = nc.vector.tensor_scalar(y, src, w, bias[:, c:c + 1], ALU.mult, ALU.add)
                    else:
                        last = nc.vector.scalar_tensor_tensor(out=y, in0=src, scalar=w, in1=y, op0=ALU.mult, op1=ALU.add)
                    last.then_inc(chain, 1)
                link.n += 2
                dve.wait_ge(chain, link.n)

    return dict(sync_first=sync_first, sync_last=sync_last, scalar_first=scalar_first, vector=vector)


def conv_norm(nc, t, ones, out):
    CT = CONV_CH // P
    with ExitStack() as ctx:
        sq = sb(ctx, nc, "ln_sq", [P, CT, W])
        vecs = sb(ctx, nc, "conv_a_vecs", [P, 3, CT])
        rstd = sb(ctx, nc, "ln_rstd", [P, W])
        psum = banks(ctx, nc, "ln_psum", 2 * SPLIT).ap().rearrange("p (s n) c -> p s n c", s=2)
        sem = phase_semaphores(ctx, nc, "conv_norm_")
        params_in, summed, centred, sq_ready, sq_summed, var_ready, root_ready, scaled, out_done, chain = (
            sem(s) for s in ("params_in", "summed", "centred", "sq_ready", "sq_summed", "var_ready", "root_ready",
                             "scaled", "out_done", "chain"))
        block = ctx.enter_context(nc.Block())
        thirds = lambda ap: ap.rearrange("p (n c) -> p n c", n=SPLIT)

        @block.sync
        def _(sp):
            sp.dma_start(vecs[:, :, :], t["conv_a_vecs"]).then_inc(params_in, 16)

        @block.scalar
        def _(act):
            for c in range(CT):
                act.wait_ge(centred, c + 1)
                act.activation(sq[:, c, :], out[:, c, :], ACT.Square).then_inc(sq_ready, 1)
            act.wait_ge(var_ready, 1)
            act.activation(rstd[:, :], rstd[:, :], ACT.Sqrt).then_inc(root_ready, 1)
            act.wait_ge(params_in, 16)
            for c in range(CT):
                act.wait_ge(scaled, c + 1)
                act.activation(out[:, c, :], out[:, c, :], ACT.Silu, bias=vecs[:, 2, c:c + 1]).then_inc(out_done, 1)
            act.wait_ge(out_done, CT)

        @block.tensor
        def _(pe):
            for c in range(CT):
                for n in range(SPLIT):
                    last = nc.tensor.matmul(psum[:, 0, n, 0:WN], ones[:, :], out[:, c, n * WN:(n + 1) * WN],
                                            start=c == 0, stop=c == CT - 1)
            last.then_inc(summed, 1)
            for c in range(CT):
                pe.wait_ge(sq_ready, c + 1)
                for n in range(SPLIT):
                    last = nc.tensor.matmul(psum[:, 1, n, 0:WN], ones[:, :], sq[:, c, n * WN:(n + 1) * WN],
                                            start=c == 0, stop=c == CT - 1)
            last.then_inc(sq_summed, 1)

        @block.vector
        def _(dve):
            link = Chain(dve, chain)
            dve.wait_ge(summed, 1)
            for c in range(CT):
                nc.vector.scalar_tensor_tensor(out=thirds(out[:, c, :]), in0=psum[:, 0, :, 0:WN], scalar=-1.0 / CONV_CH,
                                               in1=thirds(out[:, c, :]), op0=ALU.mult, op1=ALU.add).then_inc(centred, 1)
            dve.wait_ge(sq_summed, 1)
            link(nc.vector.tensor_scalar(thirds(rstd[:, :]), psum[:, 1, :, 0:WN], 1.0 / CONV_CH, EPS, ALU.mult, ALU.add))
            nc.vector.reciprocal(rstd[:, :], rstd[:, :]).then_inc(var_ready, 1)
            dve.wait_ge(root_ready, 1)
            dve.wait_ge(params_in, 16)
            dve.wait_ge(centred, CT)
            for c in range(CT):
                nc.vector.scalar_tensor_tensor(out=out[:, c, :], in0=out[:, c, :], scalar=vecs[:, 1, c:c + 1],
                                               in1=rstd[:, :], op0=ALU.mult, op1=ALU.mult).then_inc(scaled, 1)


def gdn_inputs(nc, u, t, ones, ident, qkv, by_token, conv_out):
    NTILE, PAD = 12, GDN_CONV_W - 1
    RING = 3
    with ExitStack() as ctx:
        xp = sb(ctx, nc, "short_prompt", [P, RING, PAD + TP])
        xs = sb(ctx, nc, "short_sample", [P, RING, NB, PAD + TS])
        sq = sb(ctx, nc, "qk_sq", [P, 2, W])
        rn = sb(ctx, nc, "qk_rnorm", [P, 2, W])
        taps = sb(ctx, nc, "short_taps", [P, GDN_CONV_W, NTILE])
        misc = sb(ctx, nc, "misc", [64, W])
        mabs = sb(ctx, nc, "misc_abs", [64, W])
        avec = sb(ctx, nc, "decay_vecs", [64, 3])
        psum = banks(ctx, nc, "qk_psum", 2 * SPLIT).ap().rearrange("p (s n) c -> p s n c", s=2)
        tpsum = banks(ctx, nc, "misc_psum", 1)
        sem = phase_semaphores(ctx, nc, "gdn_in_")
        params_in, misc_in, states_out = sem("params_in"), sem("misc_in"), sem("states_out")
        tile_in = [sem(f"tile_in{c}") for c in range(RING)]
        states_sent = [sem(f"states_sent{c}") for c in range(RING)]
        padded, conv_done, silu_done, sq_ready, sq_summed, mean_ready, root_ready, chain, achain, misc_ready, turned = (
            sem(s) for s in ("padded", "conv_done", "silu_done", "sq_ready", "sq_summed", "mean_ready", "root_ready",
                             "chain", "achain", "misc_ready", "turned"))
        block = ctx.enter_context(nc.Block())
        thirds = lambda ap: ap.rearrange("p (n c) -> p n c", n=SPLIT)
        A = slice(32, 36)

        @block.sync
        def _(sp):
            sp.dma_start(misc[0:32, :], u[T_MISC, 0:32, :]).then_inc(misc_in, 16)
            sp.dma_start(misc[A, :], u[T_MISC, 0:4, :]).then_inc(misc_in, 16)
            sp.dma_start(avec[A, 0:2], t["decay_vecs"]).then_inc(misc_in, 16)
            sp.dma_start(taps[:, :, :], t["gdn_conv_w"]).then_inc(params_in, 16)
            for c in range(NTILE):
                s = c % RING
                if c >= RING:
                    sp.wait_ge(conv_done, c - RING + 1)
                    sp.wait_ge(states_sent[s], 32 * (c // RING))
                sp.dma_start(xp[:, s, PAD:PAD + TP], u[T_QKV + c, :, 0:TP]).then_inc(tile_in[s], 16)
                sp.dma_start(xs[:, s, :, 0:PAD], t["state_conv_qkv"][c]).then_inc(tile_in[s], 16)
                sp.dma_start(xs[:, s, :, PAD:PAD + TS], u[T_QKV + c, :, TP:W].rearrange("p (b s) -> p b s", b=NB)
                             ).then_inc(tile_in[s], 16)

        @block.gpsimd
        def _(pool):
            nc.gpsimd.memset(xp[:, :, 0:PAD], 0.0).then_inc(padded, 1)

        @block.scalar
        def _(act):
            def send_state(c):
                s = c % RING
                act.wait_ge(tile_in[s], 48 * (c // RING + 1))
                act.dma_start(conv_out[0][c], xp[:, s, TP:TP + PAD]).then_inc(states_sent[s], 16)
                act.dma_start(conv_out[1][c], xs[:, s, :, TS:TS + PAD]).then_inc(states_sent[s], 16)
            for c in range(NTILE):
                send_state(c)
                act.wait_ge(conv_done, c + 1)
                act.activation(qkv[:, c, :], qkv[:, c, :], ACT.Silu).then_inc(silu_done, 1)
            link = Chain(act, achain)
            act.wait_ge(misc_in, 48)
            link(act.activation(mabs[A, :], misc[A, :], ACT.Abs, bias=avec[A, 1:2]))
            link(act.activation(misc[0:32, :], misc[0:32, :], ACT.Sigmoid))
            link(act.activation(mabs[A, :], mabs[A, :], ACT.Exp, scale=-1.0))
            link(act.activation(avec[A, 2:3], avec[A, 0:1], ACT.Exp))
            link(act.activation(mabs[A, :], mabs[A, :], ACT.Ln, bias=1.0))
            act.wait_ge(silu_done, 8)
            for c in range(8 + 2):
                if c >= 2:
                    act.wait_ge(mean_ready, c - 1)
                    act.activation(rn[:, c % 2, :], rn[:, c % 2, :], ACT.Sqrt).then_inc(root_ready, 1)
                if c < 8:
                    act.activation(sq[:, c % 2, :], qkv[:, c, :], ACT.Square).then_inc(sq_ready, 1)
            for s in range(RING):
                act.wait_ge(states_sent[s], 32 * (NTILE // RING))

        @block.tensor
        def _(pe):
            for c in range(8):
                pe.wait_ge(sq_ready, c + 1)
                if c >= 2:
                    pe.wait_ge(mean_ready, c - 1)
                for n in range(SPLIT):
                    last = nc.tensor.matmul(psum[:, c % 2, n, 0:WN], ones[:, :], sq[:, c % 2, n * WN:(n + 1) * WN],
                                            start=True, stop=True)
                last.then_inc(sq_summed, 1)
            pe.wait_ge(misc_ready, 1)
            for i in range(NT + 1):
                n = P if i < NT else NB * TS
                last = nc.tensor.transpose(tpsum[0:n, 0, i * 36:(i + 1) * 36], misc[0:36, i * P:i * P + n], ident[0:36, 0:36])
            last.then_inc(turned, 1)

        @block.vector
        def _(dve):
            link = Chain(dve, chain)
            dve.wait_ge(params_in, 16)
            dve.wait_ge(padded, 1)
            for c in range(NTILE):
                s = c % RING
                dve.wait_ge(tile_in[s], 48 * (c // RING + 1))
                yp = qkv[:, c, 0:TP]
                ys = qkv[:, c, TP:W].rearrange("p (b s) -> p b s", b=NB)
                for k in range(GDN_CONV_W):
                    w = taps[:, k, c:c + 1]
                    for y, src in ((yp, xp[:, s, k:k + TP]), (ys, xs[:, s, :, k:k + TS])):
                        if k == 0:
                            last = nc.vector.tensor_scalar(y, src, w, None, ALU.mult)
                        else:
                            last = nc.vector.scalar_tensor_tensor(out=y, in0=src, scalar=w, in1=y,
                                                                  op0=ALU.mult, op1=ALU.add)
                        if k < GDN_CONV_W - 1 or y is yp:
                            last.then_inc(chain, 1)
                            link.n += 1
                        else:
                            last.then_inc(conv_done, 1)
                    dve.wait_ge(chain, link.n)
            dve.wait_ge(achain, 5)
            link(nc.vector.tensor_scalar(misc[A, :], misc[A, :], avec[A, 1:2], 0.0, ALU.add, ALU.max))
            link(nc.vector.tensor_tensor(misc[A, :], misc[A, :], mabs[A, :], ALU.add))
            nc.vector.tensor_scalar(misc[A, :], misc[A, :], avec[A, 2:3], -1.0, ALU.mult, ALU.mult).then_inc(misc_ready, 1)
            for c in range(8):
                dve.wait_ge(sq_summed, c + 1)
                if c >= 2:
                    dve.wait_ge(chain, link.n)
                link(nc.vector.tensor_scalar(thirds(rn[:, c % 2, :]), psum[:, c % 2, :, 0:WN], EPS, None, ALU.add))
                nc.vector.reciprocal(rn[:, c % 2, :], rn[:, c % 2, :]).then_inc(mean_ready, 1)
                dve.wait_ge(root_ready, c + 1)
                scale = float(P) ** -0.5 if c < GH else 1.0
                link(nc.vector.scalar_tensor_tensor(out=qkv[:, c, :], in0=qkv[:, c, :], scalar=scale, in1=rn[:, c % 2, :],
                                                    op0=ALU.mult, op1=ALU.mult))
            dve.wait_ge(turned, 1)
            link(nc.vector.tensor_copy(by_token[:, 0:NT, :], tpsum[:, 0, 0:NT * 36].rearrange("p (t c) -> p t c", c=36)))
            link(nc.vector.tensor_copy(by_token[0:NB * TS, NT, :], tpsum[0:NB * TS, 0, NT * 36:(NT + 1) * 36]))


def delta_rule(nc, name, qkv, by_token, ones, ident, masks, t_dram, n, levels, tiles, at, out, state_out, batches=0):
    H, Q = GH, GH * n
    CH = 3
    with ExitStack() as ctx:
        S = lambda nm, shape: sb(ctx, nc, name + "_" + nm, shape)
        tri, bound, lmask = S("tri", [n, n]), S("bound", [n, n]), S("lmask", [n, levels, n])
        qs, ks, vs = S("q", [P, H, n]), S("k", [P, H, n]), S("v", [P, H, n])
        gu, bi = S("gu", [n, H, n]), S("bi", [n, H, n])
        gc, egc, be = S("gc", [n, H]), S("egc", [n, H]), S("be", [n, H])
        dt_, egrow = S("dt", [n, H, n]), S("egrow", [P, H, n])
        at_, atl, qkt = S("at", [n, H, n]), S("atl", [n, levels, H, n]), S("qkt", [n, H, n])
        ys, x, xt = S("y", [n, H, n]), S("x", [n, H, n]), S("xt", [n, H, n])
        kbg, vb, kd, qg = S("kbg", [n, H, P]), S("vb", [n, H, P]), S("kd", [n, H, P]), S("qg", [P, H, n])
        vw, kcd, vn = S("vw", [n, H, P]), S("kcd", [P, H, n]), S("vn", [n, H, P])
        dend = S("dend", [n, H])
        if batches:
            bmask, rmask = S("bmask", [P, batches, n]), S("rmask", [n, batches])
            state = S("state", [P, batches, H, P])
            kcdm, vexp, oin = S("kcdm", [P, H, batches, n]), S("vexp", [n, H, batches, P]), S("oin", [P, H, n])
        else:
            state = S("state", [P, H, P])
        ps = banks(ctx, nc, name + "_psum", 8)
        hv = lambda b, p=P, w=n: ps[0:p, b, 0:H * w].rearrange("p (h c) -> p h c", h=H)
        ROW, BETA, COL, KK, KQ, KT, VT, Y = range(8)
        PAIRS, PH = 2, H // 2
        pair_banks = ((Y, KK, KQ), (ROW, BETA, COL))
        pair_of = lambda p: slice(p * PH, (p + 1) * PH)
        XY, YX, VW, KCD, P1, OUT, DS = KK, KQ, KT, VT, Y, ROW, BETA
        sem = phase_semaphores(ctx, nc, name + "_")
        (params_in, state_ready, in_ready, gu_ready, pre_mm, gc_ready, egc_ready, diff_ready, dt_ready, egrow_ready,
         at_ready, level_ready, factors_ready, y_mm, y_ready, xy_mm, x_ready, sol_mm, sol_ready, p1_mm, vn_ready,
         o_mm, o_out, ds_mm, chain, updated, sent) = (sem(s) for s in (
            "params_in", "state_ready", "in_ready", "gu_ready", "pre_mm", "gc_ready", "egc_ready", "diff_ready",
            "dt_ready", "egrow_ready", "at_ready", "level_ready", "factors_ready", "y_mm", "y_ready", "xy_mm",
            "x_ready", "sol_mm", "sol_ready", "p1_mm", "vn_ready", "o_mm", "o_out", "ds_mm", "chain", "updated", "sent"))
        block = ctx.enter_context(nc.Block())
        wide = lambda ap, k: ap.unsqueeze(2).to_broadcast([ap.shape[0], ap.shape[1], k])
        heads = lambda ap: ap.unsqueeze(1).to_broadcast([ap.shape[0], H, ap.shape[1]])

        def tile_loop(eng, body):
            if tiles == 1:
                body(0)
            else:
                with eng.Fori(0, tiles) as t:
                    body(t)

        @block.sync
        def _(sp):
            sp.dma_start(tri[:, :], masks["tri"]).then_inc(params_in, 16)
            sp.dma_start(bound[:, :], masks["bound"]).then_inc(params_in, 16)
            sp.dma_start(lmask[:, :, :], masks["levels"]).then_inc(params_in, 16)
            if batches:
                sp.dma_start(bmask[:, :, :], masks["batch_cols"]).then_inc(params_in, 16)
                sp.dma_start(rmask[:, :], masks["batch_rows"]).then_inc(params_in, 16)
                sp.dma_start(state[:, :, :, :], t_dram["state_gdn"]).then_inc(state_ready, 16)
            if batches:
                sp.wait_ge(updated, 2 * H)
            else:
                sp.wait_ge(state_ready, tiles + 1)
            sp.dma_start(state_out, state.ap()).then_inc(sent, 16)
            sp.wait_ge(sent, 16)

        @block.scalar
        def _(act):
            def body(t):
                if not batches:
                    act.wait_ge(state_ready, t + 1)
                cols = bass.DynSlice(t * n + at, n)
                act.activation(qs[:, :, :], qkv[:, 0:4, cols], ACT.Copy)
                act.activation(ks[:, :, :], qkv[:, 4:8, cols], ACT.Copy)
                act.activation(vs[:, :, :], qkv[:, 8:12, cols], ACT.Copy).then_inc(in_ready, 1)
                act.wait_ge(pre_mm, t + 1)
                act.activation(egrow[:, :, :], hv(ROW), ACT.Exp).then_inc(egrow_ready, 1)
                act.wait_ge(gc_ready, t + 1)
                act.activation(egc[:, :], gc[:, :], ACT.Exp).then_inc(egc_ready, 1)
                act.wait_ge(diff_ready, t + 1)
                act.activation(dt_[:, :, :], dt_[:, :, :], ACT.Exp).then_inc(dt_ready, 1)
                for l in range(1, levels):
                    for p in range(PAIRS):
                        act.wait_ge(y_mm, (t * levels + l) * PAIRS + p + 1)
                        act.activation(ys[:, pair_of(p), :], hv(pair_banks[p][0], n)[:, pair_of(p), :], ACT.Copy).then_inc(y_ready, 1)
                act.wait_ge(sol_mm, t + 1)
                act.activation(vw[:, :, :], hv(VW, n, P), ACT.Copy)
                act.activation(kcd[:, :, :], hv(KCD), ACT.Copy).then_inc(sol_ready, 1)
                act.wait_ge(o_mm, t + 1)
                if batches:
                    act.activation(oin[:, :, :], hv(COL), ACT.Copy).then_inc(o_out, 1)
                else:
                    act.activation(out[:, :, cols], hv(OUT), ACT.Copy).then_inc(o_out, 1)
            tile_loop(act, body)

        @block.gpsimd
        def _(pool):
            pool.wait_ge(params_in, 80 if batches else 48)

            def body(t):
                pool.wait_ge(at_ready, t + 1)
                for l in range(levels):
                    nc.gpsimd.tensor_tensor(atl[:, l, :, :], at_[:, :, :], heads(lmask[:, l, :]), ALU.mult
                                            ).then_inc(level_ready, 1)
                pool.wait_ge(level_ready, (t + 1) * levels)
            tile_loop(pool, body)

        @block.tensor
        def _(pe):
            mm = nc.tensor.matmul

            def body(t):
                pe.wait_ge(in_ready, t + 1)
                pe.wait_ge(gu_ready, t + 1)
                mm(ps[:, ROW, 0:Q], ones[0:n, :], gu[:, :, :], start=True, stop=True)
                mm(ps[0:n, BETA, 0:Q], ones[0:n, 0:n], bi[:, :, :], start=True, stop=True)
                mm(ps[0:n, COL, 0:H], tri[:, :], by_token[0:n, bass.DynSlice(t + at // P, 1), 32:36].rearrange("p a h -> p (a h)"),
                   start=True, stop=True)
                for h in range(H):
                    mm(hv(KK, n)[:, h, :], ks[:, h, :], ks[:, h, :], start=True, stop=True)
                for h in range(H):
                    mm(hv(KQ, n)[:, h, :], ks[:, h, :], qs[:, h, :], start=True, stop=True)
                for h in range(H):
                    nc.tensor.transpose(hv(KT, n, P)[:, h, :], ks[:, h, :], ident[:, :])
                for h in range(H):
                    last = nc.tensor.transpose(hv(VT, n, P)[:, h, :], vs[:, h, :], ident[:, :])
                last.then_inc(pre_mm, 1)
                for l in range(levels):
                    pe.wait_ge(level_ready, t * levels + l + 1)
                    for p in range(PAIRS):
                        if l:
                            pe.wait_ge(x_ready, (t * levels + l - 1) * PAIRS + p + 1)
                        for h in range(p * PH, (p + 1) * PH):
                            last = mm(hv(pair_banks[p][0], n)[:, h, :], atl[:, l, h, :], x[:, h, :] if l else ident[0:n, 0:n],
                                      start=True, stop=True)
                        last.then_inc(y_mm, 1)
                    for p in range(PAIRS if l else 0):
                        pe.wait_ge(y_ready, (t * (levels - 1) + l - 1) * PAIRS + p + 1)
                        if l < levels - 1:
                            for h in range(p * PH, (p + 1) * PH):
                                mm(hv(pair_banks[p][1], n)[:, h, :], xt[:, h, :], ys[:, h, :], start=True, stop=True)
                        for h in range(p * PH, (p + 1) * PH):
                            last = mm(hv(pair_banks[p][2], n)[:, h, :], ys[:, h, :], xt[:, h, :], start=True, stop=True)
                        last.then_inc(xy_mm, 1)
                pe.wait_ge(x_ready, (t + 1) * levels * PAIRS)
                pe.wait_ge(factors_ready, t + 1)
                for h in range(H):
                    mm(hv(VW, n, P)[:, h, :], xt[:, h, :], vb[:, h, :], start=True, stop=True)
                for h in range(H):
                    last = mm(hv(KCD)[:, h, :], kbg[:, h, :], xt[:, h, :], start=True, stop=True)
                last.then_inc(sol_mm, 1)
                if batches:
                    pe.wait_ge(state_ready, 16)
                    pe.wait_ge(vn_ready, 1)
                    for h in range(H):
                        for b in range(batches):
                            last = mm(hv(P1, n, P)[:, h, :], kcdm[:, h, b, :], state[:, b, h, :],
                                      start=b == 0, stop=b == batches - 1)
                    last.then_inc(p1_mm, 1)
                    for h in range(H):
                        for b in range(batches):
                            w = n // batches
                            mm(hv(OUT)[:, h, b * w:(b + 1) * w], state[:, b, h, :], qg[:, h, b * w:(b + 1) * w],
                               start=True, stop=True)
                    pe.wait_ge(vn_ready, 2)
                    for h in range(H):
                        last = mm(hv(COL)[:, h, :], vn[:, h, :], qkt[:, h, :], start=True, stop=True)
                    last.then_inc(o_mm, 1)
                    for h in range(H):
                        pe.wait_ge(vn_ready, 3 + h)
                        if h >= 1:
                            pe.wait_ge(updated, 2 * h)
                        for half in range(2):
                            last = mm(ps[:, KQ + half, :], kd[:, h, :],
                                      vexp[:, h, half * 4:(half + 1) * 4, :], start=True, stop=True)
                        last.then_inc(ds_mm, 1)
                else:
                    pe.wait_ge(sol_ready, t + 1)
                    for h in range(H):
                        last = mm(hv(P1, n, P)[:, h, :], kcd[:, h, :], state[:, h, :], start=True, stop=True)
                    last.then_inc(p1_mm, 1)
                    pe.wait_ge(vn_ready, t + 1)
                    for h in range(H):
                        last = mm(hv(DS, P, P)[:, h, :], kd[:, h, :], vn[:, h, :], start=True, stop=True)
                    for h in range(H):
                        mm(hv(OUT)[:, h, :], state[:, h, :], qg[:, h, :], start=True, stop=False)
                        last = mm(hv(OUT)[:, h, :], vn[:, h, :], qkt[:, h, :], start=False, stop=True)
                    last.then_inc(o_mm, 1)
            tile_loop(pe, body)

        @block.vector
        def _(dve):
            V = nc.vector
            dve.wait_ge(params_in, 80 if batches else 48)
            if not batches:
                V.memset(state[:, :, :], 0.0).then_inc(state_ready, 1)
                dve.wait_ge(state_ready, 1)

            def body(t):
                cols = by_token[0:n, bass.DynSlice(t + at // P, 1), :].rearrange("p a c -> p (a c)")
                g, beta = cols[:, 32:36], cols[:, 4:8]
                V.tensor_tensor(gu[:, :, :], heads(tri[:, :]), wide(g, n), ALU.mult)
                V.tensor_tensor(bi[:, :, :], heads(ident[0:n, 0:n]), wide(beta, n), ALU.mult).then_inc(gu_ready, 1)
                dve.wait_ge(pre_mm, t + 1)
                V.tensor_copy(gc[:, :], ps[0:n, COL, 0:H]).then_inc(gc_ready, 1)
                dve.wait_ge(gc_ready, t + 1)
                dve.wait_ge(egrow_ready, t + 1)
                for h in range(H):
                    last = V.scalar_tensor_tensor(out=dt_[:, h, :], in0=hv(ROW, n)[:, h, :], scalar=gc[:, h:h + 1],
                                                  in1=bound[:, :], op0=ALU.subtract, op1=ALU.min)
                last.then_inc(diff_ready, 1)
                dve.wait_ge(dt_ready, t + 1)
                V.tensor_tensor(at_[:, :, :], hv(KK, n), dt_[:, :, :], ALU.mult).then_inc(chain, 1)
                V.tensor_tensor(qkt[:, :, :], hv(KQ, n), dt_[:, :, :], ALU.mult)
                if batches:
                    V.tensor_reduce(dend[:, :], dt_[:, :, TS - 1::TS], AX_X, ALU.add).then_inc(chain, 1)
                else:
                    V.tensor_copy(dend[:, :], dt_[:, :, n - 1]).then_inc(chain, 1)
                dve.wait_ge(chain, t * CH + 2)
                V.tensor_tensor(at_[:, :, :], at_[:, :, :], hv(BETA, n), ALU.mult).then_inc(at_ready, 1)
                dve.wait_ge(egc_ready, t + 1)
                V.tensor_tensor(be[:, :], beta, egc[:, :], ALU.mult).then_inc(chain, 1)
                V.tensor_tensor(vb[:, :, :], hv(VT, n, P), wide(beta, P), ALU.mult)
                V.tensor_tensor(kd[:, :, :], hv(KT, n, P), wide(dend[:, :], P), ALU.mult)
                V.tensor_tensor(qg[:, :, :], qs[:, :, :], egrow[:, :, :], ALU.mult)
                dve.wait_ge(chain, t * CH + 3)
                V.tensor_tensor(kbg[:, :, :], hv(KT, n, P), wide(be[:, :], P), ALU.mult).then_inc(factors_ready, 1)
                for p in range(PAIRS):
                    hs, unit = pair_of(p), ident[0:n, 0:n].unsqueeze(1).to_broadcast([n, PH, n])
                    dve.wait_ge(level_ready, t * levels + 1)
                    dve.wait_ge(y_mm, t * levels * PAIRS + p + 1)
                    V.tensor_tensor(x[:, hs, :], unit, hv(pair_banks[p][0], n)[:, hs, :], ALU.subtract)
                    V.tensor_tensor(xt[:, hs, :], unit, atl[:, 0, hs, :], ALU.subtract).then_inc(x_ready, 1)
                for l in range(1, levels):
                    for p in range(PAIRS):
                        hs = pair_of(p)
                        dve.wait_ge(xy_mm, (t * (levels - 1) + l - 1) * PAIRS + p + 1)
                        dve.wait_ge(x_ready, (t * levels + l - 1) * PAIRS + p + 1)
                        if l < levels - 1:
                            V.tensor_tensor(x[:, hs, :], x[:, hs, :], hv(pair_banks[p][1], n)[:, hs, :], ALU.subtract)
                        V.tensor_tensor(xt[:, hs, :], xt[:, hs, :], hv(pair_banks[p][2], n)[:, hs, :], ALU.subtract
                                        ).then_inc(x_ready, 1)
                dve.wait_ge(sol_ready, t + 1)
                if batches:
                    w = n // batches
                    for h in range(H):
                        last = V.tensor_tensor(kcdm[:, h, :, :], bmask[:, :, :],
                                               kcd[:, h, :].unsqueeze(1).to_broadcast([P, batches, n]), ALU.mult)
                    last.then_inc(vn_ready, 1)
                    dve.wait_ge(p1_mm, 1)
                    V.tensor_tensor(vn[:, :, :], vw[:, :, :], hv(P1, n, P), ALU.subtract).then_inc(vn_ready, 1)
                    dve.wait_ge(vn_ready, 2)
                    for h in range(H):
                        V.tensor_tensor(vexp[:, h, :, :], vn[:, h, :].unsqueeze(1).to_broadcast([n, batches, P]),
                                        wide(rmask[:, :], P), ALU.mult).then_inc(vn_ready, 1)
                    dve.wait_ge(o_out, 1)
                    V.tensor_tensor(out[:, :, at:at + n], oin[:, :, :], hv(OUT), ALU.add)
                    dve.wait_ge(state_ready, 16)
                    for h in range(H):
                        sh = state[:, :, h, :]
                        dve.wait_ge(p1_mm, 1)
                        dve.wait_ge(o_mm, 1)
                        V.tensor_tensor(sh, sh, wide(egrow[:, h, w - 1::w], P), ALU.mult).then_inc(updated, 1)
                        dve.wait_ge(updated, 2 * h + 1)
                        dve.wait_ge(ds_mm, h + 1)
                        V.tensor_tensor(sh, sh, ps[:, KQ:KQ + 2, :].rearrange("p a (b c) -> p (a b) c", b=4), ALU.add
                                        ).then_inc(updated, 1)
                else:
                    dve.wait_ge(p1_mm, t + 1)
                    V.tensor_tensor(vn[:, :, :], vw[:, :, :], hv(P1, n, P), ALU.subtract).then_inc(vn_ready, 1)
                    dve.wait_ge(o_mm, t + 1)
                    for h in range(H):
                        last = V.scalar_tensor_tensor(out=state[:, h, :], in0=state[:, h, :], scalar=egrow[:, h, n - 1:n],
                                                      in1=hv(DS, P, P)[:, h, :], op0=ALU.mult, op1=ALU.add)
                    last.then_inc(state_ready, 1)
                    dve.wait_ge(state_ready, t + 2)
            tile_loop(dve, body)


def gate_output(nc, o, u, ones, norm_g, out):
    with ExitStack() as ctx:
        z = sb(ctx, nc, "z", [P, GH, W])
        sq = sb(ctx, nc, "o_sq", [P, 2, W])
        rn = sb(ctx, nc, "o_rnorm", [P, 2, W])
        psum = banks(ctx, nc, "o_psum", 2 * SPLIT).ap().rearrange("p (s n) c -> p s n c", s=2)
        sem = phase_semaphores(ctx, nc, "gate_")
        z_in, z_ready, sq_ready, summed, mean_ready, root_ready, chain, scaled = (sem(s) for s in (
            "z_in", "z_ready", "sq_ready", "summed", "mean_ready", "root_ready", "chain", "scaled"))
        block = ctx.enter_context(nc.Block())
        thirds = lambda ap: ap.rearrange("p (n c) -> p n c", n=SPLIT)

        @block.sync
        def _(sp):
            sp.dma_start(z[:, :, :], u[T_Z:T_Z + GH].rearrange("h p n -> p h n")).then_inc(z_in, 16)

        @block.scalar
        def _(act):
            for h in range(GH):
                if h >= 2:
                    act.wait_ge(summed, h - 1)
                act.activation(sq[:, h % 2, :], o[:, h, :], ACT.Square).then_inc(sq_ready, 1)
            act.wait_ge(z_in, 16)
            act.activation(z[:, :, :], z[:, :, :], ACT.Silu).then_inc(z_ready, 1)
            for h in range(GH):
                act.wait_ge(mean_ready, h + 1)
                act.activation(rn[:, h % 2, :], rn[:, h % 2, :], ACT.Sqrt).then_inc(root_ready, 1)

        @block.tensor
        def _(pe):
            for h in range(GH):
                pe.wait_ge(sq_ready, h + 1)
                if h >= 2:
                    pe.wait_ge(mean_ready, h - 1)
                for n in range(SPLIT):
                    last = nc.tensor.matmul(psum[:, h % 2, n, 0:WN], ones[:, :], sq[:, h % 2, n * WN:(n + 1) * WN],
                                            start=True, stop=True)
                last.then_inc(summed, 1)

        @block.vector
        def _(dve):
            link = Chain(dve, chain)
            dve.wait_ge(z_ready, 1)
            for h in range(GH):
                dve.wait_ge(summed, h + 1)
                link(nc.vector.tensor_scalar(thirds(rn[:, h % 2, :]), psum[:, h % 2, :, 0:WN], 1.0 / P, EPS, ALU.mult, ALU.add))
                nc.vector.reciprocal(rn[:, h % 2, :], rn[:, h % 2, :]).then_inc(mean_ready, 1)
                link(nc.vector.scalar_tensor_tensor(out=z[:, h, :], in0=z[:, h, :], scalar=norm_g, in1=o[:, h, :],
                                                    op0=ALU.mult, op1=ALU.mult))
                dve.wait_ge(root_ready, h + 1)
                nc.vector.tensor_tensor(out[:, h, :], z[:, h, :], rn[:, h % 2, :], ALU.mult).then_inc(scaled, 1)
                dve.wait_ge(scaled, h + 1)


LB_FULL, LB_WIN = 1152, 768


def bias_rows(nc, t, rows, toeplitz, rb):
    L = LB_FULL + LB_WIN
    with ExitStack() as ctx:
        hot = sb(ctx, nc, "prompt_onehot", [N_BUCKETS + 1, L])
        out = sb(ctx, nc, "bias_out", [NSA_HEADS, L])
        psum = banks(ctx, nc, "bias_psum", 5)
        sem = phase_semaphores(ctx, nc, "bias_")
        hot_in, mm, copied, sent, spread = (sem(s) for s in ("hot_in", "mm", "copied", "sent", "spread"))
        block = ctx.enter_context(nc.Block())
        WB = 384

        @block.sync
        def _(sp):
            sp.dma_start(hot[:, :], t["prompt_onehot"]).then_inc(hot_in, 16)
            sp.wait_ge(copied, 1)
            sp.dma_start(rows, out[:, :]).then_inc(sent, 16)
            sp.wait_ge(sent, 16)
            for off, n, to in ((0, TP, 0), (LB_FULL, 640, TP)):
                src = bass.AP(rows.tensor, off + P - 1, [[L, NSA_HEADS], [-1, P], [1, n]])
                sp.dma_start(toeplitz[:, :, to:to + n], src).then_inc(spread, 16)
            sp.wait_ge(spread, 32)

        @block.tensor
        def _(pe):
            pe.wait_ge(hot_in, 16)
            for i in range(L // WB):
                last = nc.tensor.matmul(psum[0:NSA_HEADS, i, 0:WB], rb[:, :], hot[:, i * WB:(i + 1) * WB], start=True, stop=True)
            last.then_inc(mm, 1)

        @block.vector
        def _(dve):
            dve.wait_ge(mm, 1)
            nc.vector.tensor_copy(out[:, :].rearrange("p (n c) -> p n c", c=WB), psum[0:NSA_HEADS, :, 0:WB]).then_inc(copied, 1)


def sparse_prompt(nc, t, u, kv, toeplitz, ident, by_token, out, pages, kct_past, vct_past):
    SETS, PER = 2, 8
    SB = PER * PAGE // L_CMP
    NC = TP // L_CMP
    with ExitStack() as ctx:
        kvp = sb(ctx, nc, "kv_prompt", [P, 6, TP])
        vtok = sb(ctx, nc, "v_by_token", [P, 2, NT, P])
        kc, vct = sb(ctx, nc, "k_cmp", [P, NC]), sb(ctx, nc, "v_cmp_t", [P, NC])
        vc = sb(ctx, nc, "v_cmp", [NC, P])
        wpos = sb(ctx, nc, "w_pos", [P, 2, L_CMP])
        with ExitStack() as c2:
            tmp = sb(c2, nc, "cmp_tmp", [P, 2, TP])
            ps = banks(c2, nc, "nsa_prep_psum", 5)
            sem = phase_semaphores(c2, nc, "nsa_prep_")
            kv_in, w_in, cmp_ready, turned, chain, copied = (sem(s) for s in ("kv_in", "w_in", "cmp_ready", "turned", "chain", "copied"))
            block = c2.enter_context(nc.Block())

            @block.sync
            def _(sp):
                sp.dma_start(wpos[:, :, :].rearrange("p a b -> p (a b)"),
                             t["nsa_cmp_w"].partition_broadcast(P)).then_inc(w_in, 16)
                sp.dma_start(kvp[:, :, :], kv[:, :, 0:TP].rearrange("k p n -> p k n")).then_inc(kv_in, 16)

            @block.vector
            def _(dve):
                dve.wait_ge(w_in, 16)
                dve.wait_ge(kv_in, 16)
                blocks = lambda ap: ap.rearrange("p (n l) -> p n l", l=L_CMP)
                for s in range(2):
                    nc.vector.tensor_tensor(blocks(tmp[:, s, :]), blocks(kvp[:, s, :]),
                                            wpos[:, s, :].unsqueeze(1).to_broadcast([P, NC, L_CMP]), ALU.mult).then_inc(chain, 1)
                dve.wait_ge(chain, 2)
                nc.vector.tensor_reduce(kc[:, :], blocks(tmp[:, 0, :]), AX_X, ALU.add)
                nc.vector.tensor_reduce(vct[:, :], blocks(tmp[:, 1, :]), AX_X, ALU.add).then_inc(cmp_ready, 1)

            @block.tensor
            def _(pe):
                pe.wait_ge(kv_in, 16)
                for i, kind in enumerate((KV_VSLC, KV_VWIN)):
                    for b in range(NT):
                        nc.tensor.transpose(ps[:, 2 * i + b // 4, (b % 4) * P:(b % 4 + 1) * P],
                                            kvp[:, kind, b * P:(b + 1) * P], ident[:, :])
                pe.wait_ge(cmp_ready, 1)
                nc.tensor.transpose(ps[0:NC, 4, 0:P], vct[:, :], ident[:, :]).then_inc(turned, 1)

            @block.scalar
            def _(act):
                act.wait_ge(turned, 1)
                act.activation(vtok[:, :, :, :], ps[:, 0:4, :], ACT.Copy)
                act.activation(vc[:, :], ps[0:NC, 4, 0:P], ACT.Copy).then_inc(copied, 1)

        q = sb(ctx, nc, "q_heads", [P, 2, TP])
        rfull = sb(ctx, nc, "bias_full", [P, 2, 2, TP])
        rwin = sb(ctx, nc, "bias_win", [P, 2, 2, 640])
        WOFF, COFF, SW = TP, TP + 640, TP + 640 + 32
        SLOTS = 3
        s_ = sb(ctx, nc, "probs", [P, SLOTS, SW])
        page_ring = sb(ctx, nc, "page_ring", [P, SETS, 2, PER, PAGE])
        weighted = sb(ctx, nc, "pages_weighted", [P, SETS, 2, PER * PAGE])
        mx, negm, sums, scale = (sb(ctx, nc, "nsa_" + n, [P, SLOTS, 3]) for n in ("max", "negmax", "sums", "scale"))
        idle = sb(ctx, nc, "idle", [1, 1])
        pt = sb(ctx, nc, "probs_t", [P, 2, 4, P])
        ps = banks(ctx, nc, "nsa_psum", 8)
        flat = ps.ap().rearrange("p b c -> p (b c)")
        sem = phase_semaphores(ctx, nc, "nsa_")
        loads = [sem("loads0"), sem("loads1")]
        (scores_mm, biased, negm_ready, exp_ready, chain, probs_ready, pt_mm, pt_out, pv_mm, o_out) = (sem(s) for s in (
            "scores_mm", "biased", "negm_ready", "exp_ready", "chain", "probs_ready", "pt_mm", "pt_out", "pv_mm", "o_out"))
        pages_in = [sem("pages_in0"), sem("pages_in1")]
        pages_weighted, pages_summed = sem("pages_weighted"), sem("pages_summed")
        block = ctx.enter_context(nc.Block())

        items = [(tt, g) for tt in range(NT) for g in range(2)]

        def sizes(tt):
            return P * (tt + 1), P * min(tt + 1, 5), 4 * (tt + 1)

        def groups(tt):
            blocks = [("slc", b * P, b) for b in range(tt + 1)]
            blocks += [("win", WOFF + j * P, max(0, tt - 4) + j) for j in range(min(tt + 1, 5))]
            return [blocks[i:i + 4] for i in range(0, len(blocks), 4)] + [[("cmp", COFF, 0)]]

        first_group, NG = [], 0
        for tt, g in items:
            first_group.append(NG)
            NG += len(groups(tt))
        NI = len(items)

        def head_loop(eng, body):
            with eng.Fori(0, 2) as i:
                for s in range(2):
                    body(i * 2 + s, s, i)

        @block.gpsimd
        def _(pool):
            pool.sem_inc(pages_weighted, 2)
            with pool.Fori(0, 2 * NI // SETS) as i:
                for s in range(SETS):
                    pool.wait_ge(pages_in[s], i * (16 * PER) + 16 * PER)
                    pool.wait_ge(pages_summed, i * SETS + (s + 1))
                    for x in range(2):
                        last = nc.gpsimd.tensor_tensor(
                            weighted[:, s, x, :].rearrange("p (b l) -> p b l", l=L_CMP),
                            page_ring[:, s, x, :, :].rearrange("p k n -> p (k n)").rearrange("p (b l) -> p b l", l=L_CMP),
                            wpos[:, x, :].unsqueeze(1).to_broadcast([P, SB, L_CMP]), ALU.mult)
                    last.then_inc(pages_weighted, 1)

        @block.sync
        def _(sp):
            def body(r, slot, i2):
                sp.wait_ge(o_out, i2 * (NI * (1 + slot)) + 1)
                sp.dma_start(q[:, slot, :], u[bass.DynSlice(r + T_Q, 1), :, 0:TP].rearrange("a p n -> (a p) n")).then_inc(loads[slot], 16)
                for g in range(2):
                    for dst, off, n in ((rfull[:, slot, g, :], 0, TP), (rwin[:, slot, g, :], TP, 640)):
                        sp.dma_start(dst, toeplitz[bass.DynSlice(r + g * GQ, 1), :, off:off + n].rearrange("a p n -> (a p) n")
                                     ).then_inc(loads[slot], 16)
                for j in range(NI // 2):
                    sp.wait_ge(pages_weighted, r * (NI // 2) + (j + 1))
                    for k in range(PER):
                        page = sp.value_load(pages[0:1, bass.DynSlice(r * (NI // 2 * PER) + (j * PER + k), 1)],
                                             min_val=0, max_val=N_POOL - 1)
                        sp.dma_start(page_ring[:, j % 2, :, k, :],
                                     t["cache_cmp"][bass.DynSlice(page, 1), :, :].rearrange("a p (x n) -> (a p) x n", x=2)
                                     ).then_inc(pages_in[j % 2], 16)
            head_loop(sp, body)

        @block.tensor
        def _(pe):
            mm = nc.tensor.matmul
            pe.sem_inc(pv_mm, 1)

            def scores(r, slot, i):
                tt, g = items[i]
                nk, nw, ncmp = sizes(tt)
                if i == 0:
                    pe.wait_ge(loads[slot], (r - slot) * 40 + 80)
                pe.wait_ge(biased, r * NI + (i + 1))
                rowsg = slice(g * DH, (g + 1) * DH)
                qt = q[rowsg, slot, tt * P:(tt + 1) * P]
                for c in range(0, nk, BANK):
                    w = min(BANK, nk - c)
                    mm(flat[:, c:c + w], qt, kvp[rowsg, KV_KSLC, c:c + w], start=True, stop=True)
                k0 = max(0, tt - 4) * P
                for c in range(0, nw, BANK):
                    w = min(BANK, nw - c)
                    mm(flat[:, WOFF + c:WOFF + c + w], qt, kvp[rowsg, KV_KWIN, k0 + c:k0 + c + w], start=True, stop=True)
                mm(flat[:, COFF:COFF + ncmp], qt, kc[rowsg, 0:ncmp], start=True, stop=True).then_inc(scores_mm, 1)

            def tail(r, slot, i):
                tt, g = items[i]
                nk, nw, ncmp = sizes(tt)
                gs = groups(tt)
                pe.wait_ge(probs_ready, r * NI + (i + 1))
                pe.wait_ge(o_out, r * NI + max(i, 1))
                done = 0
                for k in range(len(gs) + 1):
                    G = first_group[i] + k
                    if k < len(gs):
                        pe.wait_ge(pt_out, r * NG + max(G, 1))
                        for j, (kind, col, vb) in enumerate(gs[k]):
                            w = ncmp if kind == "cmp" else P
                            last = nc.tensor.transpose(ps[0:w, 4 + G % 2, j * P:(j + 1) * P], s_[:, i % SLOTS, col:col + w], ident[:, :])
                        last.then_inc(pt_mm, 1)
                    if k >= 1:
                        pe.wait_ge(pt_out, r * NG + (G + 1))
                        for j, (kind, col, vb) in enumerate(gs[k - 1]):
                            w = ncmp if kind == "cmp" else P
                            v = vc[0:w, :] if kind == "cmp" else vtok[:, 0 if kind == "slc" else 1, vb, :]
                            last = mm(ps[:, 6 + i % 2, 0:P], v, pt[0:w, (G - 1) % 2, j, :], start=done == 0, stop=kind == "cmp")
                            done += 1
                        last.then_inc(pv_mm, 1)

            def body(r, slot, i2):
                scores(r, slot, 0)
                scores(r, slot, 1)
                for i in range(2, NI):
                    scores(r, slot, i)
                    tail(r, slot, i - 2)
                tail(r, slot, NI - 2)
                tail(r, slot, NI - 1)
            head_loop(pe, body)

        @block.vector
        def _(dve):
            V = nc.vector
            dve.sem_inc(biased, 1)
            dve.sem_inc(pages_summed, 2)

            def biases(r, slot, i):
                tt, g = items[i]
                nk, nw, ncmp = sizes(tt)
                if i == 0:
                    dve.wait_ge(loads[slot], (r - slot) * 40 + 80)
                dve.wait_ge(scores_mm, r * NI + (i + 1))
                if i >= SLOTS:
                    dve.wait_ge(pv_mm, r * NG + (first_group[i - SLOTS + 1] + 1))
                p = i % SLOTS
                V.memset(idle[:, :], 0.0)
                V.tensor_tensor_reduce(s_[:, p, 0:nk], flat[:, 0:nk], rfull[:, slot, g, 896 - P * tt:896 - P * tt + nk],
                                       1.0, NEG * 3, ALU.add, ALU.max, mx[:, p, 1:2])
                w0 = 512 - P * min(tt, 4)
                V.tensor_tensor_reduce(s_[:, p, WOFF:WOFF + nw], flat[:, WOFF:WOFF + nw], rwin[:, slot, g, w0:w0 + nw],
                                       1.0, NEG * 3, ALU.add, ALU.max, mx[:, p, 2:3])
                c0 = L_CMP - 1 + 896 - P * tt
                V.tensor_tensor_reduce(s_[:, p, COFF:COFF + ncmp], flat[:, COFF:COFF + ncmp],
                                       rfull[:, slot, g, c0:c0 + L_CMP * (ncmp - 1) + 1:L_CMP],
                                       1.0, NEG * 3, ALU.add, ALU.max, mx[:, p, 0:1]).then_inc(biased, 1)
                dve.wait_ge(biased, r * NI + (i + 2))
                V.tensor_scalar(negm[:, p, :], mx[:, p, :], 0.1 * NEG, -1.0, ALU.max, ALU.mult).then_inc(negm_ready, 1)

            def scales(r, slot, i):
                tt, g = items[i]
                nk, nw, ncmp = sizes(tt)
                p = i % SLOTS
                dve.wait_ge(exp_ready, r * NI + (i + 1))
                V.tensor_scalar(scale[:, p, :], sums[:, p, :], 1e-30, None, ALU.max).then_inc(chain, 1)
                dve.wait_ge(chain, r * 3 * NI + 3 * i + 1)
                V.reciprocal(scale[:, p, :], scale[:, p, :]).then_inc(chain, 1)
                dve.wait_ge(chain, r * 3 * NI + 3 * i + 2)
                gates = by_token[:, tt, bass.DynSlice(r + (8 + g * GQ), 3, 8)]
                V.tensor_tensor(scale[:, p, :], scale[:, p, :], gates, ALU.mult).then_inc(chain, 1)
                dve.wait_ge(chain, r * 3 * NI + 3 * i + 3)
                V.tensor_scalar(s_[:, p, 0:nk], s_[:, p, 0:nk], scale[:, p, 1:2], None, ALU.mult)
                V.tensor_scalar(s_[:, p, WOFF:WOFF + nw], s_[:, p, WOFF:WOFF + nw], scale[:, p, 2:3], None, ALU.mult)
                V.tensor_scalar(s_[:, p, COFF:COFF + ncmp], s_[:, p, COFF:COFF + ncmp], scale[:, p, 0:1], None, ALU.mult
                                ).then_inc(probs_ready, 1)

            def sum_pages(r, j):
                dve.wait_ge(pages_weighted, r * (NI // 2) + (j + 3))
                for x, dst in enumerate((kct_past, vct_past)):
                    last = V.tensor_reduce(dst[:, bass.DynSlice(r * (NI // 2 * SB) + j * SB, SB)],
                                           weighted[:, j % 2, x, :].rearrange("p (b l) -> p b l", l=L_CMP), AX_X, ALU.add)
                last.then_inc(pages_summed, 1)

            def body(r, slot, i2):
                biases(r, slot, 0)
                for i in range(1, NI):
                    biases(r, slot, i)
                    scales(r, slot, i - 1)
                    if i % 2:
                        sum_pages(r, i // 2)
                scales(r, slot, NI - 1)
            head_loop(dve, body)

        @block.scalar
        def _(act):
            act.sem_inc(o_out, 1)
            act.sem_inc(pt_out, 1)

            def exps(r, i):
                tt, g = items[i]
                nk, nw, ncmp = sizes(tt)
                p = i % SLOTS
                act.wait_ge(negm_ready, r * NI + (i + 1))
                for x, col, n in ((1, 0, nk), (2, WOFF, nw), (0, COFF, ncmp)):
                    last = act.activation(s_[:, p, col:col + n], s_[:, p, col:col + n], ACT.Exp, bias=negm[:, p, x:x + 1],
                                          accum_out=sums[:, p, x:x + 1])
                    if x:
                        yield
                last.then_inc(exp_ready, 1)
                yield

            def copies(r, i, exp_parts=iter(())):
                next(exp_parts, None)
                tt, g = items[i]
                ncmp = sizes(tt)[2]
                for k, group in enumerate(groups(tt)):
                    G = first_group[i] + k
                    act.wait_ge(pt_mm, r * NG + (G + 1))
                    act.wait_ge(pv_mm, r * NG + max(G, 1))
                    w, n = (ncmp, P) if group[0][0] == "cmp" else (P, P * len(group))
                    act.activation(pt[0:w, G % 2, :, :].rearrange("p a b -> p (a b)")[:, 0:n], ps[0:w, 4 + G % 2, 0:n], ACT.Copy).then_inc(pt_out, 1)
                    next(exp_parts, None)
                for _ in exp_parts:
                    pass
                act.wait_ge(pv_mm, r * NG + (first_group[i] + len(groups(tt)) + 1))
                half = slice(g * DH, (g + 1) * DH)
                act.activation(out[half, bass.DynSlice(r, 1), tt * P:(tt + 1) * P].rearrange("p a n -> p (a n)"),
                               ps[half, 6 + i % 2, 0:P], ACT.Copy).then_inc(o_out, 1)

            def body(r, slot, i2):
                for _ in exps(r, 0):
                    pass
                for i in range(2, NI + 1):
                    copies(r, i - 2, exps(r, i - 1))
                copies(r, NI - 1)
            head_loop(act, body)
def sparse_sample(nc, t, u, kv, pages, kct, vct, rb, ident, by_token, gate_rows, out):
    HB, SETS = NB // 2, 2
    NBLK = N_PAGES * PAGE // L_SEL + 1
    NCMP, NW, NX = PAST // L_CMP, WINDOW + TS, TS
    C_CMP, C_WIN, C_DIFF, C_FAR = 0, NCMP, NCMP + NW, NCMP + NW + PAGE + TS
    NBIAS = C_FAR + 1
    NT_ALL = N_PAGES + 4 + 1
    with ExitStack() as ctx:
        S = lambda nm, shape: sb(ctx, nc, "ss_" + nm, shape)
        hot, rbx, bias = S("hot", [N_BUCKETS + 1, TS, NBIAS]), S("rbx", [N_BUCKETS + 1, TS, P]), S("bias", [P, NBIAS])
        qs, kvs = S("q", [P, GQ, NB * TS]), S("kv_new", [P, 6, NB * TS])
        same, forced, lower = S("same", [P, P]), S("forced", [P, NBLK]), S("lower", [P, NBLK, NBLK])
        gates = S("gates", [P, 2, 3])
        qp = S("q_padded", [P, HB, P])
        kvn, vcth, vc, vn = S("kvn", [P, 6, HB * TS]), S("vcth", [P, HB * P]), S("vc", [P, HB, P]), S("vn", [TS, 2, HB, P])
        kwin, vwin = S("kwin", [P, HB, WINDOW]), S("vwin", [P, HB, 4, P])
        kring, vring = S("kring", [P, SETS, HB, 4 * PAGE]), S("vring", [P, SETS, 16, P])
        sc, sw, ss = S("s_cmp", [P, NCMP]), S("s_win", [P, NW]), S("s_slc", [P, NBLK * NBLK])
        gtm = ss[:, :].rearrange("p (a b) -> p a b", a=NBLK)
        score, cnt, addm = S("score", [P, NBLK]), S("cnt", [P, NBLK]), S("addm", [P, NBLK])
        mx, negm, sums, scale = S("max", [P, 3]), S("negm", [P, 3]), S("sums", [P, 3]), S("scale", [P, 3])
        pt, ptx = S("pt", [P, NT_ALL, P]), S("ptx", [TS, 2, P])
        eqm = pt[:, :, :].rearrange("p a b -> p (a b)")[:, 0:NBLK * NBLK].rearrange("p (a b) -> p a b", a=NBLK)
        ps = banks(ctx, nc, "ss_psum", 8)
        B_CMP, B_WIN, B_X, B_S, B_T, B_O = 0, 1, 2, 3, 5, 7
        sem = phase_semaphores(ctx, nc, "ss_")
        (consts_in, gates_out, gates_in, rbx_ready, bias_mm, bias_ready, win_in, staged, turn_mm, turned, q_ready,
         c_mm, c_negm, c_exp, pc_ready, imp_mm, w_mm, w_negm, w_exp, s_mm, s_ev, s_negm, s_exp, probs_ready,
         pt_mm, pt_out, b_done, o_out, chain) = (sem(s) for s in (
            "consts_in", "gates_out", "gates_in", "rbx_ready", "bias_mm", "bias_ready", "win_in", "staged", "turn_mm",
            "turned", "q_ready", "c_mm", "c_negm", "c_exp", "pc_ready", "imp_mm", "w_mm", "w_negm", "w_exp", "s_mm",
            "s_ev", "s_negm", "s_exp", "probs_ready", "pt_mm", "pt_out", "b_done", "o_out", "chain"))
        k_in = [sem("k_in0"), sem("k_in1")]
        v_in = [sem("v_in0"), sem("v_in1")]
        k_in_pool = [sem("k_in_pool0"), sem("k_in_pool1")]
        v_in_pool = [sem("v_in_pool0"), sem("v_in_pool1")]
        v_used = sem("v_used")
        block = ctx.enter_context(nc.Block())
        CHUNK = N_PAGES // 4
        NG = 11
        GROUPS = [[(sc, 0, NT_ALL - 1)], [(sw, j * P, N_PAGES + j) for j in range(4)]]
        GROUPS += [[(ss, (4 * c + j) * P, 4 * c + j) for j in range(4)] for c in range(8)]

        def page(eng, index, dst, src, landed):
            n = eng.value_load(pages[0:1, bass.DynSlice(index, 1)], min_val=0, max_val=N_POOL - 1)
            eng.dma_start(dst, src[bass.DynSlice(n, 1), :, :].rearrange("a p n -> (a p) n")).then_inc(landed, 16)

        PLACES = (range(0, 6), range(6, 11), range(11, 16))

        def load_keys(eng, hf, places, landed):
            with eng.Fori(0, CHUNK // 2) as i:
                for s in range(SETS):
                    eng.wait_ge(s_mm, hf * CHUNK + i * 2 + (s + 1))
                    for b, k in ((x // 4, x % 4) for x in places):
                        page(eng, hf * (HB * N_PAGES) + i * 8 + (b * N_PAGES + s * 4 + k),
                             kring[:, s, b, k * PAGE:(k + 1) * PAGE], t["cache_kslc"], landed[s])

        def load_values(eng, hf, places, landed):
            with eng.Fori(0, HB) as b:
                for s in range(SETS):
                    eng.wait_ge(v_used, hf * (2 * HB) + b * 2 + (s + 1))
                    for k in places:
                        page(eng, hf * (HB * N_PAGES) + b * N_PAGES + (s * 16 + k), vring[:, s, k, :], t["cache_vslc"], landed[s])

        def wait_pages(eng, landed, sets_before):
            n = len(PLACES[2])
            eng.wait_ge(landed[0], sets_before * (16 * (16 - n)) + 16 * (16 - n))
            eng.wait_ge(landed[1], sets_before * (16 * n) + 16 * n)

        @block.gpsimd
        def _(pool):
            with pool.Fori(0, 2) as hf:
                load_keys(pool, hf, PLACES[2], k_in_pool)
                load_values(pool, hf, PLACES[2], v_in_pool)

        @block.sync
        def _(sp):
            for b in range(NB):
                sp.dma_start(gate_rows[b * 32:(b + 1) * 32, :].rearrange("(h t) x -> t x h", t=TS),
                             by_token[b * TS:(b + 1) * TS, NT, 8:32].rearrange("t (x h) -> t x h", x=3),
                             allow_slow_non_contiguous=True).then_inc(gates_out, 16)
            loads = [(hot[:, :, :], t["sample_onehot"]), (same[:, :], t["same_query"]),
                     (forced[:, :], t["forced"].partition_broadcast(P)),
                     (lower[:, :, :].rearrange("p a b -> p (a b)"), t["lower"].partition_broadcast(P)),
                     (qs[:, :, :], u[T_Q:T_Q + GQ, :, TP:W].rearrange("r p n -> p r n")),
                     (kvs[:, :, :], kv[:, :, TP:W].rearrange("k p n -> p k n"))]
            for dst, src in loads:
                sp.dma_start(dst, src).then_inc(consts_in, 16)
            sp.wait_ge(gates_out, 16 * NB)
            sp.dma_start(gates[:, :, :], gate_rows.rearrange("(a p) x -> p a x", p=P)).then_inc(gates_in, 16)
            with sp.Fori(0, 2) as hf:
                sp.wait_ge(b_done, hf * HB + 1)
                sp.dma_start(kwin[:, :, :], t["cache_kwin"][bass.DynSlice(hf * HB, HB), :, :].rearrange("b p n -> p b n")
                             ).then_inc(win_in, 16)
                sp.dma_start(vwin[:, :, :, :].rearrange("p b j n -> p b (j n)"),
                             t["cache_vwin"][bass.DynSlice(hf * HB, HB), :, :].rearrange("b p n -> p b n")).then_inc(win_in, 16)
                load_keys(sp, hf, PLACES[0], k_in)
                load_values(sp, hf, PLACES[0], v_in)

        @block.tensor
        def _(pe):
            mm, tr = nc.tensor.matmul, nc.tensor.transpose
            pe.sem_inc(s_mm, 2)
            pe.sem_inc(v_used, 2)
            pe.sem_inc(b_done, 1)
            pe.wait_ge(rbx_ready, 1)
            for c0, c1, b in ((0, BANK, 0), (BANK, NBIAS, 1)):
                for tt in range(TS):
                    last = mm(ps[:, b, 0:c1 - c0], rbx[:, tt, :], hot[:, tt, c0:c1], start=tt == 0, stop=tt == TS - 1)
            last.then_inc(bias_mm, 1)
            pe.wait_ge(bias_ready, 1)
            with pe.Fori(0, 2) as hf:
                pe.wait_ge(staged, hf + 1)
                for b in range(HB):
                    tr(ps[:, B_T, b * P:(b + 1) * P], vcth[:, b * P:(b + 1) * P], ident[:, :])
                for b in range(HB):
                    tr(ps[0:TS, B_T + 1, b * P:(b + 1) * P], kvn[:, KV_VSLC, b * TS:(b + 1) * TS], ident[:, :])
                for b in range(HB):
                    last = tr(ps[0:TS, B_S, b * P:(b + 1) * P], kvn[:, KV_VWIN, b * TS:(b + 1) * TS], ident[:, :])
                last.then_inc(turn_mm, 1)
                pe.wait_ge(q_ready, hf + 1)
                for b in range(HB):
                    last = mm(ps[:, B_CMP, 0:NCMP], qp[:, b, :], kct[:, bass.DynSlice(hf * (HB * NCMP) + b * NCMP, NCMP)],
                              start=b == 0, stop=b == HB - 1)
                last.then_inc(c_mm, 1)
                pe.wait_ge(win_in, hf * 32 + 32)
                for b in range(HB):
                    mm(ps[:, B_WIN, :], qp[:, b, :], kwin[:, b, :], start=b == 0, stop=b == HB - 1)
                for j, kind in enumerate((KV_KWIN, KV_KSLC)):
                    for b in range(HB):
                        last = mm(ps[:, B_X, j * TS:(j + 1) * TS], qp[:, b, :], kvn[:, kind, b * TS:(b + 1) * TS],
                                  start=b == 0, stop=b == HB - 1)
                last.then_inc(w_mm, 1)
                pe.wait_ge(turned, hf + 1)
                pe.wait_ge(pc_ready, hf + 1)
                mm(ps[:, B_CMP, NCMP:2 * NCMP], same[:, :], sc[:, :], start=True, stop=True).then_inc(imp_mm, 1)
                with pe.Fori(0, CHUNK // 2) as i:
                    for s in range(SETS):
                        wait_pages(pe, (k_in[s], k_in_pool[s]), hf * (CHUNK // 2) + i)
                        pe.wait_ge(s_ev, hf * CHUNK + i * 2 + (s + 1))
                        for b in range(HB):
                            last = mm(ps[:, B_S + s, :], qp[:, b, :], kring[:, s, b, :], start=b == 0, stop=b == HB - 1)
                        last.then_inc(s_mm, 1)
                for k, group in enumerate(GROUPS):
                    pe.wait_ge(probs_ready, hf * 3 + min(k + 1, 3))
                    pe.wait_ge(pt_out, hf * NG + max(k, 1))
                    for j, (src, col, to) in enumerate(group):
                        last = tr(ps[:, B_T + k % 2, j * P:(j + 1) * P], src[:, col:col + P], ident[:, :])
                    last.then_inc(pt_mm, 1)
                pe.wait_ge(pt_out, hf * NG + NG - 1)
                tr(ps[0:TS, B_T, 0:P], sw[:, WINDOW:WINDOW + TS], ident[:, :])
                tr(ps[0:TS, B_T, P:2 * P], ss[:, PAST:PAST + TS], ident[:, :]).then_inc(pt_mm, 1)
                pe.wait_ge(pt_out, hf * NG + NG + 1)
                for b in range(HB):
                    o = ps[:, B_O, b * 32:(b + 1) * 32]
                    cols = slice(b * 32, (b + 1) * 32)
                    mm(o, vc[:, b, :], pt[:, NT_ALL - 1, cols], start=True, stop=False)
                    for j in range(4):
                        mm(o, vwin[:, b, j, :], pt[:, N_PAGES + j, cols], start=False, stop=False)
                    mm(o, vn[:, 1, b, :], ptx[:, 0, cols], start=False, stop=False)
                    mm(o, vn[:, 0, b, :], ptx[:, 1, cols], start=False, stop=False)
                    for s in range(SETS):
                        wait_pages(pe, (v_in[s], v_in_pool[s]), hf * HB + b)
                        for k in range(16):
                            last = mm(o, vring[:, s, k, :], pt[:, s * 16 + k, cols], start=False, stop=s == 1 and k == 15)
                        last.then_inc(v_used, 1)
                pe.wait_ge(v_used, hf * (2 * HB) + 2 * HB + 2)
                pe.sem_inc(b_done, HB)

        @block.scalar
        def _(act):
            act.sem_inc(pt_out, 1)
            act.wait_ge(bias_mm, 1)
            act.activation(bias[:, :], ps[:, 0:2, :].rearrange("p a b -> p (a b)")[:, 0:NBIAS], ACT.Copy).then_inc(bias_ready, 1)
            act.wait_ge(consts_in, 16 * 6)
            with act.Fori(0, 2) as hf:
                act.activation(kvn[:, :, :], kvs[:, :, bass.DynSlice(hf * (HB * TS), HB * TS)], ACT.Copy)
                act.activation(vcth[:, :], vct[:, bass.DynSlice(hf * (HB * P), HB * P)], ACT.Copy).then_inc(staged, 1)
                act.wait_ge(turn_mm, hf + 1)
                act.activation(vc[:, :, :], ps[:, B_T, :].rearrange("p (b n) -> p b n", b=HB), ACT.Copy)
                act.activation(vn[:, 0, :, :], ps[0:TS, B_T + 1, :].rearrange("p (b n) -> p b n", b=HB), ACT.Copy)
                act.activation(vn[:, 1, :, :], ps[0:TS, B_S, :].rearrange("p (b n) -> p b n", b=HB), ACT.Copy).then_inc(turned, 1)
                for x, (ready, done, src) in enumerate(((c_negm, c_exp, sc[:, :]), (w_negm, w_exp, sw[:, :]), (s_negm, s_exp, ss[:, 0:PAST + TS]))):
                    if x == 2:
                        load_keys(act, hf, PLACES[1], k_in)
                    act.wait_ge(ready, hf + 1)
                    act.activation(src, src, ACT.Exp, bias=negm[:, x:x + 1], accum_out=sums[:, x:x + 1]).then_inc(done, 1)
                for k, group in enumerate(GROUPS):
                    act.wait_ge(pt_mm, hf * NG + (k + 1))
                    n, to = len(group), group[0][2]
                    act.activation(pt[:, to:to + n, :].rearrange("p a b -> p (a b)"), ps[:, B_T + k % 2, 0:n * P], ACT.Copy).then_inc(pt_out, 1)
                act.wait_ge(pt_mm, hf * NG + NG)
                act.activation(ptx[:, :, :].rearrange("p a b -> p (a b)"), ps[0:TS, B_T, 0:2 * P], ACT.Copy).then_inc(pt_out, 1)
                load_values(act, hf, PLACES[1], v_in)
                act.wait_ge(b_done, hf * HB + HB + 1)
                for g in range(2):
                    half = slice(g * DH, (g + 1) * DH)
                    dst = out[half, :, bass.DynSlice(hf * (HB * TS) + TP, HB * TS)].rearrange("p r (b t) -> p b r t", b=HB)
                    src = ps[half, B_O, 0:HB * 32].rearrange("p (b g r t) -> p b g r t", g=2, r=GQ, t=TS)[:, :, g]
                    for b in range(HB):
                        last = act.activation(dst[:, b], src[:, b], ACT.Copy)
                last.then_inc(o_out, 1)
                act.wait_ge(o_out, hf + 1)

        @block.vector
        def _(dve):
            V = nc.vector
            V.memset(rbx[:, :, :], 0.0).then_inc(chain, 1)
            V.memset(qp[:, :, :], 0.0).then_inc(chain, 1)
            dve.wait_ge(chain, 2)
            for tt in range(TS):
                last = V.tensor_copy(rbx[:, tt, :].rearrange("k (b h t) -> k b h t", b=HB, t=TS)[:, :, :, tt],
                                     rb[:, :].unsqueeze(1).to_broadcast([N_BUCKETS + 1, HB, NSA_HEADS]))
            dve.wait_ge(consts_in, 16 * 6)
            last = V.tensor_copy(score[:, :], forced[:, :]).then_inc(rbx_ready, 1)
            dve.wait_ge(gates_in, 16)
            dve.wait_ge(bias_ready, 1)
            dve.sem_inc(s_ev, 2)
            L = 20
            with dve.Fori(0, 2) as hf:
                n_link = [0]

                def link(ins):
                    n_link[0] += 1
                    ins.then_inc(chain, 1)
                    dve.wait_ge(chain, hf * L + (2 + n_link[0]))

                dve.wait_ge(b_done, hf * HB + 1)
                for b in range(HB):
                    for g in range(2):
                        half = slice(g * DH, (g + 1) * DH)
                        last = V.tensor_copy(qp[half, b, b * 32 + g * 16:b * 32 + (g + 1) * 16].rearrange("p (r t) -> p r t", t=TS),
                                             qs[half, :, bass.DynSlice(hf * (HB * TS) + b * TS, TS)])
                last.then_inc(q_ready, 1)
                dve.wait_ge(c_mm, hf + 1)
                link(V.tensor_tensor(sc[:, :], ps[:, B_CMP, 0:NCMP], bias[:, C_CMP:C_CMP + NCMP], ALU.add))
                link(V.tensor_reduce(mx[:, 0:1], sc[:, :], AX_X, ALU.max))
                V.tensor_scalar(negm[:, 0:1], mx[:, 0:1], -1.0, None, ALU.mult).then_inc(c_negm, 1)
                dve.wait_ge(w_mm, hf + 1)
                V.tensor_tensor(sw[:, 0:WINDOW], ps[:, B_WIN, :], bias[:, C_WIN:C_WIN + WINDOW], ALU.add)
                link(V.tensor_tensor(sw[:, WINDOW:NW], ps[:, B_X, 0:TS], bias[:, C_WIN + WINDOW:C_WIN + NW], ALU.add))
                link(V.tensor_reduce(mx[:, 1:2], sw[:, :], AX_X, ALU.max))
                V.tensor_scalar(negm[:, 1:2], mx[:, 1:2], -1.0, None, ALU.mult).then_inc(w_negm, 1)
                dve.wait_ge(c_exp, hf + 1)
                link(V.reciprocal(scale[:, 0:1], sums[:, 0:1]))
                V.tensor_scalar(sc[:, :], sc[:, :], scale[:, 0:1], None, ALU.mult).then_inc(pc_ready, 1)
                dve.wait_ge(imp_mm, hf + 1)
                link(V.tensor_reduce(score[:, 0:NBLK - 1], ps[:, B_CMP, NCMP:2 * NCMP].rearrange("p (n a) -> p n a", a=2), AX_X, ALU.add))
                link(V.tensor_tensor(score[:, 0:NBLK - 1], score[:, 0:NBLK - 1], forced[:, 0:NBLK - 1], ALU.add))
                col = score[:, :].unsqueeze(2).to_broadcast([P, NBLK, NBLK])
                row = score[:, :].unsqueeze(1).to_broadcast([P, NBLK, NBLK])
                V.tensor_tensor(gtm, row, col, ALU.is_gt)
                link(V.tensor_tensor(eqm, row, col, ALU.is_equal))
                link(V.tensor_tensor(eqm, eqm, lower[:, :, :], ALU.mult))
                link(V.tensor_tensor(gtm, gtm, eqm, ALU.add))
                link(V.tensor_reduce(cnt[:, :], gtm, AX_X, ALU.add))
                link(V.tensor_scalar(addm[:, :], cnt[:, :], N_SEL - 0.5, NEG, ALU.is_ge, ALU.mult))
                link(V.tensor_scalar(addm[:, :], addm[:, :], bias[:, C_FAR:C_FAR + 1], None, ALU.add))
                V.tensor_scalar(sc[:, :], sc[:, :], gates[:, bass.DynSlice(hf, 1), 0:1].rearrange("p a b -> p (a b)"), None, ALU.mult).then_inc(probs_ready, 1)
                dve.wait_ge(w_exp, hf + 1)
                link(V.reciprocal(scale[:, 1:2], sums[:, 1:2]))
                link(V.tensor_tensor(scale[:, 1:2], scale[:, 1:2], gates[:, bass.DynSlice(hf, 1), 1 + 1:3].rearrange("p a b -> p (a b)"), ALU.mult))
                V.tensor_scalar(sw[:, :], sw[:, :], scale[:, 1:2], None, ALU.mult).then_inc(probs_ready, 1)
                with dve.Fori(0, CHUNK // 2) as i:
                    for s in range(SETS):
                        dve.wait_ge(s_mm, hf * CHUNK + i * 2 + (s + 3))
                        V.tensor_tensor(ss[:, bass.DynSlice(i * 1024 + s * BANK, BANK)].rearrange("p (n l) -> p n l", l=L_SEL),
                                        ps[:, B_S + s, :].rearrange("p (n l) -> p n l", l=L_SEL),
                                        addm[:, bass.DynSlice(i * 16 + s * 8, 8)].unsqueeze(2).to_broadcast([P, 8, L_SEL]),
                                        ALU.add).then_inc(s_ev, 1)
                dve.wait_ge(s_ev, hf * CHUNK + (CHUNK + 2))
                link(V.tensor_scalar(ss[:, PAST:PAST + TS], ps[:, B_X, TS:2 * TS], addm[:, NBLK - 1:NBLK], None, ALU.add))
                near = ss[:, PAST - PAGE:PAST + TS]
                link(V.tensor_tensor(near, near, bias[:, C_DIFF:C_FAR], ALU.add))
                link(V.tensor_reduce(mx[:, 2:3], ss[:, 0:PAST + TS], AX_X, ALU.max))
                V.tensor_scalar(negm[:, 2:3], mx[:, 2:3], -1.0, None, ALU.mult).then_inc(s_negm, 1)
                dve.wait_ge(s_exp, hf + 1)
                link(V.reciprocal(scale[:, 2:3], sums[:, 2:3]))
                link(V.tensor_tensor(scale[:, 2:3], scale[:, 2:3], gates[:, bass.DynSlice(hf, 1), 1:2].rearrange("p a b -> p (a b)"), ALU.mult))
                V.tensor_scalar(ss[:, 0:PAST + TS], ss[:, 0:PAST + TS], scale[:, 2:3], None, ALU.mult).then_inc(probs_ready, 1)
                assert n_link[0] == L, n_link[0]


def cross_prompt(nc, xq, mem, ident, out):
    KC = XD // P
    MC = N_MEM // P
    NI = NT
    with ExitStack() as ctx:
        S = lambda nm, shape: sb(ctx, nc, "xp_" + nm, shape)
        q, kt, vt = S("q", [P, 2, KC, TP]), S("kt", [P, 2, KC, N_MEM]), S("vt", [P, 2, KC, N_MEM])
        v = S("v", [P, 2, MC, XD])
        SLOTS = 3
        s_, pt = S("probs", [P, SLOTS, N_MEM]), S("pt", [P, 2, MC, P])
        mx, negm, sums, scale = (S(n, [P, SLOTS]) for n in ("max", "negm", "sums", "scale"))
        ps = banks(ctx, nc, "xp_psum", 8)
        B_S, B_T, B_O, B_V = 0, 2, 4, 6
        sem = phase_semaphores(ctx, nc, "xp_")
        loads = [sem("loads0"), sem("loads1")]
        v_mm, v_ready, scores_mm, negm_ready, exp_ready, chain, probs_ready, pt_mm, pt_out, o_mm, o_out = (sem(s) for s in (
            "v_mm", "v_ready", "scores_mm", "negm_ready", "exp_ready", "chain", "probs_ready", "pt_mm", "pt_out", "o_mm", "o_out"))
        block = ctx.enter_context(nc.Block())

        def head_loop(eng, body):
            with eng.Fori(0, XH // 2) as i:
                for s in range(2):
                    body(i * 2 + s, s, i)

        @block.sync
        def _(sp):
            def body(h, slot, i):
                sp.wait_ge(o_out, i * (NI * (1 + slot)) + 1)
                tiles = lambda src, at: src[bass.DynSlice(h * KC + at, KC), :, :].rearrange("c p n -> p c n")
                sp.dma_start(q[:, slot, :, :], tiles(xq, 0)[:, :, 0:TP]).then_inc(loads[slot], 16)
                sp.dma_start(kt[:, slot, :, :], tiles(mem, 0)).then_inc(loads[slot], 16)
                sp.dma_start(vt[:, slot, :, :], tiles(mem, CHUNKS)).then_inc(loads[slot], 16)
            head_loop(sp, body)

        @block.tensor
        def _(pe):
            mm = nc.tensor.matmul
            pe.sem_inc(o_mm, 1)

            def scores(h, slot, i, t):
                if t == 0:
                    pe.wait_ge(loads[slot], i * 48 + 48)
                    for c in range(KC):
                        for m in range(MC):
                            last = nc.tensor.transpose(ps[:, B_V, m * XD + c * P:m * XD + (c + 1) * P],
                                                       vt[:, slot, c, m * P:(m + 1) * P], ident[:, :])
                    last.then_inc(v_mm, 1)
                pe.wait_ge(exp_ready, h * NI + max(t, 1))
                for c in range(KC):
                    last = mm(ps[:, B_S + t % 2, 0:N_MEM], q[:, slot, c, t * P:(t + 1) * P], kt[:, slot, c, :],
                              start=c == 0, stop=c == KC - 1)
                last.then_inc(scores_mm, 1)

            def tail(h, slot, t):
                pe.wait_ge(probs_ready, h * NI + (t + 1))
                for m in range(MC):
                    last = nc.tensor.transpose(ps[:, B_T + t % 2, m * P:(m + 1) * P], s_[:, t % SLOTS, m * P:(m + 1) * P], ident[:, :])
                last.then_inc(pt_mm, 1)
                pe.wait_ge(pt_out, h * NI + (t + 2))
                pe.wait_ge(o_out, h * NI + max(t, 1))
                pe.wait_ge(v_ready, h + 1)
                for c in range(KC):
                    for m in range(MC):
                        last = mm(ps[:, B_O + t % 2, c * P:(c + 1) * P], v[:, slot, m, c * P:(c + 1) * P],
                                  pt[:, t % 2, m, :], start=m == 0, stop=m == MC - 1)
                last.then_inc(o_mm, 1)

            def body(h, slot, i):
                scores(h, slot, i, 0)
                scores(h, slot, i, 1)
                for t in range(2, NI):
                    scores(h, slot, i, t)
                    tail(h, slot, t - 2)
                tail(h, slot, NI - 2)
                tail(h, slot, NI - 1)
            head_loop(pe, body)

        @block.vector
        def _(dve):
            V = nc.vector

            def maxima(h, t):
                p = t % SLOTS
                dve.wait_ge(scores_mm, h * NI + (t + 1))
                V.tensor_reduce(mx[:, p:p + 1], ps[:, B_S + t % 2, 0:N_MEM], AX_X, ALU.max).then_inc(chain, 1)
                dve.wait_ge(chain, h * (2 * NI) + (2 * t + 1) if t == 0 else h * (2 * NI) + 2 * t)
                V.tensor_scalar(negm[:, p:p + 1], mx[:, p:p + 1], -1.0, None, ALU.mult).then_inc(negm_ready, 1)

            def scales(h, t):
                p = t % SLOTS
                dve.wait_ge(exp_ready, h * NI + (t + 2))
                V.reciprocal(scale[:, p:p + 1], sums[:, p:p + 1]).then_inc(chain, 1)
                dve.wait_ge(chain, h * (2 * NI) + (2 * t + 3 if t < NI - 1 else 2 * NI))
                V.tensor_scalar(s_[:, p, :], s_[:, p, :], scale[:, p:p + 1], None, ALU.mult).then_inc(probs_ready, 1)

            def body(h, slot, i):
                maxima(h, 0)
                for t in range(1, NI):
                    maxima(h, t)
                    scales(h, t - 1)
                scales(h, NI - 1)
            head_loop(dve, body)

        @block.scalar
        def _(act):
            for started in (exp_ready, o_out, pt_out):
                act.sem_inc(started, 1)

            def exps(h, t):
                p = t % SLOTS
                act.wait_ge(negm_ready, h * NI + (t + 1))
                act.activation(s_[:, p, :], ps[:, B_S + t % 2, 0:N_MEM], ACT.Exp, bias=negm[:, p:p + 1],
                               accum_out=sums[:, p:p + 1]).then_inc(exp_ready, 1)

            def copies(h, t):
                act.wait_ge(pt_mm, h * NI + (t + 1))
                act.wait_ge(o_mm, h * NI + max(t, 1))
                act.activation(pt[:, t % 2, :, :].rearrange("p a b -> p (a b)"), ps[:, B_T + t % 2, 0:MC * P], ACT.Copy).then_inc(pt_out, 1)
                act.wait_ge(o_mm, h * NI + (t + 2))
                act.activation(out[:, bass.DynSlice(h * KC, KC), t * P:(t + 1) * P],
                               ps[:, B_O + t % 2, 0:KC * P].rearrange("p (c n) -> p c n", c=KC), ACT.Copy).then_inc(o_out, 1)

            def body(h, slot, i):
                exps(h, 0)
                act.wait_ge(v_mm, h + 1)
                act.activation(v[:, slot, :, :].rearrange("p a b -> p (a b)"), ps[:, B_V, :], ACT.Copy).then_inc(v_ready, 1)
                for t in range(2, NI + 1):
                    exps(h, t - 1)
                    copies(h, t - 2)
                copies(h, NI - 1)
            head_loop(act, body)


def cross_sample(nc, t, xq, ident, out):
    R = XH * TS
    MC = N_MEM // P
    MS = 4
    with ExitStack() as ctx:
        S = lambda nm, shape: sb(ctx, nc, "xs_" + nm, shape)
        qs, qb = S("q", [P, CHUNKS, NB * TS]), S("qb", [P, 2, CHUNKS, R])
        kt, v = S("kt", [P, MS, CHUNKS, N_MEM]), S("v", [P, MS, MC, D])
        s_, pt = S("probs", [P, 2, N_MEM]), S("pt", [P, 2, MC, R])
        mx, negm, sums, scale = (S(n, [R, 2]) for n in ("max", "negm", "sums", "scale"))
        ps = banks(ctx, nc, "xs_psum", 6)
        B_S, B_T, B_O = 0, 2, 4
        sem = phase_semaphores(ctx, nc, "xs_")
        loads, q_in = [sem(f"loads{m}") for m in range(MS)], sem("q_in")
        qb_ready, scores_mm, negm_ready, exp_ready, chain, probs_ready, pt_mm, pt_out, o_mm, o_out, zeroed = (sem(s) for s in (
            "qb_ready", "scores_mm", "negm_ready", "exp_ready", "chain", "probs_ready", "pt_mm", "pt_out", "o_mm", "o_out", "zeroed"))
        block = ctx.enter_context(nc.Block())

        def staggered(front, back):
            front(0, 0)
            for b in range(1, NB):
                front(b, b % 2)
                back(b - 1, (b - 1) % 2)
            back(NB - 1, (NB - 1) % 2)

        @block.sync
        def _(sp):
            sp.dma_start(qs[:, :, :], xq[:, :, TP:W].rearrange("c p n -> p c n")).then_inc(q_in, 16)

            for b in range(NB):
                m = b % MS
                if b >= MS:
                    sp.wait_ge(o_mm, b - MS + 1)
                sp.dma_start(kt[:, m, :, :], t["cache_mem_k"][b].rearrange("p (c n) -> p c n", c=CHUNKS)).then_inc(loads[m], 16)
                sp.dma_start(v[:, m, :, :], t["cache_mem_v"][b].rearrange("p (c n) -> p c n", c=MC)).then_inc(loads[m], 16)

        @block.tensor
        def _(pe):
            mm = nc.tensor.matmul

            def scores(b, s):
                pe.wait_ge(loads[b % MS], 32 * (b // MS + 1))
                pe.wait_ge(qb_ready, b + 1)
                for c in range(CHUNKS):
                    last = mm(ps[0:R, B_S + s, 0:N_MEM], qb[:, s, c, :], kt[:, b % MS, c, :], start=c == 0, stop=c == CHUNKS - 1)
                last.then_inc(scores_mm, 1)

            def tail(b, s):
                pe.wait_ge(probs_ready, b + 1)
                for m in range(MC):
                    last = nc.tensor.transpose(ps[:, B_T + s, m * P:(m + 1) * P], s_[:, s, m * P:(m + 1) * P], ident[:, :])
                last.then_inc(pt_mm, 1)
                pe.wait_ge(pt_out, b + 1)
                if b >= 2:
                    pe.wait_ge(o_out, b - 1)
                for c in range(CHUNKS):
                    h = c // (CHUNKS // XH)
                    for m in range(MC):
                        last = mm(ps[:, B_O + s, c * TS:(c + 1) * TS], v[:, b % MS, m, c * P:(c + 1) * P],
                                  pt[:, s, m, h * TS:(h + 1) * TS], start=m == 0, stop=m == MC - 1)
                last.then_inc(o_mm, 1)
            staggered(scores, tail)

        @block.vector
        def _(dve):
            V = nc.vector
            V.memset(qb[:, :, :, :], 0.0).then_inc(zeroed, 1)
            V.memset(s_[:, :, :], 0.0).then_inc(zeroed, 1)
            dve.wait_ge(zeroed, 2)
            dve.wait_ge(q_in, 16)

            def maxima(b, s):
                for h in range(XH):
                    last = V.tensor_copy(qb[:, s, 2 * h:2 * h + 2, h * TS:(h + 1) * TS],
                                         qs[:, 2 * h:2 * h + 2, b * TS:(b + 1) * TS])
                last.then_inc(qb_ready, 1)
                dve.wait_ge(scores_mm, b + 1)
                V.tensor_reduce(mx[:, s:s + 1], ps[0:R, B_S + s, 0:N_MEM], AX_X, ALU.max).then_inc(chain, 1)
                dve.wait_ge(chain, max(1, b * 2))
                V.tensor_scalar(negm[:, s:s + 1], mx[:, s:s + 1], -1.0, None, ALU.mult).then_inc(negm_ready, 1)

            def scales(b, s):
                dve.wait_ge(exp_ready, b + 1)
                V.reciprocal(scale[:, s:s + 1], sums[:, s:s + 1]).then_inc(chain, 1)
                dve.wait_ge(chain, min(2 * NB, b * 2 + 3))
                V.tensor_scalar(s_[0:R, s, :], s_[0:R, s, :], scale[:, s:s + 1], None, ALU.mult).then_inc(probs_ready, 1)
            staggered(maxima, scales)

        @block.scalar
        def _(act):
            def exps(b, s):
                act.wait_ge(negm_ready, b + 1)
                act.activation(s_[0:R, s, :], ps[0:R, B_S + s, 0:N_MEM], ACT.Exp, bias=negm[:, s:s + 1],
                               accum_out=sums[:, s:s + 1]).then_inc(exp_ready, 1)

            def copies(b, s):
                act.wait_ge(pt_mm, b + 1)
                act.activation(pt[:, s, :, :], ps[:, B_T + s, 0:MC * P].rearrange("p (m c) -> p m c", m=MC)[:, :, 0:R], ACT.Copy).then_inc(pt_out, 1)
                act.wait_ge(o_mm, b + 1)
                act.activation(out[:, :, TP + b * TS:TP + (b + 1) * TS],
                               ps[:, B_O + s, 0:CHUNKS * TS].rearrange("p (c n) -> p c n", c=CHUNKS), ACT.Copy).then_inc(o_out, 1)
            staggered(exps, copies)


def window_cache(nc, t, kv, ident, new_win):
    N = NB * TS
    with ExitStack() as ctx:
        new_t = sb(ctx, nc, "win_new_t", [P, 2, N])
        new = sb(ctx, nc, "win_new", [N, 2, P])
        ps = banks(ctx, nc, "win_psum", 1)
        sem = phase_semaphores(ctx, nc, "win_")
        landed, turned, copied, sent = (sem(s) for s in ("landed", "turned", "copied", "sent"))
        block = ctx.enter_context(nc.Block())

        @block.sync
        def _(sp):
            sp.dma_start(new_t[:, :, :], kv[KV_KWIN:KV_VWIN + 1, :, TP:W].rearrange("k p n -> p k n")).then_inc(landed, 16)
            sp.dma_start(new_win[:, 0:WINDOW - TS, :], t["cache_win"][:, TS:WINDOW, :]).then_inc(sent, 16)
            sp.wait_ge(copied, 1)
            for b in range(NB):
                sp.dma_start(new_win[b, WINDOW - TS:WINDOW, :], new[b * TS:(b + 1) * TS, :, :].rearrange("t k c -> t (k c)")
                             ).then_inc(sent, 16)
            sp.wait_ge(sent, 16 * (NB + 1))

        @block.tensor
        def _(pe):
            pe.wait_ge(landed, 16)
            for k in range(2):
                last = nc.tensor.transpose(ps[0:N, 0, k * P:(k + 1) * P], new_t[:, k, :], ident[:, :])
            last.then_inc(turned, 1)

        @block.vector
        def _(dve):
            dve.wait_ge(turned, 1)
            nc.vector.tensor_copy(new[:, :, :].rearrange("t k c -> t (k c)"), ps[0:N, 0, 0:2 * P]).then_inc(copied, 1)


def decoder_layer(nc, t, o):
    dram = lambda name, shape: nc.dram_tensor(name, shape, F32, kind=SCRATCH).ap()
    u = dram("u_scratch", [N_LINEAR + N_GATE, P, W])
    xq = dram("xq_scratch", [CHUNKS, P, W])
    toeplitz = dram("toeplitz", [NSA_HEADS, P, TP + 640])
    kv = o["kv"]
    with ExitStack() as top:
        ones = sb(top, nc, "ones", [P, P])
        ident = sb(top, nc, "ident", [P, P])
        gains = sb(top, nc, "gains", [P, 4, CHUNKS])
        rb = sb(top, nc, "rel_bias", [N_BUCKETS + 1, NSA_HEADS])
        norm_g = sb(top, nc, "norm_g", [P, 1])
        load_all(nc, "constants", [(ones[:, :], t["ones"]), (ident[:, :], t["ident"]), (gains[:, :, :], t["gains"]),
                                   (rb[:, :], t["rel_bias"]), (norm_g[:, :], t["gdn_norm_g"])])

        with ExitStack() as mixers:
            branches = sb(mixers, nc, "branches", [P, 3, 4, W])
            with ExitStack() as ctx:
                h_low, h_high = (sb(ctx, nc, n, [P, CHUNKS, W], F32R) for n in ("h_low", "h_high"))
                with ExitStack() as c2:
                    x = sb(c2, nc, "x_in", [P, CHUNKS, W])
                    sq = sb(c2, nc, "sq", [P, 2, W])
                    load_all(nc, "load_x", [(x[:, c, :], t["x"][c]) for c in range(CHUNKS)])
                    rmsnorm(nc, "norm_mix", x, gains[:, 0, :], ones, h_low, sq, h_high)
                kept = dict(func=ACT.Copy, rhs=(h_high, h_low), dram=u)
                gemm(nc, "w_in", t["w_in"], [
                    (0, T_Q, kept),
                    (T_Q, 4, dict(kept, at=T_Q, scale=DH ** -0.5)),
                    (T_KV, 6, dict(kept, dram=kv)),
                    (T_MISC, 1, dict(kept, at=T_MISC))], CHUNKS, W, finish_copy)
                with ExitStack() as c2:
                    glu_conv = conv_beside(c2, nc, u, t, branches[:, 0], (o["conv_a_p"], o["conv_a_s"]))
                    gemm(nc, "w_gates", t["w_in"], [(T_GATE, N_GATE, dict(kept, at=T_GATE, func=ACT.Sigmoid))],
                         CHUNKS, W, finish_copy, beside=glu_conv)
            conv_norm(nc, t, ones, branches[:, 0])
            by_token = sb(mixers, nc, "by_token", [P, NT + 1, 36])
            window_cache(nc, t, kv, ident, o["win_s"])
            with ExitStack() as ctx:
                qkv = sb(ctx, nc, "qkv", [P, 12, W])
                go = sb(ctx, nc, "gdn_o", [P, GH, W])
                gdn_inputs(nc, u, t, ones, ident, qkv, by_token, (o["conv_qkv_p"], o["conv_qkv_s"]))
                delta_rule(nc, "gdnp", qkv, by_token, ones, ident,
                           dict(tri=t["tri_p"], bound=t["bound_p"], levels=t["levels_p"]), t, P, 7, NT, 0, go, o["gdn_p"])
                delta_rule(nc, "gdns", qkv, by_token, ones, ident,
                           dict(tri=t["tri_s"], bound=t["bound_s"], levels=t["levels_s"],
                                batch_cols=t["batch_cols"], batch_rows=t["batch_rows"]),
                           t, NB * TS, 2, 1, TP, go, o["gdn_s"], batches=NB)
                gate_output(nc, go, u, ones, norm_g[:, 0:1], branches[:, 1])
            bias_rows(nc, t, dram("bias_rows", [NSA_HEADS, LB_FULL + LB_WIN]), toeplitz, rb)
            with ExitStack() as ctx:
                pages = sb(ctx, nc, "pages", [1, NB * N_PAGES], I32)
                kct, vct = (sb(ctx, nc, n, [P, NB * PAST // L_CMP]) for n in ("kct", "vct"))
                load_all(nc, "load_pages", [(pages[:, :], t["page_table"])])
                sparse_prompt(nc, t, u, kv, toeplitz, ident, by_token, branches[:, 2], pages, kct, vct)
                sparse_sample(nc, t, u, kv, pages, kct, vct, rb, ident, by_token, dram("gate_rows", [NB * 32, 3]), branches[:, 2])

            with ExitStack() as ctx:
                mixed = branches[:, :, :, :].rearrange("p i c n -> p (i c) n")[:, 0:CHUNKS, :]
                with ExitStack() as c2:
                    halves = [sb(c2, nc, n, [P, 3, 4, W], F32R) for n in ("branches_high", "branches_low")]
                    split_tiles(nc, "split_branches", [(branches[:, i, c, :],) + tuple(x[:, i, c, :] for x in halves)
                                                       for i in range(3) for c in range(4)])
                    gemm(nc, "w_branch", t["w_branch"], [
                        (8 * i, 8, dict(rhs=[x[:, i] for x in halves], out=mixed, part=i, aux=u, aux_at=T_GATE + 8 * i))
                        for i in range(3)], 4, W, finish_gated, on_vector=True)
                x = sb(top, nc, "x", [P, CHUNKS, W], side="right")
                mix = [sb(ctx, nc, n, [P, CHUNKS, W], F32R) for n in ("mix_high", "mix_low")]
                split_tiles(nc, "split_mix", [(mixed[:, c, :],) + tuple(x[:, c, :] for x in mix) for c in range(CHUNKS)])
                load_all(nc, "reload_x", [(x[:, c, :], t["x"][c]) for c in range(CHUNKS)])
                gemm(nc, "w_o", t["w_o"], [(0, CHUNKS, dict(rhs=mix, out=x))], CHUNKS, W, finish_residual, on_vector=True)

        with ExitStack() as ctx:
            h_low, h_high = (sb(ctx, nc, n, [P, CHUNKS, W], F32R) for n in ("hx_low", "hx_high"))
            mem_split = [sb(ctx, nc, n, [P, CHUNKS, N_MEM], F32R) for n in ("mem_high", "mem_low")]
            sq = sb(ctx, nc, "sq_x", [P, 2, W])
            mem = sb(ctx, nc, "mem", [P, CHUNKS, N_MEM])
            rmsnorm(nc, "norm_x", x, gains[:, 1, :], ones, h_low, sq, h_high)
            load_all(nc, "load_mem", [(mem[:, c, :], t["mem"][c]) for c in range(CHUNKS)])
            split_tiles(nc, "split_mem", [(mem[:, :, :], mem_split[0][:, :, :], mem_split[1][:, :, :])])
            gemm(nc, "w_mem", t["w_mem"], [(0, 16, dict(func=ACT.Copy, rhs=mem_split, dram=o["mem"]))], CHUNKS, N_MEM, finish_copy)
            gemm(nc, "w_xq", t["w_xq"], [(0, CHUNKS, dict(func=ACT.Copy, rhs=(h_high, h_low), dram=xq, scale=XD ** -0.5))],
                 CHUNKS, W, finish_copy)
        with ExitStack() as ctx:
            xo = sb(ctx, nc, "x_attended", [P, CHUNKS, W])
            cross_prompt(nc, xq, o["mem"], ident, xo)
            cross_sample(nc, t, xq, ident, xo)
            xo_split = [sb(ctx, nc, n, [P, CHUNKS, W], F32R) for n in ("xo_high", "xo_low")]
            split_tiles(nc, "split_xo", [(xo[:, c, :],) + tuple(y[:, c, :] for y in xo_split) for c in range(CHUNKS)])
            gemm(nc, "w_xo", t["w_xo"], [(0, CHUNKS, dict(rhs=xo_split, out=x))], CHUNKS, W, finish_residual, on_vector=True)

        with ExitStack() as ctx:
            h_low, h_high = (sb(ctx, nc, n, [P, CHUNKS, W], F32R) for n in ("hm_low", "hm_high"))
            with ExitStack() as c2:
                rmsnorm(nc, "norm_mlp", x, gains[:, 2, :], ones, h_low, sb(c2, nc, "sq_mlp", [P, 2, W]), h_high)
            hidden = [sb(ctx, nc, n, [P, CHUNKS, W], F32R) for n in ("hidden_high", "hidden_low")]
            up = lambda q: dict(rhs=(h_high, h_low), out=hidden, finish=finish_square, skipped=8 * q)
            down = dict(rhs=hidden, out=x, finish=finish_residual, settled=True)
            gemm(nc, "w_mlp", t["w_mlp"], [(16 * q + 8 * x2, 8, down if x2 else up(q)) for q in range(4) for x2 in range(2)],
                 CHUNKS, W, None, on_vector=True)
        with ExitStack() as ctx:
            h = sb(ctx, nc, "normed", [P, CHUNKS, W])
            rmsnorm(nc, "norm_final", x, gains[:, 3, :], ones, h, sb(ctx, nc, "sq_final", [P, 2, W]))
            load_all(nc, "store_y", [(o["y"][c], h[:, c, :]) for c in range(CHUNKS)])


SCRATCH = "Internal"
OUTPUTS = {
    "y": [CHUNKS, P, W], "kv": [6, P, W],
    "gdn_p": [P, GH, P], "gdn_s": [P, NB, GH, P],
    "win_s": [NB, WINDOW, 2 * P],
    "mem": [16, P, N_MEM],
    "conv_a_p": [4, P, CONV_W - 1], "conv_a_s": [4, P, NB, CONV_W - 1],
    "conv_qkv_p": [12, P, GDN_CONV_W - 1], "conv_qkv_s": [12, P, NB, GDN_CONV_W - 1],
}


def weight_tiles(w):
    k, m = w.shape
    return np.ascontiguousarray(w.reshape(k // P, P, m // P, P).transpose(2, 1, 0, 3)).reshape(m // P, P, k)


def block_masks(n, block, levels):
    j, i = np.mgrid[0:n, 0:n]
    valid = (j <= i) & (j // block == i // block)
    parts = [(i // (2 << l) == j // (2 << l)) & (i >> l != j >> l) & (i > j) for l in range(levels)]
    return (valid.astype(np.float32), np.where(valid, 0.0, NEG).astype(np.float32),
            np.ascontiguousarray(np.stack(parts, 1)).astype(np.float32))


def per_channel(v):
    v = v.reshape(v.shape[:-1] + (v.shape[-1] // P, P))
    return np.ascontiguousarray(np.moveaxis(v, -1, 0))


def channel_major(x_prompt, x_sample):
    tokens = np.concatenate([x_prompt.reshape(TP, -1), x_sample.reshape(NB * TS, -1)], 0)
    return np.ascontiguousarray(tokens.T).reshape(-1, P, W)


def kernel(**inputs):
    import concourse.bacc as bacc
    from concourse.bass_utils import run_bass_kernel_spmd

    a = {k: np.asarray(v) for k, v in inputs.items()}
    arrays = {}
    arrays["x"] = channel_major(a["x_prompt"], a["x_sample"])
    arrays["ones"] = np.ones((P, P), np.float32)
    arrays["ident"] = np.eye(P, dtype=np.float32)
    arrays["gains"] = per_channel(np.stack([a["norm_mix"][0], a["norm_x"][0], a["norm_mlp"][0], a["norm_final"]]))
    w = a["w_in"][0]
    conv, qkvz, ab = w[:, :1024], w[:, 1024:3072], w[:, 3072:3080]
    q = w[:, 3080:3592].reshape(D, NSA_KV, GQ, DH).transpose(0, 2, 1, 3).reshape(D, 512)
    kv, gl, gates = w[:, 3592:4360], w[:, 4360:4384], w[:, 4384:]
    arrays["w_in"] = weight_tiles(np.concatenate([conv, qkvz, q, kv, ab, gl, np.zeros((D, 96), np.float32), gates], 1))
    arrays["conv_a_w"] = per_channel(a["conv_a_w"][0])
    arrays["conv_a_vecs"] = per_channel(np.stack([a["conv_a_b"][0], a["ln_a_g"][0], a["ln_a_b"][0]]))
    arrays["state_conv_a"] = np.ascontiguousarray(
        a["state_conv_a"][0].reshape(NB, CONV_W - 1, 4, P).transpose(2, 3, 0, 1))
    arrays["gdn_conv_w"] = per_channel(a["gdn_conv_w"][0])
    arrays["state_conv_qkv"] = np.ascontiguousarray(
        a["state_conv_qkv"][0].reshape(NB, GDN_CONV_W - 1, 12, P).transpose(2, 3, 0, 1))
    arrays["decay_vecs"] = np.stack([a["gdn_a_log"][0], a["gdn_dt_bias"][0]], 1)
    arrays["gdn_norm_g"] = a["gdn_norm_g"][0].reshape(P, 1)
    arrays["tri_p"], arrays["bound_p"], arrays["levels_p"] = block_masks(P, P, 7)
    arrays["tri_s"], arrays["bound_s"], arrays["levels_s"] = block_masks(NB * TS, TS, 2)
    own = (np.arange(NB)[:, None] == np.arange(NB * TS)[None, :] // TS).astype(np.float32)
    arrays["batch_cols"] = np.broadcast_to(own, (P, NB, NB * TS)).copy()
    arrays["batch_rows"] = own.T.copy()
    arrays["state_gdn"] = np.ascontiguousarray(a["state_gdn"][0].transpose(2, 0, 1, 3))
    arrays["nsa_cmp_w"] = a["nsa_cmp_w"][0].reshape(-1)
    arrays["rel_bias"] = np.concatenate([a["rel_bias"], np.full((1, NSA_HEADS), NEG, np.float32)], 0)
    far = 639 - np.arange(LB_WIN)
    arrays["prompt_onehot"] = np.concatenate([bucket_onehot(1023 - np.arange(LB_FULL)),
                                              bucket_onehot(np.where(far < WINDOW, far, -1))], 1)
    arrays["page_table"] = a["page_table"].reshape(1, -1)
    cache = a["cache_nsa_kv"][0].reshape(N_POOL, PAGE, 4, P)
    arrays["cache_cmp"] = np.ascontiguousarray(cache[:, :, 0:2].transpose(0, 3, 2, 1)).reshape(N_POOL, P, 2 * PAGE)
    arrays["cache_kslc"] = np.ascontiguousarray(cache[:, :, 2].transpose(0, 2, 1))
    arrays["cache_vslc"] = np.ascontiguousarray(cache[:, :, 3])
    win = a["cache_win_kv"][0].reshape(NB, WINDOW, 2, P)
    arrays["cache_win"] = win.reshape(NB, WINDOW, 2 * P)
    arrays["cache_kwin"] = np.ascontiguousarray(win[:, :, 0].transpose(0, 2, 1))
    arrays["cache_vwin"] = np.ascontiguousarray(win[:, :, 1].reshape(NB, 4, P, P).transpose(0, 2, 1, 3)).reshape(NB, P, 4 * P)
    hots = []
    for s in range(TS):
        i = np.arange(WINDOW + TS)
        w = WINDOW + s - i
        near = PAGE + s - np.arange(PAGE + TS)
        last = bucket_onehot(np.array([MAX_DIST]))
        hots.append(np.concatenate([bucket_onehot(PAST + s - (np.arange(PAST // L_CMP) * L_CMP + L_CMP - 1)),
                                    bucket_onehot(np.where(w < WINDOW, w, -1)), bucket_onehot(near) - last, last], 1))
    arrays["sample_onehot"] = np.ascontiguousarray(np.stack(hots, 1))
    row = np.arange(P)
    query = row // 16 * TS + row % TS
    arrays["same_query"] = (query[:, None] == query[None, :]).astype(np.float32)
    blocks = np.arange(PAST // L_SEL + 1)
    cur = PAST // L_SEL
    arrays["forced"] = np.where((blocks == 0) | (blocks == cur) | (blocks == cur - 1), FORCE_BONUS, 0.0).astype(np.float32)
    arrays["lower"] = (blocks[None, :] < blocks[:, None]).astype(np.float32).reshape(-1)
    w_pc = a["w_pc"][0].reshape(NSA_KV, GQ, DH, D).transpose(1, 0, 2, 3).reshape(-1, D)
    arrays["w_branch"] = np.concatenate([weight_tiles(x) for x in (a["w_pa"][0], a["w_pb"][0], w_pc)], 0)
    for name in ("w_o", "w_xq", "w_xo"):
        arrays[name] = weight_tiles(a[name][0])
    arrays["w_mem"] = weight_tiles(np.concatenate([a["w_xk"][0], a["w_xv"][0]], 1))
    up, down = weight_tiles(a["w_ff1"][0]), [weight_tiles(a["w_ff2"][0][i:i + D]) for i in range(0, D_FF, D)]
    arrays["w_mlp"] = np.concatenate([part for q in range(D_FF // D) for part in (up[8 * q:8 * q + 8], down[q])], 0)
    arrays["mem"] = np.ascontiguousarray(a["mem_prompt"][0].T).reshape(CHUNKS, P, N_MEM)
    mkv = a["cache_mem_kv"][0].reshape(NB, N_MEM, 2, D)
    arrays["cache_mem_k"] = np.ascontiguousarray(mkv[:, :, 0].transpose(0, 2, 1).reshape(NB, CHUNKS, P, N_MEM)
                                                 .transpose(0, 2, 1, 3)).reshape(NB, P, CHUNKS * N_MEM)
    arrays["cache_mem_v"] = np.ascontiguousarray(mkv[:, :, 1].reshape(NB, 2, P, D).transpose(0, 2, 1, 3)).reshape(NB, P, 2 * D)
    nc = bacc.Bacc("TRN2", target_bir_lowering=False, num_devices=1)
    t = {k: nc.dram_tensor("in_" + k, v.shape, mybir.dt.from_np(v.dtype), kind="ExternalInput").ap()
         for k, v in arrays.items()}
    o = {k: nc.dram_tensor("out_" + k, s, F32, kind="ExternalOutput").ap() for k, s in OUTPUTS.items()}
    decoder_layer(nc, t, o)
    r = run_bass_kernel_spmd(nc, [{"in_" + k: v for k, v in arrays.items()}], core_ids=[0]).results[0]
    g = {k: r["out_" + k] for k in OUTPUTS}
    y, kv = (g[k].reshape(-1, W) for k in ("y", "kv"))
    y, kv = y.T, kv.T.reshape(W, 6, NSA_KV, DH)
    new = kv[TP:].reshape(NB, TS, 6, NSA_KV, DH)
    lay = lambda x, axes, shape: np.ascontiguousarray(x.transpose(axes).reshape(shape))
    return (
        np.ascontiguousarray(y[:TP]).reshape(1, TP, D),
        np.ascontiguousarray(y[TP:]).reshape(NB, TS, D),
        np.ascontiguousarray(kv[None, None, :TP, 0:4]),
        np.ascontiguousarray(kv[None, None, TP - WINDOW:TP, 4:6]),
        lay(g["conv_a_p"], (2, 0, 1), (1, 1, CONV_W - 1, CONV_CH)),
        lay(g["conv_qkv_p"], (2, 0, 1), (1, 1, GDN_CONV_W - 1, 12 * P)),
        lay(g["gdn_p"], (1, 0, 2), (1, 1, GH, P, P)),
        lay(g["mem"], (2, 0, 1), (1, 1, N_MEM, 2, XH, XD)),
        np.ascontiguousarray(new[None, :, :, 0:4]),
        g["win_s"].reshape(1, NB, WINDOW, 2, NSA_KV, DH),
        lay(g["conv_a_s"], (2, 3, 0, 1), (1, NB, CONV_W - 1, CONV_CH)),
        lay(g["conv_qkv_s"], (2, 3, 0, 1), (1, NB, GDN_CONV_W - 1, 12 * P)),
        lay(g["gdn_s"], (1, 2, 0, 3), (1, NB, GH, P, P)),
    )
```
